# Optimizing a Trainium2 kernel written in Bass

```python
import jax, jax.numpy as jnp
from jax import lax
import numpy as np

D_MODEL = 1024
BATCH = 1
SEQ = 256
DEPTH = 2

HEAD_DIM = 64
D_MIX = D_MODEL
CONV_WIDTH = D_MIX // 2
N_CONV_GROUPS = CONV_WIDTH // HEAD_DIM
ATTN_WIDTH = D_MIX - CONV_WIDTH
N_Q_HEADS = ATTN_WIDTH // HEAD_DIM
N_KV_GROUPS = 2
Q_PER_KV = N_Q_HEADS // N_KV_GROUPS
KV_WIDTH = N_KV_GROUPS * HEAD_DIM
N_GATES = 3
CMP_LEN = 32
CMP_STRIDE = 16
CMP_HIDDEN = 256
SLC_LEN = 64
SLC_TOPK = 16
WINDOW = 512
Q_CHUNK = 32
ROPE_THETA = 500000.0
ROPE_DIM = HEAD_DIM // 4
CONV_K = 3
FFN_CONV_K = 3
D_FF = 2816
ALPHA = (2.0 * DEPTH) ** 0.25
BETA = (8.0 * DEPTH) ** -0.25
NEG = -1e30
BIG = 1e9

kernel_name = 'hymba_shortconv_nsa_convffn_deepnorm'

def _in_split_points():
    sizes = [CONV_WIDTH] * 3 + [ATTN_WIDTH] + [KV_WIDTH] * 6 + [N_Q_HEADS * N_GATES]
    return [int(v) for v in np.cumsum(sizes)[:-1]], int(sum(sizes))

def _layer_norm(x, g, b, eps=1e-5):
    x32 = x.astype(jnp.float32)
    mu = jnp.mean(x32, -1, keepdims=True)
    var = jnp.mean(jnp.square(x32 - mu), -1, keepdims=True)
    return ((x32 - mu) * lax.rsqrt(var + eps) * g + b).astype(x.dtype)

def _head_rmsnorm(y, g, eps=1e-6):
    B, T, W = y.shape
    y32 = y.astype(jnp.float32).reshape(B, T, W // HEAD_DIM, HEAD_DIM)
    y32 = y32 * lax.rsqrt(jnp.mean(jnp.square(y32), -1, keepdims=True) + eps)
    return (y32.reshape(B, T, W) * g).astype(y.dtype)

def _causal_dwconv(z, w):
    K = w.shape[0]
    T = z.shape[1]
    zp = jnp.pad(z, ((0, 0), (K - 1, 0), (0, 0)))
    return sum(zp[:, k:k + T] * w[k] for k in range(K))

def _rope_tables(T):
    half = ROPE_DIM // 2
    inv_freq = ROPE_THETA ** (-(np.arange(half, dtype=np.float32) * 2.0 / ROPE_DIM))
    ang = jnp.arange(T, dtype=jnp.float32)[:, None] * jnp.asarray(inv_freq, jnp.float32)[None]
    return jnp.cos(ang)[:, None, :], jnp.sin(ang)[:, None, :]

def _partial_rope(x, cos, sin):
    half = ROPE_DIM // 2
    x1, x2, xp = x[..., :half], x[..., half:ROPE_DIM], x[..., ROPE_DIM:]
    rot = jnp.concatenate([x1 * cos - x2 * sin, x2 * cos + x1 * sin], -1).astype(x.dtype)
    return jnp.concatenate([rot, xp], -1)

def _masked_softmax(s, mask):
    s32 = jnp.where(mask, s.astype(jnp.float32), NEG)
    return jnp.where(mask, jax.nn.softmax(s32, axis=-1), 0.0)

def _slc_aggregation(T):
    nc = T // CMP_STRIDE - CMP_LEN // CMP_STRIDE + 1
    ns = T // SLC_LEN
    sc = np.arange(nc)[:, None] * CMP_STRIDE
    ss = np.arange(ns)[None, :] * SLC_LEN
    ov = np.clip(np.minimum(sc + CMP_LEN, ss + SLC_LEN) - np.maximum(sc, ss), 0, None)
    return jnp.asarray(ov / CMP_LEN, dtype=jnp.float32)

def _compress(a, pe, w1, b1, w2, b2):
    B, G, T, dk = a.shape
    r = CMP_LEN // CMP_STRIDE
    nsub = T // CMP_STRIDE
    nc = nsub - r + 1
    sub = a.reshape(B, G, nsub, CMP_STRIDE, dk)
    blocks = jnp.concatenate([sub[:, :, j:j + nc] for j in range(r)], axis=3)
    blocks = (blocks + pe).reshape(B, G, nc, CMP_LEN * dk)
    return jax.nn.gelu(blocks @ w1 + b1) @ w2 + b2

def _nsa(q, kc, vc, ks, vs, kw, vw, gates, pe, w1, b1, w2, b2):
    B, T, H, dk = q.shape
    G, R = N_KV_GROUPS, Q_PER_KV
    scale = dk ** -0.5
    qg = q.reshape(B, T, G, R, dk).transpose(0, 2, 3, 1, 4)
    to_g = lambda a: a.transpose(0, 2, 1, 3)
    k_cmp = _compress(to_g(kc), pe[0], w1[0], b1[0], w2[0], b2[0])
    v_cmp = _compress(to_g(vc), pe[1], w1[1], b1[1], w2[1], b2[1])
    nc = k_cmp.shape[2]
    cmp_end = jnp.arange(nc) * CMP_STRIDE + CMP_LEN - 1
    agg = _slc_aggregation(T)
    ns = T // SLC_LEN
    topk = min(SLC_TOPK, ns)
    kb_s = to_g(ks).reshape(B, G, ns, SLC_LEN, dk)
    vb_s = to_g(vs).reshape(B, G, ns, SLC_LEN, dk)
    pad = ((0, 0), (0, 0), (WINDOW, 0), (0, 0))
    kw_p = jnp.pad(to_g(kw), pad)
    vw_p = jnp.pad(to_g(vw), pad)
    blk = jnp.arange(ns)
    gather = jax.vmap(jax.vmap(lambda kb, ix: kb[ix]))

    def chunk(s):
        t = s + jnp.arange(Q_CHUNK)
        qc = lax.dynamic_slice_in_dim(qg, s, Q_CHUNK, axis=3) * scale
        sc = jnp.einsum('bgrqd,bgcd->bgrqc', qc, k_cmp)
        p_cmp = _masked_softmax(sc, cmp_end[None, :] <= t[:, None])
        o_cmp = jnp.einsum('bgrqc,bgcd->bgrqd', p_cmp, v_cmp)
        imp = jnp.einsum('bgrqc,cs->bgqs', p_cmp, agg)
        tb = t // SLC_LEN
        forced = (blk[None] == 0) | (blk[None] == tb[:, None]) | (blk[None] == tb[:, None] - 1)
        score = jnp.where(forced, BIG, imp)
        score = jnp.where(blk[None] <= tb[:, None], score, -BIG)
        _, idx = lax.top_k(score, topk)
        ks_sel = gather(kb_s, idx)
        vs_sel = gather(vb_s, idx).reshape(B, G, Q_CHUNK, topk * SLC_LEN, dk)
        ss = jnp.einsum('bgrqd,bgqnld->bgrqnl', qc, ks_sel).reshape(B, G, R, Q_CHUNK, topk * SLC_LEN)
        key_pos = idx[..., None] * SLC_LEN + jnp.arange(SLC_LEN)
        ms = (key_pos <= t[:, None, None]).reshape(B, G, 1, Q_CHUNK, topk * SLC_LEN)
        o_slc = jnp.einsum('bgrqm,bgqmd->bgrqd', _masked_softmax(ss, ms), vs_sel)
        kwin = lax.dynamic_slice_in_dim(kw_p, s, Q_CHUNK + WINDOW, axis=2)
        vwin = lax.dynamic_slice_in_dim(vw_p, s, Q_CHUNK + WINDOW, axis=2)
        wpos = s - WINDOW + jnp.arange(Q_CHUNK + WINDOW)
        mw = (wpos[None] <= t[:, None]) & (wpos[None] > t[:, None] - WINDOW) & (wpos[None] >= 0)
        sw = jnp.einsum('bgrqd,bgkd->bgrqk', qc, kwin)
        o_win = jnp.einsum('bgrqk,bgkd->bgrqd', _masked_softmax(sw, mw), vwin)
        return o_cmp, o_slc, o_win

    starts = jnp.arange(T // Q_CHUNK) * Q_CHUNK
    o_c, o_s, o_w = lax.map(chunk, starts)
    unchunk = lambda o: o.transpose(1, 0, 4, 2, 3, 5).reshape(B, T, H, dk)
    g = jax.nn.sigmoid(gates.astype(jnp.float32))
    out = g[..., 0:1] * unchunk(o_c) + g[..., 1:2] * unchunk(o_s) + g[..., 2:3] * unchunk(o_w)
    return out.astype(q.dtype).reshape(B, T, H * dk)

def setup_inputs(seed: int = 0) -> dict:
    key = jax.random.key(seed)
    ks = jax.random.split(key, 20)
    _, in_cols = _in_split_points()
    nrm = lambda k, shape, s: jax.random.normal(k, shape, jnp.float32) * s
    L = DEPTH
    return {
        'x': nrm(ks[0], (BATCH, SEQ, D_MODEL), 1.0),
        'w_in': nrm(ks[1], (L, D_MODEL, in_cols), D_MODEL ** -0.5),
        'short_conv_w': nrm(ks[2], (L, CONV_K, CONV_WIDTH), CONV_K ** -0.5),
        'cmp_pe': nrm(ks[3], (L, 2, CMP_LEN, HEAD_DIM), 0.02),
        'cmp_w1': nrm(ks[4], (L, 2, CMP_LEN * HEAD_DIM, CMP_HIDDEN), (CMP_LEN * HEAD_DIM) ** -0.5),
        'cmp_b1': nrm(ks[5], (L, 2, CMP_HIDDEN), 0.01),
        'cmp_w2': nrm(ks[6], (L, 2, CMP_HIDDEN, HEAD_DIM), CMP_HIDDEN ** -0.5),
        'cmp_b2': nrm(ks[7], (L, 2, HEAD_DIM), 0.01),
        'head_norm_g': 1.0 + nrm(ks[8], (L, D_MIX), 0.02),
        'w_out': nrm(ks[9], (L, D_MIX, D_MODEL), BETA * D_MIX ** -0.5),
        'ln1_g': 1.0 + nrm(ks[10], (L, D_MODEL), 0.02),
        'ln1_b': nrm(ks[11], (L, D_MODEL), 0.01),
        'w_up': nrm(ks[12], (L, D_MODEL, 2 * D_FF), D_MODEL ** -0.5),
        'ffn_conv_w': nrm(ks[13], (L, FFN_CONV_K, 2 * D_FF), FFN_CONV_K ** -0.5),
        'ffn_conv_b': nrm(ks[14], (L, 2 * D_FF), 0.01),
        'w_down': nrm(ks[15], (L, D_FF, D_MODEL), BETA * D_FF ** -0.5),
        'ln2_g': 1.0 + nrm(ks[16], (L, D_MODEL), 0.02),
        'ln2_b': nrm(ks[17], (L, D_MODEL), 0.01),
    }

def reference(x, w_in, short_conv_w, cmp_pe, cmp_w1, cmp_b1, cmp_w2, cmp_b2, head_norm_g,
              w_out, ln1_g, ln1_b, w_up, ffn_conv_w, ffn_conv_b, w_down, ln2_g, ln2_b):
    B, T, _ = x.shape
    split_points, _ = _in_split_points()
    cos, sin = _rope_tables(T)
    for i in range(DEPTH):
        proj = x @ w_in[i]
        (b_g, c_g, h, q, kc, vc, k_s, v_s, k_w, v_w, gates) = jnp.split(proj, split_points, axis=-1)
        conv_out = b_g * _causal_dwconv(c_g * h, short_conv_w[i])
        heads = lambda a, n: a.reshape(B, T, n, HEAD_DIM)
        q = _partial_rope(heads(q, N_Q_HEADS), cos, sin)
        kc = _partial_rope(heads(kc, N_KV_GROUPS), cos, sin)
        k_s = _partial_rope(heads(k_s, N_KV_GROUPS), cos, sin)
        k_w = _partial_rope(heads(k_w, N_KV_GROUPS), cos, sin)
        attn_out = _nsa(q, kc, heads(vc, N_KV_GROUPS), k_s, heads(v_s, N_KV_GROUPS), k_w,
                        heads(v_w, N_KV_GROUPS), gates.reshape(B, T, N_Q_HEADS, N_GATES),
                        cmp_pe[i], cmp_w1[i], cmp_b1[i], cmp_w2[i], cmp_b2[i])
        mixed = _head_rmsnorm(jnp.concatenate([conv_out, attn_out], -1), head_norm_g[i])
        x = _layer_norm(ALPHA * x + mixed @ w_out[i], ln1_g[i], ln1_b[i])
        u = _causal_dwconv(x @ w_up[i], ffn_conv_w[i]) + ffn_conv_b[i]
        val, gate = u[..., :D_FF], u[..., D_FF:]
        x = _layer_norm(ALPHA * x + (jax.nn.silu(gate) * val) @ w_down[i], ln2_g[i], ln2_b[i])
    return x


_drawn_inputs = setup_inputs


def setup_inputs(seed=0):
    import zlib

    import numpy as np

    out = dict(_drawn_inputs(seed))
    spreads = {}
    factors = {'cmp_pe': 6.867,
     'cmp_b1': 8.0,
     'cmp_b2': 7.064,
     'head_norm_g': 5.526,
     'ln1_b': 3.385,
     'ffn_conv_b': 8.0,
     'ln2_b': 3.494}
    for name, (base, spread) in spreads.items():
        noise = np.random.default_rng([zlib.crc32(name.encode()), seed]).standard_normal(out[name].shape)
        drawn = base * np.exp(spread * noise) if base else spread * noise
        out[name] = __import__('jax').numpy.asarray(drawn.astype(out[name].dtype))
    for name, factor in factors.items():
        out[name] = (out[name] * factor).astype(out[name].dtype)
    return out
```

```python
from contextlib import ExitStack

import concourse.bass as bass
import numpy as np
from concourse import mybir

P = 128
D_MODEL, SEQ, DEPTH, HEAD = 1024, 256, 2, 64
KT = D_MODEL // P
TT = SEQ // P
CONV_W, ATTN_W, KV_W = 512, 512, 128
NH, NG = ATTN_W // HEAD, 2
NPAIR = NH // NG
ROPE = HEAD // 4
NBLK = SEQ // 16 - 1
NJ = 16
CMP_HID = 256
D_FF = 2816
STEPS = D_FF // (2 * P)
ALPHA = (2.0 * DEPTH) ** 0.25
SCALE = HEAD ** -0.5
MASKED = -1e30
Q0, KV0, KW0, G0COL = 3 * CONV_W, 3 * CONV_W + ATTN_W, 3 * CONV_W + ATTN_W + 4 * KV_W, 3 * CONV_W + ATTN_W + 6 * KV_W
NGATE = NH * 3

UNIT = 2048
RAWS, SLOTS = 3, 6
NU = 15 + 3 * STEPS
U_CONV, U_OUT, U_FFN = 5, 11, 15
N_ATT = 13

C_ID, C_CM, C_CC, C_SS = 0, 128, 256, 288
C_MA, C_M01, C_BM, C_BLK = 320, 350, 380, 388
C_ALL = C_BLK + 2


def shape_constants():
    c = np.zeros((P, C_ALL), np.float32)
    p = np.arange(P)
    c[:, C_ID:C_ID + P] = np.eye(P)
    c[:, C_CM:C_CM + P] = np.where(p[None, :] > p[:, None], MASKED, 0.0)
    half = ROPE // 2
    inv_freq = (500000.0 ** (-(np.arange(half, dtype=np.float32) * 2.0 / ROPE))).astype(np.float32)
    for t in range(TT):
        ang = (p + P * t).astype(np.float32)[:, None] * inv_freq[None]
        cos, sin = np.cos(ang), np.sin(ang)
        c[:, C_CC + 16 * t:C_CC + 16 * t + 16] = np.concatenate([cos, cos], 1)
        c[:, C_SS + 16 * t:C_SS + 16 * t + 16] = np.concatenate([-sin, sin], 1)
        seen = (np.arange(NBLK)[None] * 16 + 31) <= (p + P * t)[:, None]
        c[:, C_MA + NBLK * t:C_MA + NBLK * (t + 1)] = np.where(seen, 0.0, MASKED)
        c[:, C_M01 + NBLK * t:C_M01 + NBLK * (t + 1)] = seen
    pos = p[:, None] // NBLK
    c[:, C_BM:C_BM + NH] = NPAIR * (pos % NG) + pos // NG == np.arange(NH)[None]
    c[:, C_BLK:C_BLK + 2] = (p[:, None] // HEAD == np.arange(2)[None]) / HEAD
    return c


class Chain:

    def __init__(self, eng, sem, layer, per_layer):
        self.eng, self.sem, self.base, self.per_layer, self.k = eng, sem, layer * per_layer, per_layer, 0

    def mark(self, ins):
        ins.then_inc(self.sem, 1)
        self.k += 1

    def wait(self):
        self.eng.wait_ge(self.sem, self.base + self.k)

    def close(self):
        assert self.k == self.per_layer, (self.k, self.per_layer)


def att_units():
    out = []
    for br in range(2):
        for t in range(TT):
            for g in range(NG):
                n = NPAIR // (t + 1)
                for part in range(t + 1):
                    out.append((br, t, g, range(part * n, part * n + n), t + 1))
    return out


ATT = att_units()
O_READY = [2, 6, 8, 12, 13, 14]

POOL_UNITS = {0, 1, 3, 5, 7, 9, 11, 13, 15, 17}

DVE_STEPS, POOL_STEPS = 67, 8
CREDIT = 1
FY_CREDIT = 4
H_CREDIT = 2


def build(nc, x, w_in, short_conv_w, cmp_pe, cmp_w1, cmp_b1, cmp_w2, cmp_b2, head_norm_g, w_out, ln1_g, ln1_b,
          w_up, ffn_conv_w, ffn_conv_b, w_down, ln2_g, ln2_b, consts, out):
    fp32, f32r, bf16 = mybir.dt.float32, mybir.dt.float32r, mybir.dt.bfloat16
    ALU, ACT, AX = mybir.AluOpType, mybir.ActivationFunctionType, mybir.AxisListType

    with ExitStack() as ctx:
        def sb(name, shape, dt=fp32):
            return ctx.enter_context(nc.sbuf_tensor(name, shape, dt))

        def sem(name):
            return ctx.enter_context(nc.semaphore(name))

        raw = [sb(f"raw{i}", [P, UNIT]) for i in range(RAWS)]
        ring_hi = [sb(f"ring_hi{i}", [P, UNIT], f32r) for i in range(SLOTS)]
        ring_lo = [sb(f"ring_lo{i}", [P, UNIT], f32r) for i in range(SLOTS)]
        x_tok = sb("x_tok", [P, TT, D_MODEL])
        xh = sb("xh", [P, KT, SEQ], f32r)
        xl = sb("xl", [P, KT, SEQ], f32r)
        cst = sb("cst", [P, C_ALL])
        ident = cst[:, C_ID:C_ID + P]
        ident_b = sb("ident_b", [P, P], bf16)
        cmask_b = sb("cmask_b", [P, P], bf16)
        ones = sb("ones", [1, P])
        neg_half = sb("neg_half", [P, 1])
        stage = sb("stage", [P, 4 * P])
        ffn_stage = stage[0:4 * STEPS, :].rearrange("c (k p) -> c k p", k=4)
        par_stage = sb("par_stage", [56, P])
        ffn_par = sb("ffn_par", [P, STEPS, 2, 2, 4])
        step_par = sb("step_par", [P, 2, 2, 2, 4])
        par = sb("par", [P, 56])
        gate_w = sb("gate_w", [P, KT, NGATE])
        gate_wh = sb("gate_wh", [P, KT, NGATE], f32r)
        gate_wl = sb("gate_wl", [P, KT, NGATE], f32r)
        qkv = sb("qkv", [P, TT, 20 * HEAD])
        ln_par = qkv[:, :, :].rearrange("p t f -> p (t f)")[:, 0:2 * D_MODEL].rearrange("p (a f) -> p a f", a=2)
        w1_raw = sb("w1_raw", [P, 2, NJ // 2 * CMP_HID])
        work = w1_raw[:, :, :].rearrange("p a f -> p (a f)")
        acc = work[:, 0:1024].rearrange("p (t f) -> p t f", t=TT)
        part = work[:, 1024:2048].rearrange("p (t f) -> p t f", t=TT)
        ffn_y = work[:, 2048:4096].rearrange("p (s v c n) -> p s v c n", s=2, v=2, c=2)
        w2 = sb("w2", [P, 2, 2, HEAD])
        b2 = sb("b2", [1, 2, HEAD])
        egate = sb("egate", [P, TT, NGATE])
        qT = sb("qT", [P, NPAIR, SEQ])
        kT = sb("kT", [P, 2, SEQ])
        cmpA = sb("cmpA", [P, 2, 3, P])
        hid = sb("hid", [P, 2, 45])
        hx = sb("hx", [P, 2, 2 * NBLK])
        hu = sb("hu", [P, 2, 2 * NBLK])
        ht = sb("ht", [P, 2, 2 * NBLK])
        hk = sb("hk", [P, 2, 2 * NBLK])
        hv = sb("hv", [P, 2, NH * NBLK])
        kcT = sb("kcT", [P, NG, NBLK])
        vbd = stage[0:NH * NBLK, :].rearrange("p (h d) -> p h d", h=NH)
        probs = [sb(f"probs{i}", [P, 512]) for i in range(2)]
        probsT = [sb(f"probsT{i}", [P, 512]) for i in range(2)]
        smax = sb("smax", [P, N_ATT - 1, NPAIR])
        cmax = sb("cmax", [P, TT * NH])
        nmax = sb("nmax", [P, 2, NPAIR])
        rsum = sb("rsum", [P, 3, TT, NH])
        coef = sb("coef", [P, 3, TT, NH])
        mstat = sb("mstat", [P, TT, NH])
        mroot = sb("mroot", [P, TT, NH])
        conv_z = sb("conv_z", [P, 2, SEQ])
        conv_y = sb("conv_y", [P, 2, SEQ])
        conv_o = sb("conv_o", [P, 4, SEQ])
        conv_sq = sb("conv_sq", [P, 2, SEQ])
        rope_a, rope_b = (conv_sq[:, n, 0:14 * ROPE].rearrange("p (h d) -> p h d", h=14) for n in range(2))
        cstat = sb("cstat", [P, 2, TT, 4])
        croot = sb("croot", [P, 2, TT, 4])
        hTh = sb("hTh", [P, 2, 2, SEQ], f32r)
        hTl = sb("hTl", [P, 2, 2, SEQ], f32r)
        stats = sb("stats", [P, TT, 2, 6])
        mv = sb("mv", [P, TT, 2])
        veps = sb("veps", [P, TT])
        rstd = sb("rstd", [P, TT])
        bank = [ctx.enter_context(nc.psum_tensor(f"bank{i}", [P, 512], fp32)) for i in range(8)]

        raw_in = [sem(f"raw_in{i}") for i in range(RAWS)]
        split_done = [sem(f"split_done{i}") for i in range(RAWS)]
        slot_free = [sem(f"slot_free{i}") for i in range(SLOTS)]
        hi_done = sem("hi_done")
        x_in, const_in, par_in, gate_in = sem("x_in"), sem("const_in"), sem("par_in"), sem("gate_in")
        w1_in = [sem("w1_in0"), sem("w1_in1")]
        ln_in, out_done, stage_free = sem("ln_in"), sem("out_done"), sem("stage_free")
        const_ready, masks_ready = sem("const_ready"), sem("masks_ready")
        par_T, par_ready, gate_hi, gate_lo = sem("par_T"), sem("par_ready"), sem("gate_hi"), sem("gate_lo")
        x_ready, xT_done, xT_hi, xT_lo = sem("x_ready"), sem("xT_done"), sem("xT_hi"), sem("xT_lo")
        x1_ready, x1T_done, x1T_hi, x1T_lo = sem("x1_ready"), sem("x1T_done"), sem("x1T_hi"), sem("x1T_lo")
        proj_done, qkv_copied, rope_done = sem("proj_done"), sem("qkv_copied"), sem("rope_done")
        qkT_done, qkT_copied, cmpA_copied = sem("qkT_done"), sem("qkT_copied"), sem("cmpA_copied")
        hid_done, tanh_in, tanh_done, hid_ready = sem("hid_done"), sem("tanh_in"), sem("tanh_done"), sem("hid_ready")
        cmp_done, cmp_copied = sem("cmp_done"), sem("cmp_copied")
        s_done, max_done, exp_done, cmp_p = sem("s_done"), sem("max_done"), sem("exp_done"), sem("cmp_p")
        pT_done, pT_copied, pv_done, o_read = sem("pT_done"), sem("pT_copied"), sem("pv_done"), sem("o_read")
        att_ss, att_root, att_ready, mixT_done = sem("att_ss"), sem("att_root"), sem("att_ready"), sem("mixT_done")
        c_copied, z_done, y_init = sem("c_copied"), sem("z_done"), sem("y_init")
        conv_out, sq_done, ms_used = sem("conv_out"), sem("sq_done"), sem("ms_used")
        ms_read, conv_root, bc_done, conv_norm = sem("ms_read"), sem("conv_root"), sem("bc_done"), sem("conv_norm")
        mix_hi, mix_lo, y1_done = sem("mix_hi"), sem("mix_lo"), sem("y1_done")
        ln_stats, ln_root = sem("ln_stats"), sem("ln_root")
        step_par_in, fy_init = sem("step_par_in"), sem("fy_init")
        fy_mid, fy_done = sem("fy_mid"), sem("fy_done")
        silu_done, h_done, h_hi, h_lo = sem("silu_done"), sem("h_done"), sem("h_hi"), sem("h_lo")
        y2_done = sem("y2_done")
        passed = sem("passed")
        dve_seq, pool_seq = sem("dve_seq"), sem("pool_seq")

        def raw_round(L, u, i=0):
            return L * (NU // RAWS) + u // RAWS + 2 * i

        def slot_round(L, u, i=0):
            return L * (NU // SLOTS) + u // SLOTS + i

        def unit_used(eng, L, u, i=0):
            eng.wait_ge(slot_free[u % SLOTS], CREDIT + slot_round(L, u, i) + 1)

        def split_hi(act, L, u, i=0):
            act.wait_ge(raw_in[u % RAWS], 16 * (raw_round(L, u, i) + 1))
            act.wait_ge(slot_free[u % SLOTS], CREDIT + slot_round(L, u, i))
            nc.scalar.activation(ring_hi[u % SLOTS][:], raw[u % RAWS][:], ACT.Copy).then_inc(hi_done, 1)

        def split_lo(eng, L, u, i=0):
            eng.wait_ge(hi_done, L * NU + u + 6 * i + 1)
            eng.tensor_tensor(ring_lo[u % SLOTS][:], raw[u % RAWS][:], ring_hi[u % SLOTS][:].bitcast(fp32),
                              ALU.subtract).then_inc(split_done[u % RAWS], 1)

        def bcast(ap, axis, shape):
            return ap.unsqueeze(axis).to_broadcast(shape)

        def settled(eng):
            eng.sem_inc(passed, 1)

        block = ctx.enter_context(nc.Block())

        @block.sync
        def _(sp):
            def load(L, u, i, src, **view):
                dst = raw[u % RAWS][:]
                if view:
                    dst = dst.rearrange(view.pop("to"), **view)
                sp.wait_ge(split_done[u % RAWS], CREDIT + raw_round(L, u, i))
                settled(sp)
                sp.dma_start(dst, src).then_inc(raw_in[u % RAWS], 16)

            def of(w, L):
                return w[bass.ds(L, 1)].rearrange("o a b -> (o a) b")

            def load_in(L, u, k0, nk, col):
                src = of(w_in, L)[P * k0:P * (k0 + nk), col:col + UNIT // nk].rearrange("(k p) n -> p k n", p=P)
                load(L, u, 0, src, to="p (k n) -> p k n", k=nk)

            def load_up(L, u, i, gate, step):
                src = of(w_up, L)[:, bass.ds(D_FF * gate + step * 2 * P, 2 * P)].rearrange("(k p) n -> p k n", p=P)
                load(L, u, i, src, to="p (k n) -> p k n", k=KT)

            def load_rows(L, u, i, w, row):
                src = of(w, L)[bass.ds(row, 2 * P), :].rearrange("(k p) n -> p k n", p=P)
                load(L, u, i, src, to="p (k n) -> p k n", k=2)

            sp.sem_inc(stage_free, CREDIT)
            for free in split_done:
                sp.sem_inc(free, CREDIT)
            with sp.Fori(0, DEPTH) as L:
                sp.wait_ge(stage_free, CREDIT + L)
                sp.dma_start(ffn_stage[:, 0:3, :], of(ffn_conv_w, L).rearrange("k (c p) -> c k p", p=P)).then_inc(par_in, 16)
                sp.dma_start(ffn_stage[:, 3, :], ffn_conv_b[bass.ds(L, 1)].rearrange("o (c p) -> (o c) p", p=P)).then_inc(par_in, 16)
                sp.dma_start(par_stage[0:8, :], head_norm_g[bass.ds(L, 1)].rearrange("o (c p) -> (o c) p", p=P)).then_inc(par_in, 16)
                sp.dma_start(par_stage[8:20, :], of(short_conv_w, L).rearrange("k (c p) -> (k c) p", p=P)).then_inc(par_in, 16)
                sp.dma_start(par_stage[20:24, :], of(cmp_b1, L).rearrange("k (c p) -> (k c) p", p=P)).then_inc(par_in, 16)
                sp.dma_start(par_stage[24:56, :], cmp_pe[bass.ds(L, 1)].rearrange("o k (j l) d -> (o k j) (l d)", l=2)).then_inc(par_in, 16)
                sp.dma_start(w2[:], cmp_w2[bass.ds(L, 1)].rearrange("o k (h p) d -> p (o k) h d", p=P)).then_inc(par_in, 16)
                sp.dma_start(b2[:], cmp_b2[bass.ds(L, 1)]).then_inc(par_in, 16)
                sp.dma_start(gate_w[:], of(w_in, L)[:, G0COL:G0COL + NGATE].rearrange("(k p) n -> p k n", p=P)).then_inc(gate_in, 16)
                load_in(L, 0, 0, 4, Q0)
                load_in(L, 1, 4, 4, Q0)
                load_in(L, 2, 0, 4, KV0)
                load_in(L, 3, 4, 4, KV0)
                load_in(L, 4, 0, 8, KW0)
                for pair in range(2):
                    for n, sect in enumerate((1, 2, 0)):
                        load_in(L, U_CONV + 3 * pair + n, 0, 8, CONV_W * sect + 2 * P * pair)
                for n in range(4):
                    load_rows(L, U_OUT + n, 0, w_out, 2 * P * n)
                load_up(L, U_FFN, 0, 0, 0)
                load_up(L, U_FFN + 1, 0, 1, 0)
                with sp.Fori(0, STEPS // 2) as i:
                    for odd in range(2):
                        load_up(L, 17 + 3 * odd, i, 0, 2 * i + 1 + odd)
                        load_up(L, 18 + 3 * odd, i, 1, 2 * i + 1 + odd)
                        load_rows(L, 19 + 3 * odd, i, w_down, (2 * i + odd) * 2 * P)
                load_rows(L, NU - 1, 0, w_down, (STEPS - 1) * 2 * P)
            for t in range(TT):
                sp.wait_ge(x_ready, 4 * DEPTH + 2 * (t + 1))
                sp.dma_start(out[0, P * t:P * (t + 1), :], x_tok[:, t, :]).then_inc(out_done, 16)
            sp.wait_ge(out_done, 16 * TT)

        @block.scalar
        def _(act):
            for free in slot_free:
                act.sem_inc(free, CREDIT)
            for t in range(TT):
                act.dma_start(x_tok[:, t, :], x[0, P * t:P * (t + 1), :]).then_inc(x_in, 16)
            act.dma_start(cst[:], consts).then_inc(const_in, 16)
            act.wait_ge(const_in, 16)
            nc.scalar.activation(ident_b[:], ident, ACT.Copy).then_inc(masks_ready, 1)
            nc.scalar.activation(cmask_b[:], cst[:, C_CM:C_CM + P], ACT.Copy).then_inc(masks_ready, 1)

            def x_high(L, banks, t, done, hi):
                for b in range(2):
                    act.wait_ge(done, 4 * L + 2 * t + b + 1)
                    nc.scalar.activation(xh[:, 4 * b:4 * b + 4, P * t:P * (t + 1)],
                                         bank[banks + 2 * t + b][:].rearrange("p (k n) -> p k n", k=4),
                                         ACT.Copy).then_inc(hi, 1)

            def copy_q(L):
                for t in range(TT):
                    if t == 0:
                        act.wait_ge(proj_done, 4 * L + 1)
                    else:
                        unit_used(act, L, 1)
                    nc.scalar.activation(qkv[:, t, 0:512].rearrange("p (i g d) -> p g i d", i=NPAIR, g=NG),
                                         bank[t][:].rearrange("p (g i d) -> p g i d", i=NPAIR, g=NG),
                                         ACT.Copy).then_inc(qkv_copied, 1)

            def kv_slots(t):
                return qkv[:, t, 512:1280].rearrange("p (b a f) -> p b a f", b=2, a=3)

            def copy_kv(L):
                for t in range(TT):
                    if t == 0:
                        act.wait_ge(proj_done, 4 * L + 2)
                    else:
                        unit_used(act, L, 3)
                    for b in range(2):
                        ins = nc.scalar.activation(kv_slots(t)[:, b, 0:2, :],
                                                   bank[2 + t][:].rearrange("p (a b f) -> p b a f", a=2, b=2)[:, b], ACT.Copy)
                    ins.then_inc(qkv_copied, 1)

            def copy_kw(L, t):
                act.wait_ge(proj_done, 4 * L + 2 + t + 1)
                nc.scalar.activation(egate[:, t, :], bank[4 + t][:, 256:256 + NGATE], ACT.Exp, scale=-1.0)
                nc.scalar.activation(kv_slots(t)[:, :, 2, :], bank[4 + t][:, 0:256].rearrange("p (b f) -> p b f", b=2),
                                     ACT.Copy).then_inc(qkv_copied, 1)

            def copy_c(L, pair):
                unit_used(act, L, U_CONV + 3 * pair)
                if pair:
                    act.wait_ge(conv_out, 2 * L + pair)
                nc.scalar.activation(conv_z[:].rearrange("p c n -> p (c n)"), bank[4 + pair][:], ACT.Copy).then_inc(c_copied, 1)

            def conv_init(L, pair):
                act.wait_ge(z_done, 2 * L + pair + 1)
                for m in range(2):
                    tap = 8 + 2 * 4 + 2 * pair + m
                    ins = nc.scalar.activation(conv_y[:, m, :], conv_z[:, m, :], ACT.Copy, scale=par[:, tap:tap + 1])
                ins.then_inc(y_init, 1)

            def conv_square(L, pair):
                act.wait_ge(conv_out, 2 * L + pair + 1)
                if pair:
                    act.wait_ge(ms_used, 2 * L + pair)
                nc.scalar.activation(conv_sq[:], conv_o[:, 2 * pair:2 * pair + 2, :], ACT.Square).then_inc(sq_done, 1)

            def exps(L, n):
                br, t, g, heads, kb = ATT[n]
                keys = P * kb
                act.wait_ge(max_done, N_ATT * L + n + 1)
                if n >= 2:
                    act.wait_ge(pT_done, N_ATT * L + n - 1)
                for j, h in enumerate(heads):
                    ins = nc.scalar.activation(probs[n % 2][:, keys * j:keys * (j + 1)], bank[n % 2][:, keys * j:keys * (j + 1)],
                                               ACT.Exp, bias=nmax[:, n % 2, j:j + 1], scale=SCALE,
                                               accum_out=rsum[:, br, t, NPAIR * g + h:NPAIR * g + h + 1])
                ins.then_inc(exp_done, 1)

            def mix_high(L, j, src):
                nc.scalar.activation(xh[:, j, :], src, ACT.Copy, scale=par[:, j:j + 1]).then_inc(mix_hi, 1)

            def ffn_step(L, s, odd, value, gate, units):
                G = L * STEPS + s
                act.wait_ge(step_par_in, G + 1)
                act.wait_ge(h_lo, H_CREDIT + G - 1)
                for v, u in enumerate((value, gate)):
                    unit_used(act, L, *u)
                    for c in range(2):
                        ins = nc.scalar.activation(ffn_y[:, odd, v, c, :], bank[4 + 2 * odd + v][:, SEQ * c:SEQ * (c + 1)],
                                                   ACT.Identity, scale=step_par[:, odd, v, c, 2:3],
                                                   bias=step_par[:, odd, v, c, 3:4])
                    ins.then_inc(fy_init, 1)
                for u in units[0:1]:
                    split_hi(act, L, *u)
                act.wait_ge(fy_done, FY_CREDIT + 2 * G + 2)
                y = ffn_y[:, odd].rearrange("p v c n -> p v (c n)")
                nc.scalar.activation(y[:, 1], y[:, 1], ACT.Silu).then_inc(silu_done, 1)
                for u in units[1:2]:
                    split_hi(act, L, *u)
                act.wait_ge(h_done, G + 1)
                nc.scalar.activation(hTh[:, odd].rearrange("p c n -> p (c n)"), y[:, 0], ACT.Copy).then_inc(h_hi, 1)
                for u in units[2:3]:
                    split_hi(act, L, *u)

            with act.Fori(0, DEPTH) as L:
                split_hi(act, L, 0)
                split_hi(act, L, 1)
                act.wait_ge(par_T, L + 1)
                for v in range(2):
                    nc.scalar.activation(
                        ffn_par[:, :, v].rearrange("p s c k -> p k s c"),
                        bank[4][:, 0:176].rearrange("p (k v s c) -> p k v s c", k=4, v=2, c=2)[:, :, v], ACT.Copy)
                nc.scalar.activation(par[:], bank[4][:, 176:232], ACT.Copy).then_inc(par_ready, 1)
                act.wait_ge(gate_in, 16 * (L + 1))
                nc.scalar.activation(gate_wh[:], gate_w[:], ACT.Copy).then_inc(gate_hi, 1)
                for t in range(TT):
                    x_high(L, 4, t, xT_done, xT_hi)
                for half in range(2):
                    act.dma_start(w1_raw[:, half, :].rearrange("p (j n) -> p j n", n=CMP_HID),
                                  cmp_w1[bass.ds(L, 1), 0, P * 8 * half:P * 8 * (half + 1), :]
                                  .rearrange("o (j p) n -> p (o j) n", p=P)).then_inc(w1_in[half], 16)
                for u in range(2, 6):
                    split_hi(act, L, u)
                copy_q(L)
                split_hi(act, L, 6)
                copy_kv(L)
                split_hi(act, L, 7)
                for t in range(TT):
                    copy_kw(L, t)
                copy_c(L, 0)
                act.wait_ge(qkT_done, 4 * L + 4)
                nc.scalar.activation(cmpA[:, :, 0:2, :].rearrange("p v g m -> p v (g m)"),
                                     bank[1][:].rearrange("p (v m) -> p v m", v=2), ACT.Copy)
                nc.scalar.activation(cmpA[:, :, 2, 0:16], par[:, 24:56].rearrange("p (v j) -> p v j", v=2),
                                     ACT.Copy).then_inc(cmpA_copied, 1)
                conv_init(L, 0)
                exps(L, 0)
                split_hi(act, L, 8)
                for half in range(2):
                    act.wait_ge(hid_done, 4 * L + half + 1)
                    act.dma_start(w1_raw[:, half, :].rearrange("p (j n) -> p j n", n=CMP_HID),
                                  cmp_w1[bass.ds(L, 1), 1, P * 8 * half:P * 8 * (half + 1), :]
                                  .rearrange("o (j p) n -> p (o j) n", p=P)).then_inc(w1_in[half], 16)
                act.wait_ge(tanh_in, 2 * L + 1)
                nc.scalar.activation(ht[:], hu[:], ACT.Tanh).then_inc(tanh_done, 1)
                exps(L, 1)
                conv_square(L, 0)
                act.wait_ge(tanh_in, 2 * L + 2)
                nc.scalar.activation(ht[:], hu[:], ACT.Tanh).then_inc(tanh_done, 1)
                split_hi(act, L, 9)
                between = {3: [lambda: copy_c(L, 1)], 4: [lambda: split_hi(act, L, 10)], 6: [lambda: conv_init(L, 1)],
                           7: [lambda: split_hi(act, L, 11)], 9: [lambda: split_hi(act, L, 12)],
                           10: [lambda: conv_square(L, 1)], 11: [lambda: split_hi(act, L, 13)]}
                for n in range(2, 12):
                    exps(L, n)
                    for step in between.get(n, []):
                        step()
                act.wait_ge(max_done, N_ATT * L + 13)
                flat = probs[0][:, 0:TT * NH * NBLK]
                nc.scalar.activation(flat, flat, ACT.Exp, scale=SCALE).then_inc(exp_done, 1)
                split_hi(act, L, 14)
                for j in range(4):
                    act.wait_ge(conv_norm, 2 * L + j // 2 + 1)
                    mix_high(L, j, conv_o[:, j, :])
                for j in range(4):
                    if j % 2 == 0:
                        act.wait_ge(mixT_done, 2 * L + j // 2 + 1)
                    mix_high(L, 4 + j, bank[6 + j // 2][:, SEQ * (j % 2):SEQ * (j % 2 + 1)])
                act.wait_ge(pv_done, 14 * L + 14)
                act.wait_ge(rope_done, 2 * L + 2)
                for a, w in enumerate((ln1_g, ln1_b)):
                    act.dma_start(ln_par[:, a, :], w[bass.ds(L, 1)].to_broadcast([P, D_MODEL])).then_inc(ln_in, 16)
                split_hi(act, L, 15)
                split_hi(act, L, 16)
                split_hi(act, L, 17)
                x_high(L, 0, 0, x1T_done, x1T_hi)
                split_hi(act, L, 18)
                x_high(L, 0, 1, x1T_done, x1T_hi)
                for a, w in enumerate((ln2_g, ln2_b)):
                    act.dma_start(ln_par[:, a, :], w[bass.ds(L, 1)].to_broadcast([P, D_MODEL])).then_inc(ln_in, 16)
                split_hi(act, L, 19)
                ffn_step(L, 0, 0, (15, 0), (16, 0), [(20, 0), (21, 0), (22, 0)])
                with act.Fori(0, (STEPS - 3) // 2) as i:
                    ffn_step(L, 2 * i + 1, 1, (17, i), (18, i), [(23, i), (24, i), (25, i)])
                    ffn_step(L, 2 * i + 2, 0, (20, i), (21, i), [(26, i), (27, i), (28, i)])
                last = (STEPS - 3) // 2
                ffn_step(L, STEPS - 2, 1, (17, last), (18, last), [(NU - 1, 0)])
                ffn_step(L, STEPS - 1, 0, (20, last), (21, last), [])

        @block.gpsimd
        def _(pool):
            nc.gpsimd.memset(neg_half[:], -0.5).then_inc(const_ready, 1)
            nc.gpsimd.memset(cmpA[:], 0.0).then_inc(const_ready, 1)
            nc.gpsimd.memset(ones[:], 1.0).then_inc(const_ready, 1)
            nc.gpsimd.memset(kcT[:], 0.0).then_inc(const_ready, 1)
            pool.wait_ge(const_ready, 4)

            def root(L, chain, var, eps_out, eps, mul, result, half, signal):
                settled(pool)
                chain.mark(nc.gpsimd.tensor_scalar(eps_out, var, mul, eps, ALU.mult, ALU.add))
                chain.wait()
                nc.gpsimd.tensor_tensor(result, eps_out, half, ALU.pow).then_inc(signal, 1)

            def conv_root_of(L, pair, chain):
                pool.wait_ge(ms_read, 2 * L + pair + 1)
                flat = [a[:, pair].rearrange("p t h -> p (t h)") for a in (cstat, croot)]
                root(L, chain, flat[0], flat[0], 1e-6, 1.0, flat[1], neg_half[:].to_broadcast([P, 4 * TT]), conv_root)

            def step_params(s, odd):
                settled(pool)
                nc.gpsimd.tensor_copy(step_par[:, odd].rearrange("p v c k -> p (v c k)"),
                                      ffn_par[:, bass.ds(s, 1)].rearrange("p o v c k -> p (o v c k)"))\
                    .then_inc(step_par_in, 1)

            def next_params(L, s, odd):
                pool.wait_ge(fy_done, FY_CREDIT + 2 * (L * STEPS + s) + 2)
                step_params(s + 2, odd)

            with pool.Fori(0, DEPTH) as L:
                chain = Chain(pool, pool_seq, L, POOL_STEPS)
                for u in (0, 1, 3, 5, 7, 9):
                    split_lo(nc.gpsimd, L, u)
                conv_root_of(L, 0, chain)
                split_lo(nc.gpsimd, L, 11)
                split_lo(nc.gpsimd, L, 13)
                conv_root_of(L, 1, chain)
                for t in range(TT):
                    pool.wait_ge(att_ss, 2 * L + t + 1)
                    root(L, chain, mstat[:, t, :], mstat[:, t, :], 1e-6, 1.0 / HEAD, mroot[:, t, :], neg_half[:].to_broadcast([P, NH]), att_root)
                split_lo(nc.gpsimd, L, 15)
                pool.wait_ge(par_ready, L + 1)
                for odd in range(2):
                    step_params(odd, odd)
                pool.wait_ge(ln_stats, 4 * L + 1)
                root(L, chain, mv[:, 0, 1:2], veps[:, 0:1], 1e-5, 1.0, rstd[:, 0:1], neg_half[:, 0:1], ln_root)
                split_lo(nc.gpsimd, L, 17)
                pool.wait_ge(ln_stats, 4 * L + 2)
                root(L, chain, mv[:, 1, 1:2], veps[:, 1:2], 1e-5, 1.0, rstd[:, 1:2], neg_half[:, 0:1], ln_root)
                split_lo(nc.gpsimd, L, 20)
                next_params(L, 0, 0)
                with pool.Fori(0, (STEPS - 3) // 2) as i:
                    split_lo(nc.gpsimd, L, 23, i)
                    next_params(L, 2 * i + 1, 1)
                    split_lo(nc.gpsimd, L, 26, i)
                    next_params(L, 2 * i + 2, 0)
                for t in range(TT):
                    pool.wait_ge(ln_stats, 4 * L + 3 + t)
                    root(L, chain, mv[:, t, 1:2], veps[:, t:t + 1], 1e-5, 1.0, rstd[:, t:t + 1], neg_half[:, 0:1], ln_root)
                chain.close()

        @block.vector
        def _(dve):
            V = nc.vector
            dve.wait_ge(x_in, 16 * TT)
            dve.sem_inc(x_ready, 4)
            dve.sem_inc(fy_done, FY_CREDIT)
            dve.sem_inc(h_lo, H_CREDIT)
            dve.wait_ge(const_in, 16)
            dve.wait_ge(const_ready, 4)

            def x_low(L, banks, t, hi, lo):
                for b in range(2):
                    dve.wait_ge(hi, 4 * L + 2 * t + b + 1)
                    dst = slice(4 * b, 4 * b + 4), slice(P * t, P * (t + 1))
                    V.tensor_tensor(xl[:, dst[0], dst[1]], bank[banks + 2 * t + b][:].rearrange("p (k n) -> p k n", k=4),
                                    xh[:, dst[0], dst[1]].bitcast(fp32), ALU.subtract).then_inc(lo, 1)

            def rope(L, t, chain):
                dve.wait_ge(qkv_copied, 6 * L + 5 + t)
                head = qkv[:, t, 0:14 * HEAD].rearrange("p (h d) -> p h d", d=HEAD)
                cc = bcast(cst[:, C_CC + 16 * t:C_CC + 16 * t + 16], 1, [P, 14, 16])
                ss = cst[:, C_SS + 16 * t:C_SS + 16 * t + 16]
                if t:
                    dve.wait_ge(rope_done, 2 * L + t)
                V.tensor_tensor(rope_a, head[:, :, 0:16], cc, ALU.mult)
                V.tensor_tensor(rope_b[:, :, 0:8], head[:, :, 8:16], bcast(ss[:, 0:8], 1, [P, 14, 8]), ALU.mult)
                chain.mark(V.tensor_tensor(rope_b[:, :, 8:16], head[:, :, 0:8], bcast(ss[:, 8:16], 1, [P, 14, 8]), ALU.mult))
                chain.wait()
                V.tensor_tensor(head[:, :, 0:16], rope_a, rope_b, ALU.add).then_inc(rope_done, 1)

            def conv_taps(L, pair, chain):
                dve.wait_ge(y_init, 2 * L + pair + 1)
                for back in (1, 2):
                    if back == 2:
                        chain.wait()
                    for m in range(2):
                        tap = 8 + (2 - back) * 4 + 2 * pair + m
                        ins = V.scalar_tensor_tensor(conv_y[:, m, back:], conv_z[:, m, 0:SEQ - back], par[:, tap:tap + 1],
                                                     conv_y[:, m, back:], ALU.mult, ALU.add)
                    chain.mark(ins)
                chain.wait()
                unit_used(dve, L, U_CONV + 3 * pair + 2)
                V.tensor_tensor(conv_o[:, 2 * pair:2 * pair + 2, :].rearrange("p c n -> p (c n)"),
                                conv_y[:].rearrange("p c n -> p (c n)"), bank[4 + pair][:], ALU.mult).then_inc(conv_out, 1)

            def conv_gate(L, pair):
                unit_used(dve, L, U_CONV + 3 * pair + 1)
                dve.wait_ge(c_copied, 2 * L + pair + 1)
                z = conv_z[:].rearrange("p c n -> p (c n)")
                V.tensor_tensor(z, z, bank[5 - pair][:], ALU.mult).then_inc(z_done, 1)

            def hidden(L, kv, chain):
                dve.wait_ge(hid_done, 4 * L + 2 * kv + 2)
                if kv:
                    dve.wait_ge(hid_ready, 2 * L + 1)
                chain.mark(V.tensor_copy(hid[:], bank[2 + kv][:, 0:96].rearrange("p (h n) -> p h n", h=2)[:, :, 0:45]))
                chain.wait()
                for h in range(2):
                    ins = V.tensor_scalar(hx[:, h, :], hid[:, h, 0:30], hid[:, h, 30:31],
                                          par[:, 20 + 2 * kv + h:21 + 2 * kv + h], ALU.add, ALU.add)
                chain.mark(ins)
                chain.wait()
                chain.mark(V.tensor_tensor(hu[:], hx[:], hx[:], ALU.mult))
                chain.wait()
                c = float(np.sqrt(2.0 / np.pi))
                chain.mark(V.tensor_scalar(hu[:], hu[:], 0.044715 * c, c, ALU.mult, ALU.add))
                chain.wait()
                V.tensor_tensor(hu[:], hu[:], hx[:], ALU.mult).then_inc(tanh_in, 1)
                dve.wait_ge(tanh_done, 2 * L + kv + 1)
                chain.mark(V.tensor_scalar(ht[:], ht[:], 0.5, 0.5, ALU.mult, ALU.add))
                chain.wait()
                if kv == 0:
                    V.tensor_tensor(hk[:], ht[:], hx[:], ALU.mult).then_inc(hid_ready, 1)
                else:
                    chain.mark(V.tensor_tensor(ht[:], ht[:], hx[:], ALU.mult))
                    chain.wait()
                    for h in range(2):
                        ins = V.tensor_copy(hv[:, h, :].rearrange("p (i n) -> p i n", i=NPAIR),
                                            bcast(ht[:, h, :], 1, [P, NPAIR, NG * NBLK]))
                    ins.then_inc(hid_ready, 1)

            def maxima(L, n, chain):
                br, t, g, heads, kb = ATT[n]
                dve.wait_ge(s_done, N_ATT * L + n + 1)
                nh = len(heads)
                chain.mark(V.tensor_reduce(smax[:, n, 0:nh], bank[n % 2][:].rearrange("p (h k) -> p h k", h=nh), AX.X, ALU.max))
                chain.wait()
                V.tensor_scalar(nmax[:, n % 2, 0:nh], smax[:, n, 0:nh], -SCALE, None, ALU.mult).then_inc(max_done, 1)

            def copy_pT(L, n):
                dve.wait_ge(pT_done, N_ATT * L + n + 1)
                if n >= 2:
                    dve.wait_ge(pv_done, 14 * L + n - 1)
                width = 512 if n < 12 else 2 * P
                rows = P if n < 12 else NH * NBLK
                V.tensor_copy(probsT[n % 2][0:rows, 0:width], bank[6 + n % 2][0:rows, 0:width]).then_inc(pT_copied, 1)

            def combine(L, og, chain):
                br, t = (0, 1, 2)[og // 2], og % 2
                if og == 0:
                    chain.mark(V.tensor_scalar(egate[:], egate[:], 1.0, None, ALU.add))
                if br < 2:
                    dve.wait_ge(exp_done, N_ATT * L + O_READY[og])
                chain.wait()
                chain.mark(V.tensor_tensor(coef[:, br, t, :], rsum[:, br, t, :],
                                           egate[:, t, :].rearrange("p (h b) -> p b h", b=3)[:, (br + 1) % 3, :], ALU.mult))
                chain.wait()
                chain.mark(V.reciprocal(coef[:, br, t, :], coef[:, br, t, :]))
                chain.wait()
                dve.wait_ge(pv_done, 14 * L + O_READY[og])
                o = bank[2][:].rearrange("p (h d) -> p h d", h=NH)
                c = bcast(coef[:, br, t, :], 2, [P, NH, HEAD])
                if og < 2:
                    ins = V.tensor_tensor(acc[:, t, :].rearrange("p (h d) -> p h d", h=NH), o, c, ALU.mult)
                    ins.then_inc(o_read, 1)
                else:
                    V.tensor_tensor(part[:, 0, :].rearrange("p (h d) -> p h d", h=NH), o, c, ALU.mult).then_inc(o_read, 1)
                    dve.wait_ge(o_read, 6 * L + og + 1)
                    chain.mark(V.tensor_tensor(acc[:, t, :], acc[:, t, :], part[:, 0, :], ALU.add))

            def copy_squares(L, pair):
                dve.wait_ge(ms_used, 2 * L + pair + 1)
                V.tensor_copy(cstat[:, pair].rearrange("p t h -> p (t h)"), bank[3][:, 8 * pair:8 * pair + 8]).then_inc(ms_read, 1)

            def mix_low(L, j, src):
                V.scalar_tensor_tensor(xl[:, j, :], src, par[:, j:j + 1], xh[:, j, :].bitcast(fp32), ALU.mult,
                                       ALU.subtract).then_inc(mix_lo, 1)

            def layer_norm(L, which, t, banks, ready, chain):
                if t == 0:
                    dve.wait_ge(y1_done if which == 0 else y2_done, L + 1)
                else:
                    unit_used(dve, L, U_OUT + 3 if which == 0 else NU - 1)
                xt = x_tok[:, t, :]
                for n in range(2):
                    cols = slice(512 * n, 512 * (n + 1))
                    chain.mark(V.scalar_tensor_tensor(xt[:, cols], xt[:, cols], ALPHA, bank[banks + 2 * t + n][:], ALU.mult, ALU.add))
                    if n:
                        dve.wait_ge(dve_seq, chain.base + chain.k - 1)
                        V.bn_stats(stats[:, t, 0, :], xt[:, 0:512])
                chain.wait()
                chain.mark(V.bn_stats(stats[:, t, 1, :], xt[:, 512:1024]))
                chain.wait()
                settled(dve)
                V.bn_aggr(mv[:, t, :], stats[:, t].rearrange("p n s -> p (n s)")).then_inc(ln_stats, 1)
                if t == 0:
                    dve.wait_ge(ln_in, 16 * (4 * L + 2 * which + 2))
                dve.wait_ge(ln_stats, 4 * L + 2 * which + t + 1)
                chain.mark(V.scalar_tensor_tensor(xt, xt, mv[:, t, 0:1], ln_par[:, 0, :], ALU.subtract, ALU.mult))
                chain.wait()
                dve.wait_ge(ln_root, 4 * L + 2 * which + t + 1)
                for n in range(2):
                    cols = slice(512 * n, 512 * (n + 1))
                    V.scalar_tensor_tensor(xt[:, cols], xt[:, cols], rstd[:, t:t + 1], ln_par[:, 1, cols], ALU.mult,
                                           ALU.add).then_inc(ready, 1)

            def ffn_step(L, s, odd, value, gate, units):
                G = L * STEPS + s
                for back in (1, 2):
                    for v in range(2):
                        b = bank[4 + 2 * odd + v]
                        if back == 1:
                            dve.wait_ge(fy_init, 2 * G + v + 1)
                        else:
                            dve.wait_ge(fy_mid, 2 * G + v + 1)
                        for c in range(2):
                            ins = V.scalar_tensor_tensor(ffn_y[:, odd, v, c, back:], b[:, SEQ * c:SEQ * (c + 1) - back],
                                                         step_par[:, odd, v, c, 2 - back:3 - back],
                                                         ffn_y[:, odd, v, c, back:], ALU.mult, ALU.add)
                        ins.then_inc(fy_mid if back == 1 else fy_done, 1)
                for u in units[0:1]:
                    split_lo(V, L, *u)
                dve.wait_ge(silu_done, G + 1)
                y = ffn_y[:, odd].rearrange("p v c n -> p v (c n)")
                V.tensor_tensor(y[:, 0], y[:, 0], y[:, 1], ALU.mult).then_inc(h_done, 1)
                for u in units[1:2]:
                    split_lo(V, L, *u)
                dve.wait_ge(h_hi, G + 1)
                V.tensor_tensor(hTl[:, odd].rearrange("p c n -> p (c n)"), y[:, 0],
                                hTh[:, odd].rearrange("p c n -> p (c n)").bitcast(fp32), ALU.subtract).then_inc(h_lo, 1)

            with dve.Fori(0, DEPTH) as L:
                chain = Chain(dve, dve_seq, L, DVE_STEPS)
                dve.wait_ge(gate_hi, L + 1)
                V.tensor_tensor(gate_wl[:], gate_w[:], gate_wh[:].bitcast(fp32), ALU.subtract).then_inc(gate_lo, 1)
                for t in range(TT):
                    x_low(L, 4, t, xT_hi, xT_lo)
                split_lo(V, L, 2)
                split_lo(V, L, 4)
                dve.wait_ge(par_ready, L + 1)
                split_lo(V, L, 6)
                for t in range(TT):
                    rope(L, t, chain)
                conv_gate(L, 0)
                for b in range(2):
                    dve.wait_ge(qkT_done, 4 * L + b + 1)
                    V.tensor_copy(qT[:, 2 * b:2 * b + 2, :], bank[6 + b][:].rearrange("p (i n) -> p i n", i=2)).then_inc(qkT_copied, 1)
                dve.wait_ge(qkT_done, 4 * L + 3)
                V.tensor_copy(kT[:], bank[0][:].rearrange("p (i n) -> p i n", i=2)).then_inc(qkT_copied, 1)
                maxima(L, 0, chain)
                split_lo(V, L, 8)
                conv_taps(L, 0, chain)
                hidden(L, 0, chain)
                maxima(L, 1, chain)
                dve.wait_ge(cmp_done, 2 * L + 1)
                for g in range(NG):
                    rows = slice(HEAD * g, HEAD * (g + 1))
                    ins = V.tensor_copy(kcT[rows, g, :], bank[2][rows, 128:128 + NBLK])
                ins.then_inc(cmp_copied, 1)
                hidden(L, 1, chain)
                copy_pT(L, 0)
                maxima(L, 2, chain)
                dve.wait_ge(cmp_done, 2 * L + 2)
                V.tensor_tensor(vbd, bcast(bank[3][0:NH * NBLK, 128:128 + HEAD], 1, [NH * NBLK, NH, HEAD]),
                                bcast(cst[0:NH * NBLK, C_BM:C_BM + NH], 2, [NH * NBLK, NH, HEAD]), ALU.mult).then_inc(cmp_copied, 1)
                copy_pT(L, 1)
                between = {2: [lambda: combine(L, 0, chain)], 3: [lambda: copy_squares(L, 0)], 4: [lambda: conv_gate(L, 1), lambda: split_lo(V, L, 10)],
                           6: [lambda: combine(L, 1, chain)], 8: [lambda: combine(L, 2, chain), lambda: conv_taps(L, 1, chain)],
                           9: [lambda: split_lo(V, L, 12)]}
                for n in range(2, 11):
                    maxima(L, n + 1, chain)
                    copy_pT(L, n)
                    for step in between.get(n, []):
                        step()
                dve.wait_ge(s_done, N_ATT * L + 13)
                dve.wait_ge(pT_done, N_ATT * L + 11)
                flat = probs[0][:, 0:TT * NH * NBLK].rearrange("p (h c) -> p h c", c=NBLK)
                sc = probs[0][:, 0:TT * NH * NBLK].rearrange("p (t h c) -> p t h c", t=TT, h=NH)
                scores = bank[0][:, 0:TT * NH * NBLK].rearrange("p (t h c) -> p t h c", t=TT, h=NH)
                for t in range(TT):
                    ins = V.tensor_tensor(sc[:, t], scores[:, t], bcast(cst[:, C_MA + NBLK * t:C_MA + NBLK * (t + 1)], 1,
                                                                        [P, NH, NBLK]), ALU.add)
                chain.mark(ins)
                chain.wait()
                chain.mark(V.tensor_reduce(cmax[:], flat, AX.X, ALU.max))
                chain.wait()
                V.tensor_tensor(flat, flat, bcast(cmax[:], 2, [P, TT * NH, NBLK]), ALU.subtract).then_inc(max_done, 1)
                copy_pT(L, 11)
                dve.wait_ge(exp_done, N_ATT * L + 13)
                for t in range(TT):
                    ins = V.tensor_reduce(rsum[:, 2, t].rearrange("p (g i) -> p i g", g=NG),
                                          sc[:, t].rearrange("p (i g) c -> p i g c", g=NG), AX.X, ALU.add)
                chain.mark(ins)
                chain.wait()
                for t in range(TT):
                    ins = V.tensor_tensor(sc[:, t], sc[:, t], bcast(cst[:, C_M01 + NBLK * t:C_M01 + NBLK * (t + 1)], 1,
                                                                    [P, NH, NBLK]), ALU.mult)
                ins.then_inc(cmp_p, 1)
                combine(L, 3, chain)
                copy_pT(L, 12)
                copy_squares(L, 1)
                for t in range(TT):
                    combine(L, 4 + t, chain)
                    chain.wait()
                    chain.mark(V.tensor_tensor(part[:, 1, :], acc[:, t, :], acc[:, t, :], ALU.mult))
                    chain.wait()
                    V.tensor_reduce(mstat[:, t, :], part[:, 1, :].rearrange("p (h d) -> p h d", h=NH), AX.X, ALU.add).then_inc(att_ss, 1)
                for b in range(2):
                    dve.wait_ge(bc_done, 2 * L + b + 1)
                    half = conv_o[:, 2 * b:2 * b + 2, :].rearrange("p c n -> p (c n)")
                    V.tensor_tensor(half, half, bank[4 + b][:], ALU.mult).then_inc(conv_norm, 1)
                for j in range(4):
                    dve.wait_ge(mix_hi, 8 * L + j + 1)
                    mix_low(L, j, conv_o[:, j, :])
                for t in range(TT):
                    dve.wait_ge(att_root, 2 * L + t + 1)
                    a = acc[:, t, :].rearrange("p (h d) -> p h d", h=NH)
                    V.tensor_tensor(a, a, bcast(mroot[:, t, :], 2, [P, NH, HEAD]), ALU.mult).then_inc(att_ready, 1)
                split_lo(V, L, 14)
                for j in range(4):
                    dve.wait_ge(mix_hi, 8 * L + 4 + 2 * (j // 2) + 2)
                    mix_low(L, 4 + j, bank[6 + j // 2][:, SEQ * (j % 2):SEQ * (j % 2 + 1)])
                split_lo(V, L, 16)
                layer_norm(L, 0, 0, 4, x1_ready, chain)
                x_low(L, 0, 0, x1T_hi, x1T_lo)
                layer_norm(L, 0, 1, 4, x1_ready, chain)
                split_lo(V, L, 18)
                x_low(L, 0, 1, x1T_hi, x1T_lo)
                split_lo(V, L, 19)
                ffn_step(L, 0, 0, (15, 0), (16, 0), [(21, 0), (22, 0)])
                with dve.Fori(0, (STEPS - 3) // 2) as i:
                    ffn_step(L, 2 * i + 1, 1, (17, i), (18, i), [(24, i), (25, i)])
                    ffn_step(L, 2 * i + 2, 0, (20, i), (21, i), [(27, i), (28, i)])
                last = (STEPS - 3) // 2
                ffn_step(L, STEPS - 2, 1, (17, last), (18, last), [(NU - 1, 0)])
                ffn_step(L, STEPS - 1, 0, (20, last), (21, last), [])
                for t in range(TT):
                    layer_norm(L, 1, t, 0, x_ready, chain)
                chain.close()

        @block.tensor
        def _(pe):
            def mm3(dst, ah, al, bh, bl, start, stop):
                pe.matmul(dst, ah, bh, start=start, stop=False)
                pe.matmul(dst, ah, bl, start=False, stop=False)
                return pe.matmul(dst, al, bh, start=False, stop=stop)

            def wait_unit(L, u, i=0):
                pe.wait_ge(split_done[u % RAWS], CREDIT + raw_round(L, u, i) + 1)

            def free_unit(ins, u):
                ins.then_inc(slot_free[u % SLOTS], 1)

            def w_view(u, k):
                return (ring_hi[u % SLOTS][:].rearrange("p (k n) -> p k n", k=k),
                        ring_lo[u % SLOTS][:].rearrange("p (k n) -> p k n", k=k))

            def transpose_x(L, ready, banks, t, done):
                for b in range(2):
                    pe.wait_ge(ready, 4 * L + 2 * t + b + 1)
                    for k in range(4):
                        ins = pe.transpose(bank[banks + 2 * t + b][:, P * k:P * (k + 1)],
                                           x_tok[:, t, P * (4 * b + k):P * (4 * b + k + 1)], ident)
                    ins.then_inc(done, 1)

            def conv_unit(L, idx, part, half=None):
                u = U_CONV + idx
                if part == 0 and half in (None, 0):
                    wait_unit(L, u)
                    if idx < 2:
                        pe.wait_ge(qkv_copied, 6 * L + 5 + idx)
                    elif idx == 2:
                        pe.wait_ge(c_copied, 2 * L + 1)
                    elif idx == 3:
                        pe.wait_ge(z_done, 2 * L + 1)
                    elif idx == 4:
                        pe.wait_ge(conv_out, 2 * L + 1)
                    else:
                        pe.wait_ge(c_copied, 2 * L + 2)
                wh, wl = w_view(u, KT)
                cols = slice(P * part, P * (part + 1))
                for k in range(KT) if half is None else range(4 * half, 4 * half + 4):
                    ins = mm3(bank[4 + idx % 2][:, SEQ * part:SEQ * (part + 1)], wh[:, k, cols], wl[:, k, cols],
                              xh[:, k, :], xl[:, k, :], k == 0, k == KT - 1)
                if part and half in (None, 1):
                    free_unit(ins, u)

            def scores(L, n):
                br, t, g, heads, kb = ATT[n]
                dst = bank[n % 2]
                if n == 0:
                    pe.wait_ge(qkT_copied, 3 * L + 3)
                elif n == 1:
                    pe.wait_ge(cmpA_copied, L + 1)
                else:
                    pe.wait_ge(exp_done, N_ATT * L + n - 1)
                rows = slice(HEAD * g, HEAD * (g + 1))
                keys = P * kb
                for j, h in enumerate(heads):
                    pe.matmul(dst[:, keys * j:keys * (j + 1)], qT[rows, h, P * t:P * (t + 1)], kT[rows, br, 0:keys],
                              start=(j == 0), stop=False, skip_group_check=True)
                diag = dst[:].rearrange("p (h k) -> p h k", k=keys)[:, :, keys - P:keys]
                pe.matmul(diag, ident_b[:], bcast(cmask_b[:], 1, [P, len(heads), P]), start=False, stop=True,
                          skip_group_check=True).then_inc(s_done, 1)

            def transpose_p(L, n):
                pe.wait_ge(exp_done, N_ATT * L + n + 1)
                if n >= 2:
                    pe.wait_ge(pT_copied, N_ATT * L + n - 1)
                for m in range(4):
                    ins = pe.transpose(bank[6 + n % 2][:, P * m:P * (m + 1)], probs[n % 2][:, P * m:P * (m + 1)], ident)
                ins.then_inc(pT_done, 1)

            def times_v(L, n):
                br, t, g, heads, kb = ATT[n]
                pe.wait_ge(pT_copied, N_ATT * L + n + 1)
                if n in O_READY:
                    pe.wait_ge(o_read, 6 * L + O_READY.index(n) + 1)
                elif n == 0:
                    pe.wait_ge(cmp_copied, 2 * L + 1)
                v0 = (16 if br == 0 else 18) * HEAD + HEAD * g
                for j, h in enumerate(heads):
                    for b in range(kb):
                        ins = pe.matmul(bank[2][:, HEAD * (NPAIR * g + h):HEAD * (NPAIR * g + h + 1)],
                                        probsT[n % 2][:, P * (kb * j + b):P * (kb * j + b + 1)], qkv[:, b, v0:v0 + HEAD],
                                        start=(b == 0), stop=(b == kb - 1))
                ins.then_inc(pv_done, 1)

            def cmp_hidden(L, kv):
                for half in range(2):
                    pe.wait_ge(w1_in[half], 16 * (2 * L + kv + 1))
                    for j in range(8):
                        for h in range(2):
                            rhs = cmpA[:, kv, :, 8 * half + j:8 * half + j + 8 * (NBLK - 1) + 1:8]
                            ins = pe.matmul(bank[2 + kv][:, 48 * h:48 * h + 45].rearrange("p (g c) -> p g c", g=3),
                                            w1_raw[:, half, CMP_HID * j + P * h:CMP_HID * j + P * (h + 1)], rhs,
                                            start=(half == 0 and j == 0 and h == 0), stop=(half == 1 and j == 7),
                                            skip_group_check=True)
                    ins.then_inc(hid_done, 1)

            def cmp_k(L):
                pe.wait_ge(hid_ready, 2 * L + 1)
                for g in range(NG):
                    dst = bank[2][HEAD * g:HEAD * (g + 1), 128:128 + NBLK]
                    for h in range(2):
                        pe.matmul(dst, w2[:, 0, h, :], hk[:, h, NBLK * g:NBLK * (g + 1)], start=(h == 0), stop=False)
                    ins = pe.matmul(dst, b2[0:1, 0, :], ones[0:1, 0:NBLK], start=False, stop=True)
                ins.then_inc(cmp_done, 1)

            def cmp_v(L):
                pe.wait_ge(hid_ready, 2 * L + 2)
                dst = bank[3][0:NH * NBLK, 128:128 + HEAD]
                for h in range(2):
                    pe.matmul(dst, hv[:, h, :], w2[:, 1, h, :], start=(h == 0), stop=False)
                pe.matmul(dst, ones[0:1, 0:NH * NBLK], b2[0:1, 1, :], start=False, stop=True).then_inc(cmp_done, 1)

            def cmp_scores(L):
                pe.wait_ge(exp_done, N_ATT * L + 11)
                pe.wait_ge(cmp_copied, 2 * L + 1)
                for t in range(TT):
                    for h in range(NPAIR):
                        c0 = NG * NBLK * (NPAIR * t + h)
                        ins = pe.matmul(bank[0][:, c0:c0 + NG * NBLK], qT[:, h, P * t:P * (t + 1)],
                                        kcT[:].rearrange("p g c -> p (g c)"), start=True, stop=True)
                ins.then_inc(s_done, 1)

            def transpose_cmp(L):
                pe.wait_ge(cmp_p, L + 1)
                pe.wait_ge(pT_copied, N_ATT * L + 11)
                for t in range(TT):
                    ins = pe.transpose(bank[6][0:NH * NBLK, P * t:P * (t + 1)],
                                       probs[0][:, NH * NBLK * t:NH * NBLK * (t + 1)], ident)
                ins.then_inc(pT_done, 1)

            def times_v_cmp(L, t):
                pe.wait_ge(pT_copied, N_ATT * L + 13)
                pe.wait_ge(cmp_copied, 2 * L + 2)
                pe.wait_ge(o_read, 6 * L + 4 + t)
                pe.matmul(bank[2][:], probsT[0][0:NH * NBLK, P * t:P * (t + 1)], vbd.rearrange("p h d -> p (h d)"),
                          start=True, stop=True).then_inc(pv_done, 1)

            def mean_squares(L, pair):
                pe.wait_ge(sq_done, 2 * L + pair + 1)
                if pair == 0:
                    pe.wait_ge(cmp_copied, 2 * L + 2)
                for t in range(TT):
                    for m in range(2):
                        c0 = 8 * pair + 4 * t + 2 * m
                        ins = pe.matmul(bank[3][:, c0:c0 + 2], conv_sq[:, m, P * t:P * (t + 1)], cst[:, C_BLK:C_BLK + 2],
                                        start=True, stop=True)
                ins.then_inc(ms_used, 1)

            def conv_roots(L, pair):
                pe.wait_ge(conv_root, 2 * L + pair + 1)
                pe.wait_ge(conv_out, 2 * L + 2)
                for m in range(2):
                    for t in range(TT):
                        for h in range(2):
                            ins = pe.matmul(bank[4 + pair][HEAD * h:HEAD * (h + 1), SEQ * m + P * t:SEQ * m + P * (t + 1)],
                                            croot[:, pair, t, 2 * m + h:2 * m + h + 1].to_broadcast([P, HEAD]), ident,
                                            start=True, stop=True)
                            if pair and m == 0 and t == 0 and h == 0:
                                ins.then_inc(stage_free, 1)
                ins.then_inc(bc_done, 1)

            def up(L, s, odd, value, gate):
                G = L * STEPS + s
                for v, u in enumerate((value, gate)):
                    wait_unit(L, *u)
                    pe.wait_ge(fy_done, FY_CREDIT + 2 * (G - 2) + v + 1)
                    wh, wl = w_view(u[0], KT)
                    for c in range(2):
                        for k in range(KT):
                            ins = mm3(bank[4 + 2 * odd + v][:, SEQ * c:SEQ * (c + 1)], wh[:, k, P * c:P * (c + 1)],
                                      wl[:, k, P * c:P * (c + 1)], xh[:, k, :], xl[:, k, :], k == 0, k == KT - 1)
                    free_unit(ins, u[0])

            def down(L, s, odd, u, first=False, last=False):
                wait_unit(L, *u)
                pe.wait_ge(h_lo, H_CREDIT + L * STEPS + s + 1)
                wh, wl = w_view(u[0], 2)
                for t in range(TT):
                    tok = slice(P * t, P * (t + 1))
                    for c in range(2):
                        for n in range(2):
                            col = slice(512 * n, 512 * (n + 1))
                            ins = mm3(bank[2 * t + n][:], hTh[:, odd, c, tok], hTl[:, odd, c, tok], wh[:, c, col], wl[:, c, col],
                                      first and c == 0, last and c == 1)
                    if last and t == 0:
                        ins.then_inc(y2_done, 1)
                free_unit(ins, u[0])

            pe.wait_ge(masks_ready, 2)
            pe.wait_ge(const_ready, 4)
            with pe.Fori(0, DEPTH) as L:
                pe.wait_ge(par_in, 16 * 8 * (L + 1))
                settled(pe)
                nf = 4 * STEPS
                for k in range(4):
                    pe.transpose(bank[4][:, nf * k:nf * (k + 1)], ffn_stage[:, k, :], ident[0:nf, 0:nf])
                pe.transpose(bank[4][:, 4 * nf:4 * nf + 56], par_stage[:], ident[0:56, 0:56]).then_inc(par_T, 1)
                pe.wait_ge(par_ready, L + 1)
                for t in range(TT):
                    transpose_x(L, x_ready, 4, t, xT_done)
                for first, nk, b0 in ((0, 4, 0), (2, 4, 2), (4, 8, 4)):
                    for u in range(first, first + KT // nk):
                        wait_unit(L, u)
                        wh, wl = w_view(u, nk)
                        for t in range(TT):
                            if first == 0:
                                pe.wait_ge(xT_lo, 4 * L + 2 * (t + 1))
                            if first == 4:
                                pe.wait_ge(gate_lo, L + 1)
                            tok = slice(P * t, P * (t + 1))
                            for kk in range(nk):
                                k = nk * (u - first) + kk
                                ins = mm3(bank[b0 + t][:, 0:UNIT // nk], xh[:, k, tok], xl[:, k, tok], wh[:, kk, :], wl[:, kk, :],
                                          k == 0, k == KT - 1)
                            if t:
                                free_unit(ins, u)
                            elif first < 4 and u == first + 1:
                                ins.then_inc(proj_done, 1)
                            if first == 4:
                                for k in range(KT):
                                    ins = mm3(bank[4 + t][:, 256:256 + NGATE], xh[:, k, tok], xl[:, k, tok], gate_wh[:, k, :],
                                              gate_wl[:, k, :], k == 0, k == KT - 1)
                                ins.then_inc(proj_done, 1)
                for part in range(2):
                    conv_unit(L, 0, part)
                for b in range(2):
                    for t in range(TT):
                        pe.wait_ge(rope_done, 2 * L + t + 1)
                        for m in range(2):
                            h = 2 * b + m
                            ins = pe.transpose(bank[6 + b][:, SEQ * m + P * t:SEQ * m + P * (t + 1)], qkv[:, t, P * h:P * (h + 1)], ident)
                    ins.then_inc(qkT_done, 1)
                for m in range(2):
                    for t in range(TT):
                        col = (10 + 2 * m) * HEAD
                        ins = pe.transpose(bank[0][:, SEQ * m + P * t:SEQ * m + P * (t + 1)], qkv[:, t, col:col + P], ident)
                ins.then_inc(qkT_done, 1)
                for kv in range(2):
                    for g in range(NG):
                        col = (8 + 6 * kv + g) * HEAD
                        for t in range(TT):
                            for odd in range(2):
                                dst = 256 * kv + P * g + 64 * t
                                ins = pe.matmul(bank[1][HEAD * odd:HEAD * (odd + 1), dst:dst + 64], qkv[:, t, col:col + HEAD],
                                                ident[:, odd:P:2], start=True, stop=True)
                ins.then_inc(qkT_done, 1)
                for part in range(2):
                    conv_unit(L, 1, part)
                scores(L, 0)
                pe.wait_ge(cmpA_copied, L + 1)
                cmp_hidden(L, 0)
                scores(L, 1)
                for part in range(2):
                    conv_unit(L, 2, part)
                cmp_k(L)
                transpose_p(L, 0)
                cmp_hidden(L, 1)
                pieces = [(idx, part, half) for idx in (3, 4, 5) for part in range(2) for half in range(2)]
                per_unit = [2, 2, 2, 2, 1, 1, 1, 1, 0, 0, 0, 0]
                for n in range(12):
                    if n < 10:
                        scores(L, n + 2)
                    elif n == 10:
                        cmp_scores(L)
                    if n < 11:
                        transpose_p(L, n + 1)
                    for _ in range(per_unit[n]):
                        conv_unit(L, *pieces.pop(0))
                    if n == 0:
                        cmp_v(L)
                    if n == 2:
                        mean_squares(L, 0)
                    if n == 11:
                        transpose_cmp(L)
                    times_v(L, n)
                mean_squares(L, 1)
                for t in range(TT):
                    times_v_cmp(L, t)
                for pair in range(2):
                    conv_roots(L, pair)
                pe.wait_ge(pT_copied, N_ATT * L + 13)
                for t in range(TT):
                    pe.wait_ge(att_ready, 2 * L + t + 1)
                    for j in range(4):
                        ins = pe.transpose(bank[6 + j // 2][:, SEQ * (j % 2) + P * t:SEQ * (j % 2) + P * (t + 1)],
                                           acc[:, t, P * j:P * (j + 1)], ident)
                        if t and j % 2:
                            ins.then_inc(mixT_done, 1)
                for t in range(TT):
                    for n in range(4):
                        u = U_OUT + n
                        if t == 0:
                            wait_unit(L, u)
                        wh, wl = w_view(u, 2)
                        for kk in range(2):
                            k = 2 * n + kk
                            if t == 0:
                                pe.wait_ge(mix_lo, 8 * L + k + 1)
                            for c in range(2):
                                ins = mm3(bank[4 + 2 * t + c][:], xh[:, k, P * t:P * (t + 1)], xl[:, k, P * t:P * (t + 1)],
                                          wh[:, kk, 512 * c:512 * (c + 1)], wl[:, kk, 512 * c:512 * (c + 1)], k == 0, k == KT - 1)
                        if t:
                            free_unit(ins, u)
                    if t == 0:
                        ins.then_inc(y1_done, 1)
                for t in range(TT):
                    transpose_x(L, x1_ready, 0, t, x1T_done)
                pe.wait_ge(x1T_lo, 4 * L + 4)
                up(L, 0, 0, (15, 0), (16, 0))
                up(L, 1, 1, (17, 0), (18, 0))
                down(L, 0, 0, (19, 0), first=True)
                up(L, 2, 0, (20, 0), (21, 0))
                down(L, 1, 1, (22, 0))
                with pe.Fori(1, STEPS // 2) as i:
                    up(L, 2 * i + 1, 1, (17, i), (18, i))
                    down(L, 2 * i, 0, (19, i))
                    up(L, 2 * i + 2, 0, (20, i), (21, i))
                    down(L, 2 * i + 1, 1, (22, i))
                down(L, STEPS - 1, 0, (NU - 1, 0), last=True)


_INS = ['x', 'w_in', 'short_conv_w', 'cmp_pe', 'cmp_w1', 'cmp_b1', 'cmp_w2', 'cmp_b2', 'head_norm_g', 'w_out', 'ln1_g',
        'ln1_b', 'w_up', 'ffn_conv_w', 'ffn_conv_b', 'w_down', 'ln2_g', 'ln2_b']


def kernel(**inputs):
    import concourse.bacc as bacc
    from concourse.bass_utils import run_bass_kernel_spmd

    nc = bacc.Bacc("TRN2", target_bir_lowering=False, num_devices=1, dynamic_dma_scratch_size=256)
    arrays, args = {}, []
    for name in _INS:
        a = np.ascontiguousarray(inputs[name])
        arrays[f"in_{name}"] = a
        args.append(nc.dram_tensor(f"in_{name}", a.shape, mybir.dt.from_np(a.dtype), kind="ExternalInput").ap())
    arrays["in_consts"] = shape_constants()
    args.append(nc.dram_tensor("in_consts", (P, C_ALL), mybir.dt.float32, kind="ExternalInput").ap())
    args.append(nc.dram_tensor("out_0", (1, SEQ, D_MODEL), mybir.dt.float32, kind="ExternalOutput").ap())
    build(nc, *args)
    return run_bass_kernel_spmd(nc, [arrays], core_ids=[0]).results[0]["out_0"]
```

```python
from contextlib import ExitStack

import concourse.bass as bass
import numpy as np
from concourse import mybir

P = 128
D_MODEL, SEQ, DEPTH, HEAD = 1024, 256, 2, 64
KT = D_MODEL // P
TT = SEQ // P
CONV_W, ATTN_W, KV_W = 512, 512, 128
NH, NG = ATTN_W // HEAD, 2
NPAIR = NH // NG
ROPE = HEAD // 4
NBLK = SEQ // 16 - 1
NJ = 16
CMP_HID = 256
D_FF = 2816
STEPS = D_FF // (2 * P)
ALPHA = (2.0 * DEPTH) ** 0.25
SCALE = HEAD ** -0.5
MASKED = -1e30
Q0, KV0, KW0, G0COL = 3 * CONV_W, 3 * CONV_W + ATTN_W, 3 * CONV_W + ATTN_W + 4 * KV_W, 3 * CONV_W + ATTN_W + 6 * KV_W
NGATE = NH * 3

UNIT = 2048
RAWS, SLOTS = 3, 6
CONV_U = (5, 6, 9, 12, 13, 14)
W1_U = ((7, 8), (10, 11))
U_OUT, U_FFN = 15, 19
NU = U_FFN + 3 * STEPS
RAW_USES = [len(range(i, NU, RAWS)) for i in range(RAWS)]
SLOT_USES = [len(range(i, NU, SLOTS)) for i in range(SLOTS)]
N_ATT = 13

C_ID, C_CM, C_CC, C_SS = 0, 128, 256, 288
C_MA, C_M01, C_BM, C_BLK = 320, 350, 380, 388
C_ALL = C_BLK + 2


def shape_constants():
    c = np.zeros((P, C_ALL), np.float32)
    p = np.arange(P)
    c[:, C_ID:C_ID + P] = np.eye(P)
    c[:, C_CM:C_CM + P] = np.where(p[None, :] > p[:, None], MASKED, 0.0)
    half = ROPE // 2
    inv_freq = (500000.0 ** (-(np.arange(half, dtype=np.float32) * 2.0 / ROPE))).astype(np.float32)
    for t in range(TT):
        ang = (p + P * t).astype(np.float32)[:, None] * inv_freq[None]
        cos, sin = np.cos(ang), np.sin(ang)
        c[:, C_CC + 16 * t:C_CC + 16 * t + 16] = np.concatenate([cos, cos], 1)
        c[:, C_SS + 16 * t:C_SS + 16 * t + 16] = np.concatenate([-sin, sin], 1)
        seen = (np.arange(NBLK)[None] * 16 + 31) <= (p + P * t)[:, None]
        c[:, C_MA + NBLK * t:C_MA + NBLK * (t + 1)] = np.where(seen, 0.0, MASKED)
        c[:, C_M01 + NBLK * t:C_M01 + NBLK * (t + 1)] = seen
    pos = p[:, None] // NBLK
    c[:, C_BM:C_BM + NH] = NPAIR * (pos % NG) + pos // NG == np.arange(NH)[None]
    c[:, C_BLK:C_BLK + 2] = (p[:, None] // HEAD == np.arange(2)[None]) / HEAD
    return c


class Chain:

    def __init__(self, eng, sem, layer, per_layer):
        self.eng, self.sem, self.base, self.per_layer, self.k = eng, sem, layer * per_layer, per_layer, 0

    def mark(self, ins):
        ins.then_inc(self.sem, 1)
        self.k += 1

    def wait(self):
        self.eng.wait_ge(self.sem, self.base + self.k)

    def close(self):
        assert self.k == self.per_layer, (self.k, self.per_layer)


def att_units():
    out = []
    for br in range(2):
        for t in range(TT):
            for g in range(NG):
                n = NPAIR // (t + 1)
                for part in range(t + 1):
                    out.append((br, t, g, range(part * n, part * n + n), t + 1))
    return out


ATT = att_units()
O_READY = [2, 6, 8, 12, 13, 14]

DVE_STEPS, POOL_STEPS = 69, 8
CREDIT = 1
FY_CREDIT = 4
H_CREDIT = 2


def build(nc, x, w_in, short_conv_w, cmp_pe, cmp_w1, cmp_b1, cmp_w2, cmp_b2, head_norm_g, w_out, ln1_g, ln1_b,
          w_up, ffn_conv_w, ffn_conv_b, w_down, ln2_g, ln2_b, consts, out):
    fp32, f32r, bf16 = mybir.dt.float32, mybir.dt.float32r, mybir.dt.bfloat16
    ALU, ACT, AX = mybir.AluOpType, mybir.ActivationFunctionType, mybir.AxisListType

    with ExitStack() as ctx:
        def sb(name, shape, dt=fp32):
            return ctx.enter_context(nc.sbuf_tensor(name, shape, dt))

        def sem(name):
            return ctx.enter_context(nc.semaphore(name))

        raw = [sb(f"raw{i}", [P, UNIT]) for i in range(RAWS)]
        ring_hi = [sb(f"ring_hi{i}", [P, UNIT], f32r) for i in range(SLOTS)]
        ring_lo = [sb(f"ring_lo{i}", [P, UNIT], f32r) for i in range(SLOTS)]
        x_tok = sb("x_tok", [P, TT, D_MODEL])
        xh = sb("xh", [P, KT, SEQ], f32r)
        xl = sb("xl", [P, KT, SEQ], f32r)
        cst = sb("cst", [P, C_ALL])
        ident = cst[:, C_ID:C_ID + P]
        ident_b = sb("ident_b", [P, P], bf16)
        ident_r = sb("ident_r", [P, P], f32r)
        cmask_b = sb("cmask_b", [P, P], bf16)
        ones = sb("ones", [1, P])
        neg_half = sb("neg_half", [P, 1])
        stage = sb("stage", [P, 4 * P])
        ffn_stage = stage[0:4 * STEPS, :].rearrange("c (k p) -> c k p", k=4)
        par_stage = sb("par_stage", [56, P])
        ffn_par = sb("ffn_par", [P, STEPS, 2, 2, 4])
        step_par = sb("step_par", [P, 2, 2, 2, 4])
        par = sb("par", [P, 56])
        gate_w = sb("gate_w", [P, KT, NGATE])
        gate_wh = sb("gate_wh", [P, KT, NGATE], f32r)
        gate_wl = sb("gate_wl", [P, KT, NGATE], f32r)
        qkv = sb("qkv", [P, TT, 20 * HEAD])
        ln_par = qkv[:, :, :].rearrange("p t f -> p (t f)")[:, 0:2 * D_MODEL].rearrange("p (a f) -> p a f", a=2)
        work = sb("work", [P, 2048])
        acc = work[:, 0:1024].rearrange("p (t f) -> p t f", t=TT)
        part = work[:, 1024:2048].rearrange("p (t f) -> p t f", t=TT)
        ffn_y = work[:].rearrange("p (s v c n) -> p s v c n", s=2, v=2, c=2)
        w2 = sb("w2", [P, 2, 2, HEAD])
        b2 = sb("b2", [1, 2, HEAD])
        egate = sb("egate", [P, TT, NGATE])
        qTh = sb("qTh", [P, NPAIR, SEQ], f32r)
        qTl = sb("qTl", [P, NPAIR, SEQ], f32r)
        kTh = sb("kTh", [P, 2, SEQ], f32r)
        kTl = sb("kTl", [P, 2, SEQ], f32r)
        blocks = [part[:, :, :].rearrange("p t f -> p (t f)")[:, 480 * kv:480 * (kv + 1)]
                  .rearrange("p (j b) -> p j b", j=NJ) for kv in range(2)]
        hid = sb("hid", [NG * NBLK, CMP_HID])
        hx = sb("hx", [P, 2, 2 * NBLK])
        hu = sb("hu", [P, 2, 2 * NBLK])
        ht = sb("ht", [P, 2, 2 * NBLK])
        hk = sb("hk", [P, 2, 2 * NBLK])
        hv = sb("hv", [P, 2, NH * NBLK])
        kcTh = sb("kcTh", [P, NG, NBLK], f32r)
        kcTl = sb("kcTl", [P, NG, NBLK], f32r)
        vbd = stage[0:NH * NBLK, :].rearrange("p (h d) -> p h d", h=NH)
        probs = [sb(f"probs{i}", [P, 512]) for i in range(2)]
        probsT = [sb(f"probsT{i}", [P, 512]) for i in range(2)]
        smax = sb("smax", [P, N_ATT - 1, NPAIR])
        cmax = sb("cmax", [P, TT * NH])
        nmax = sb("nmax", [P, 2, NPAIR])
        rsum = sb("rsum", [P, 3, TT, NH])
        coef = sb("coef", [P, 3, TT, NH])
        mstat = sb("mstat", [P, TT, NH])
        mroot = sb("mroot", [P, TT, NH])
        conv_z = sb("conv_z", [P, 2, SEQ])
        conv_y = sb("conv_y", [P, 2, SEQ])
        conv_o = sb("conv_o", [P, 4, SEQ])
        conv_sq = sb("conv_sq", [P, 2, SEQ])
        rope_a, rope_b = (conv_sq[:, n, 0:14 * ROPE].rearrange("p (h d) -> p h d", h=14) for n in range(2))
        cstat = sb("cstat", [P, 2, TT, 4])
        croot = sb("croot", [P, 2, TT, 4])
        hTh = sb("hTh", [P, 2, 2, SEQ], f32r)
        hTl = sb("hTl", [P, 2, 2, SEQ], f32r)
        blocks_h, blocks_l = ([a[:, kv].rearrange("p c n -> p (c n)")[:, 0:480].rearrange("p (j b) -> p j b", j=NJ)
                               for kv in range(2)] for a in (hTh, hTl))
        roots_h, roots_l = (a[:].rearrange("p a (t c) n -> p a t (c n)", t=TT) for a in (hTh, hTl))
        stats = sb("stats", [P, TT, 2, 6])
        mv = sb("mv", [P, TT, 2])
        veps = sb("veps", [P, TT])
        rstd = sb("rstd", [P, TT])
        bank = [ctx.enter_context(nc.psum_tensor(f"bank{i}", [P, 512], fp32)) for i in range(8)]

        raw_in = [sem(f"raw_in{i}") for i in range(RAWS)]
        split_done = [sem(f"split_done{i}") for i in range(RAWS)]
        slot_free = [sem(f"slot_free{i}") for i in range(SLOTS)]
        hi_done = sem("hi_done")
        x_in, ident_in = [sem("x_in0"), sem("x_in1")], sem("ident_in")
        const_in, par_in, gate_in = sem("const_in"), sem("par_in"), sem("gate_in")
        ln_in, out_done, stage_free = sem("ln_in"), sem("out_done"), sem("stage_free")
        const_ready, masks_ready = sem("const_ready"), sem("masks_ready")
        par_T, par_ready, gate_hi, gate_lo = sem("par_T"), sem("par_ready"), sem("gate_hi"), sem("gate_lo")
        x_ready, xT_done, xT_hi, xT_lo = sem("x_ready"), sem("xT_done"), sem("xT_hi"), sem("xT_lo")
        x1_ready, x1T_done, x1T_hi, x1T_lo = sem("x1_ready"), sem("x1T_done"), sem("x1T_hi"), sem("x1T_lo")
        proj_done, qkv_copied, rope_done = sem("proj_done"), sem("qkv_copied"), sem("rope_done")
        qkT_done, qkT_copied, qkT_hi = sem("qkT_done"), sem("qkT_copied"), sem("qkT_hi")
        blocks_in, blocks_hi, blocks_lo = sem("blocks_in"), sem("blocks_hi"), sem("blocks_lo")
        hid_copied, hidT_done = sem("hid_copied"), sem("hidT_done")
        tanh_in, tanh_done, hid_ready = sem("tanh_in"), sem("tanh_done"), sem("hid_ready")
        cmp_done, kc_hi, cmp_copied = sem("cmp_done"), sem("kc_hi"), sem("cmp_copied")
        s_done, max_done, exp_done, cmp_p = sem("s_done"), sem("max_done"), sem("exp_done"), sem("cmp_p")
        pT_done, pT_copied, pv_done, o_read = sem("pT_done"), sem("pT_copied"), sem("pv_done"), sem("o_read")
        att_ss, att_root, att_ready, mixT_done = sem("att_ss"), sem("att_root"), sem("att_ready"), sem("mixT_done")
        c_copied, z_done, y_init = sem("c_copied"), sem("z_done"), sem("y_init")
        conv_out, sq_done, ms_used = sem("conv_out"), sem("sq_done"), sem("ms_used")
        ms_read, conv_root, roots_hi, roots_lo, bc_done, conv_norm = sem("ms_read"), sem("conv_root"), sem("roots_hi"), sem("roots_lo"), sem("bc_done"), sem("conv_norm")
        mix_hi, mix_lo, y1_done = sem("mix_hi"), sem("mix_lo"), sem("y1_done")
        ln_stats, ln_root = sem("ln_stats"), sem("ln_root")
        step_par_in, fy_init = sem("step_par_in"), sem("fy_init")
        fy_mid, fy_done = sem("fy_mid"), sem("fy_done")
        silu_done, h_done, h_hi, h_lo = sem("silu_done"), sem("h_done"), sem("h_hi"), sem("h_lo")
        y2_done = sem("y2_done")
        passed = sem("passed")
        dve_seq, pool_seq = sem("dve_seq"), sem("pool_seq")

        def raw_round(L, u, i=0):
            return L * RAW_USES[u % RAWS] + u // RAWS + 2 * i

        def slot_round(L, u, i=0):
            return L * SLOT_USES[u % SLOTS] + u // SLOTS + i

        def unit_used(eng, L, u, i=0):
            eng.wait_ge(slot_free[u % SLOTS], CREDIT + slot_round(L, u, i) + 1)

        def split_hi(act, L, u, i=0):
            act.wait_ge(raw_in[u % RAWS], 16 * (raw_round(L, u, i) + 1))
            act.wait_ge(slot_free[u % SLOTS], CREDIT + slot_round(L, u, i))
            nc.scalar.activation(ring_hi[u % SLOTS][:], raw[u % RAWS][:], ACT.Copy).then_inc(hi_done, 1)

        def split_lo(eng, L, u, i=0):
            eng.wait_ge(hi_done, L * NU + u + 6 * i + 1)
            eng.tensor_tensor(ring_lo[u % SLOTS][:], raw[u % RAWS][:], ring_hi[u % SLOTS][:].bitcast(fp32),
                              ALU.subtract).then_inc(split_done[u % RAWS], 1)

        def bcast(ap, axis, shape):
            return ap.unsqueeze(axis).to_broadcast(shape)

        def settled(eng):
            eng.sem_inc(passed, 1)

        block = ctx.enter_context(nc.Block())

        @block.sync
        def _(sp):
            def load(L, u, i, src, **view):
                dst = raw[u % RAWS][:]
                if view:
                    dst = dst.rearrange(view.pop("to"), **view)
                sp.wait_ge(split_done[u % RAWS], CREDIT + raw_round(L, u, i))
                settled(sp)
                sp.dma_start(dst, src).then_inc(raw_in[u % RAWS], 16)

            def of(w, L):
                return w[bass.ds(L, 1)].rearrange("o a b -> (o a) b")

            def load_in(L, u, k0, nk, col):
                src = of(w_in, L)[P * k0:P * (k0 + nk), col:col + UNIT // nk].rearrange("(k p) n -> p k n", p=P)
                load(L, u, 0, src, to="p (k n) -> p k n", k=nk)

            def load_w1(L, kv):
                for half, u in enumerate(W1_U[kv]):
                    src = cmp_w1[bass.ds(L, 1), kv, P * 8 * half:P * 8 * (half + 1), :].rearrange("o (j p) n -> p (o j) n", p=P)
                    load(L, u, 0, src, to="p (k n) -> p k n", k=8)

            def load_up(L, u, i, gate, step):
                src = of(w_up, L)[:, bass.ds(D_FF * gate + step * 2 * P, 2 * P)].rearrange("(k p) n -> p k n", p=P)
                load(L, u, i, src, to="p (k n) -> p k n", k=KT)

            def load_rows(L, u, i, w, row):
                src = of(w, L)[bass.ds(row, 2 * P), :].rearrange("(k p) n -> p k n", p=P)
                load(L, u, i, src, to="p (k n) -> p k n", k=2)

            sp.sem_inc(stage_free, CREDIT)
            for free in split_done:
                sp.sem_inc(free, CREDIT)
            with sp.Fori(0, DEPTH) as L:
                load_in(L, 0, 0, 4, Q0)
                load_in(L, 1, 4, 4, Q0)
                load_in(L, 2, 0, 4, KV0)
                sp.wait_ge(stage_free, CREDIT + L)
                sp.dma_start(gate_w[:], of(w_in, L)[:, G0COL:G0COL + NGATE].rearrange("(k p) n -> p k n", p=P)).then_inc(gate_in, 16)
                sp.dma_start(ffn_stage[:, 0:3, :], of(ffn_conv_w, L).rearrange("k (c p) -> c k p", p=P)).then_inc(par_in, 16)
                sp.dma_start(ffn_stage[:, 3, :], ffn_conv_b[bass.ds(L, 1)].rearrange("o (c p) -> (o c) p", p=P)).then_inc(par_in, 16)
                sp.dma_start(par_stage[0:8, :], head_norm_g[bass.ds(L, 1)].rearrange("o (c p) -> (o c) p", p=P)).then_inc(par_in, 16)
                sp.dma_start(par_stage[8:20, :], of(short_conv_w, L).rearrange("k (c p) -> (k c) p", p=P)).then_inc(par_in, 16)
                sp.dma_start(par_stage[20:24, :], of(cmp_b1, L).rearrange("k (c p) -> (k c) p", p=P)).then_inc(par_in, 16)
                sp.dma_start(par_stage[24:56, :], cmp_pe[bass.ds(L, 1)].rearrange("o k (j l) d -> (o k j) (l d)", l=2)).then_inc(par_in, 16)
                sp.dma_start(w2[:], cmp_w2[bass.ds(L, 1)].rearrange("o k (h p) d -> p (o k) h d", p=P)).then_inc(par_in, 16)
                sp.dma_start(b2[:], cmp_b2[bass.ds(L, 1)]).then_inc(par_in, 16)
                load_in(L, 3, 4, 4, KV0)
                load_in(L, 4, 0, 8, KW0)
                for pair in range(2):
                    for n, sect in enumerate((1, 2, 0)):
                        if pair == 0 and n == 2:
                            load_w1(L, 0)
                        load_in(L, CONV_U[3 * pair + n], 0, 8, CONV_W * sect + 2 * P * pair)
                    if pair == 0:
                        load_w1(L, 1)
                for n in range(4):
                    load_rows(L, U_OUT + n, 0, w_out, 2 * P * n)
                for s in range(3):
                    for gate in range(2):
                        load_up(L, U_FFN + 2 * s + gate, 0, gate, s)
                with sp.Fori(0, (STEPS - 3) // 2) as i:
                    for odd in range(2):
                        load_rows(L, 25 + 3 * odd, i, w_down, (2 * i + odd) * 2 * P)
                        for gate in range(2):
                            load_up(L, 26 + 3 * odd + gate, i, gate, 2 * i + 3 + odd)
                for s in range(STEPS - 3, STEPS):
                    load_rows(L, NU - STEPS + s, 0, w_down, s * 2 * P)
            for t in range(TT):
                sp.wait_ge(x_ready, 4 * DEPTH + 2 * (t + 1))
                sp.dma_start(out[0, P * t:P * (t + 1), :], x_tok[:, t, :]).then_inc(out_done, 16)
            sp.wait_ge(out_done, 16 * TT)

        @block.scalar
        def _(act):
            for free in slot_free:
                act.sem_inc(free, CREDIT)
            act.dma_start(x_tok[:, 0, :], x[0, 0:P, :]).then_inc(x_in[0], 16)
            act.dma_start(ident, consts[:, C_ID:C_ID + P]).then_inc(ident_in, 16)
            act.dma_start(x_tok[:, 1, :], x[0, P:2 * P, :]).then_inc(x_in[1], 16)
            act.dma_start(cst[:, P:], consts[:, P:]).then_inc(const_in, 16)
            act.wait_ge(ident_in, 16)
            nc.scalar.activation(ident_b[:], ident, ACT.Copy).then_inc(masks_ready, 1)
            nc.scalar.activation(ident_r[:], ident, ACT.Copy).then_inc(masks_ready, 1)

            def x_high(L, banks, t, done, hi):
                for b in range(2):
                    act.wait_ge(done, 4 * L + 2 * t + b + 1)
                    nc.scalar.activation(xh[:, 4 * b:4 * b + 4, P * t:P * (t + 1)],
                                         bank[banks + 2 * t + b][:].rearrange("p (k n) -> p k n", k=4),
                                         ACT.Copy).then_inc(hi, 1)

            def copy_q(L, t):
                if t == 0:
                    act.wait_ge(proj_done, 4 * L + 1)
                else:
                    unit_used(act, L, 1)
                nc.scalar.activation(qkv[:, t, 0:512].rearrange("p (i g d) -> p g i d", i=NPAIR, g=NG),
                                     bank[t][:].rearrange("p (g i d) -> p g i d", i=NPAIR, g=NG),
                                     ACT.Copy).then_inc(qkv_copied, 1)

            def kv_slots(t):
                return qkv[:, t, 512:1280].rearrange("p (b a f) -> p b a f", b=2, a=3)

            def copy_kv(L, t):
                if t == 0:
                    act.wait_ge(proj_done, 4 * L + 2)
                else:
                    unit_used(act, L, 3)
                for b in range(2):
                    ins = nc.scalar.activation(kv_slots(t)[:, b, 0:2, :],
                                               bank[2 + t][:].rearrange("p (a b f) -> p b a f", a=2, b=2)[:, b], ACT.Copy)
                ins.then_inc(qkv_copied, 1)

            def copy_kw(L, t):
                act.wait_ge(proj_done, 4 * L + 2 + t + 1)
                nc.scalar.activation(egate[:, t, :], bank[4 + t][:, 256:256 + NGATE], ACT.Exp, scale=-1.0)
                nc.scalar.activation(kv_slots(t)[:, :, 2, :], bank[4 + t][:, 0:256].rearrange("p (b f) -> p b f", b=2),
                                     ACT.Copy).then_inc(qkv_copied, 1)

            def copy_c(L, pair):
                unit_used(act, L, CONV_U[3 * pair])
                if pair:
                    act.wait_ge(conv_out, 2 * L + pair)
                nc.scalar.activation(conv_z[:].rearrange("p c n -> p (c n)"), bank[4 + pair][:], ACT.Copy).then_inc(c_copied, 1)

            def conv_init(L, pair):
                act.wait_ge(z_done, 2 * L + pair + 1)
                for m in range(2):
                    tap = 8 + 2 * 4 + 2 * pair + m
                    ins = nc.scalar.activation(conv_y[:, m, :], conv_z[:, m, :], ACT.Copy, scale=par[:, tap:tap + 1])
                ins.then_inc(y_init, 1)

            def conv_square(L, pair):
                act.wait_ge(conv_out, 2 * L + pair + 1)
                if pair:
                    act.wait_ge(ms_used, 2 * L + pair)
                nc.scalar.activation(conv_sq[:], conv_o[:, 2 * pair:2 * pair + 2, :], ACT.Square).then_inc(sq_done, 1)

            def copy_hidden(L, kv):
                unit_used(act, L, W1_U[kv][1])
                if kv:
                    act.wait_ge(hidT_done, 2 * L + 1)
                nc.scalar.activation(hid[:], bank[2 + kv][0:NG * NBLK, 0:CMP_HID], ACT.Copy).then_inc(hid_copied, 1)

            def tanh(L, kv):
                act.wait_ge(tanh_in, 2 * L + kv + 1)
                nc.scalar.activation(ht[:], hu[:], ACT.Tanh).then_inc(tanh_done, 1)

            def exps(L, n):
                br, t, g, heads, kb = ATT[n]
                keys = P * kb
                act.wait_ge(max_done, N_ATT * L + n + 1)
                if n >= 2:
                    act.wait_ge(pT_done, N_ATT * L + n - 1)
                for j, h in enumerate(heads):
                    ins = nc.scalar.activation(probs[n % 2][:, keys * j:keys * (j + 1)], bank[n % 2][:, keys * j:keys * (j + 1)],
                                               ACT.Exp, bias=nmax[:, n % 2, j:j + 1], scale=SCALE,
                                               accum_out=rsum[:, br, t, NPAIR * g + h:NPAIR * g + h + 1])
                ins.then_inc(exp_done, 1)

            def roots_high(L, pair):
                act.wait_ge(conv_root, 2 * L + pair + 1)
                nc.scalar.activation(roots_h[:, pair].rearrange("p t (h d) -> p (t h) d", d=HEAD),
                                     bcast(croot[:, pair].rearrange("p t h -> p (t h)"), 2, [P, 4 * TT, HEAD]),
                                     ACT.Copy).then_inc(roots_hi, 1)

            def mix_high(L, j, src):
                nc.scalar.activation(xh[:, j, :], src, ACT.Copy, scale=par[:, j:j + 1]).then_inc(mix_hi, 1)

            def ffn_step(L, s, odd, value, gate, h_user, units):
                G = L * STEPS + s
                act.wait_ge(step_par_in, G + 1)
                act.wait_ge(h_lo, H_CREDIT + G - 1)
                for v, u in enumerate((value, gate)):
                    unit_used(act, L, *u)
                    for c in range(2):
                        ins = nc.scalar.activation(ffn_y[:, odd, v, c, :], bank[4 + 2 * odd + v][:, SEQ * c:SEQ * (c + 1)],
                                                   ACT.Identity, scale=step_par[:, odd, v, c, 2:3],
                                                   bias=step_par[:, odd, v, c, 3:4])
                    ins.then_inc(fy_init, 1)
                for u in units[0:1]:
                    split_hi(act, L, *u)
                act.wait_ge(fy_done, FY_CREDIT + 2 * G + 2)
                y = ffn_y[:, odd].rearrange("p v c n -> p v (c n)")
                nc.scalar.activation(y[:, 1], y[:, 1], ACT.Silu).then_inc(silu_done, 1)
                for u in units[1:2]:
                    split_hi(act, L, *u)
                act.wait_ge(h_done, G + 1)
                if h_user:
                    unit_used(act, L, *h_user)
                nc.scalar.activation(hTh[:, odd].rearrange("p c n -> p (c n)"), y[:, 0], ACT.Copy).then_inc(h_hi, 1)
                for u in units[2:3]:
                    split_hi(act, L, *u)

            with act.Fori(0, DEPTH) as L:
                split_hi(act, L, 0)
                split_hi(act, L, 1)
                x_high(L, 4, 0, xT_done, xT_hi)
                split_hi(act, L, 2)
                split_hi(act, L, 3)
                x_high(L, 4, 1, xT_done, xT_hi)
                split_hi(act, L, 4)
                copy_q(L, 0)
                act.wait_ge(gate_in, 16 * (L + 1))
                nc.scalar.activation(gate_wh[:], gate_w[:], ACT.Copy).then_inc(gate_hi, 1)
                split_hi(act, L, 5)
                copy_kv(L, 0)
                copy_q(L, 1)
                split_hi(act, L, 6)
                copy_kv(L, 1)
                act.wait_ge(par_T, L + 1)
                for v in range(2):
                    nc.scalar.activation(
                        ffn_par[:, :, v].rearrange("p s c k -> p k s c"),
                        bank[6][:, 0:176].rearrange("p (k v s c) -> p k v s c", k=4, v=2, c=2)[:, :, v], ACT.Copy)
                nc.scalar.activation(par[:], bank[6][:, 176:232], ACT.Copy).then_inc(par_ready, 1)
                split_hi(act, L, 7)
                for t in range(TT):
                    copy_kw(L, t)
                copy_c(L, 0)
                split_hi(act, L, 8)
                for b, (dst, src) in enumerate(((qTh[:, 0:2, :], bank[6]), (qTh[:, 2:4, :], bank[7]), (kTh[:], bank[0]))):
                    act.wait_ge(qkT_done, 4 * L + b + 1)
                    nc.scalar.activation(dst.rearrange("p i n -> p (i n)"), src[:], ACT.Copy).then_inc(qkT_hi, 1)
                for kv in range(2):
                    act.wait_ge(blocks_in, 2 * L + kv + 1)
                    nc.scalar.activation(blocks_h[kv], blocks[kv], ACT.Copy).then_inc(blocks_hi, 1)
                split_hi(act, L, 9)
                conv_init(L, 0)
                exps(L, 0)
                copy_hidden(L, 0)
                split_hi(act, L, 10)
                tanh(L, 0)
                exps(L, 1)
                split_hi(act, L, 11)
                act.wait_ge(cmp_done, 2 * L + 1)
                for g in range(NG):
                    rows = slice(HEAD * g, HEAD * (g + 1))
                    ins = nc.scalar.activation(kcTh[rows, g, :], bank[2][rows, 384:384 + NBLK], ACT.Copy)
                ins.then_inc(kc_hi, 1)
                split_hi(act, L, 12)
                copy_hidden(L, 1)
                conv_square(L, 0)
                tanh(L, 1)
                between = {2: [lambda: split_hi(act, L, 13)], 3: [lambda: copy_c(L, 1)], 4: [lambda: split_hi(act, L, 14)],
                           6: [lambda: conv_init(L, 1)], 8: [lambda: split_hi(act, L, 15)], 9: [lambda: split_hi(act, L, 16)],
                           10: [lambda: conv_square(L, 1), lambda: roots_high(L, 0)], 11: [lambda: split_hi(act, L, 17)]}
                for n in range(2, 12):
                    exps(L, n)
                    for step in between.get(n, []):
                        step()
                act.wait_ge(max_done, N_ATT * L + 13)
                flat = probs[0][:, 0:TT * NH * NBLK]
                nc.scalar.activation(flat, flat, ACT.Exp, scale=SCALE).then_inc(exp_done, 1)
                split_hi(act, L, 18)
                roots_high(L, 1)
                for j in range(4):
                    act.wait_ge(conv_norm, 2 * L + j // 2 + 1)
                    mix_high(L, j, conv_o[:, j, :])
                for j in range(4):
                    if j % 2 == 0:
                        act.wait_ge(mixT_done, 2 * L + j // 2 + 1)
                    mix_high(L, 4 + j, bank[6 + j // 2][:, SEQ * (j % 2):SEQ * (j % 2 + 1)])
                act.wait_ge(pv_done, 14 * L + 14)
                act.wait_ge(rope_done, 2 * L + 2)
                for a, w in enumerate((ln1_g, ln1_b)):
                    act.dma_start(ln_par[:, a, :], w[bass.ds(L, 1)].to_broadcast([P, D_MODEL])).then_inc(ln_in, 16)
                split_hi(act, L, 19)
                split_hi(act, L, 20)
                x_high(L, 0, 0, x1T_done, x1T_hi)
                split_hi(act, L, 21)
                split_hi(act, L, 22)
                x_high(L, 0, 1, x1T_done, x1T_hi)
                for a, w in enumerate((ln2_g, ln2_b)):
                    act.dma_start(ln_par[:, a, :], w[bass.ds(L, 1)].to_broadcast([P, D_MODEL])).then_inc(ln_in, 16)
                split_hi(act, L, 23)
                split_hi(act, L, 24)
                ffn_step(L, 0, 0, (19, 0), (20, 0), None, [(25, 0), (26, 0)])
                ffn_step(L, 1, 1, (21, 0), (22, 0), None, [(27, 0), (28, 0)])
                ffn_step(L, 2, 0, (23, 0), (24, 0), (25, 0), [(29, 0), (30, 0), (31, 0)])
                with act.Fori(0, (STEPS - 5) // 2) as i:
                    ffn_step(L, 2 * i + 3, 1, (26, i), (27, i), (28, i), [(32, i), (33, i), (34, i)])
                    ffn_step(L, 2 * i + 4, 0, (29, i), (30, i), (31, i), [(35, i), (36, i), (37, i)])
                last = (STEPS - 5) // 2
                ffn_step(L, STEPS - 2, 1, (26, last), (27, last), (28, last), [(NU - 2, 0), (NU - 1, 0)])
                ffn_step(L, STEPS - 1, 0, (29, last), (30, last), (31, last), [])

        @block.gpsimd
        def _(pool):
            nc.gpsimd.memset(neg_half[:], -0.5).then_inc(const_ready, 1)
            nc.gpsimd.memset(kcTl[:].bitcast(fp32), 0.0).then_inc(const_ready, 1)
            nc.gpsimd.memset(ones[:], 1.0).then_inc(const_ready, 1)
            nc.gpsimd.memset(kcTh[:].bitcast(fp32), 0.0).then_inc(const_ready, 1)
            pool.wait_ge(const_ready, 4)

            def root(L, chain, var, eps_out, eps, mul, result, half, signal):
                settled(pool)
                chain.mark(nc.gpsimd.tensor_scalar(eps_out, var, mul, eps, ALU.mult, ALU.add))
                chain.wait()
                nc.gpsimd.tensor_tensor(result, eps_out, half, ALU.pow).then_inc(signal, 1)

            def conv_root_of(L, pair, chain):
                pool.wait_ge(ms_read, 2 * L + pair + 1)
                flat = [a[:, pair].rearrange("p t h -> p (t h)") for a in (cstat, croot)]
                root(L, chain, flat[0], flat[0], 1e-6, 1.0, flat[1], neg_half[:].to_broadcast([P, 4 * TT]), conv_root)

            def step_params(s, odd):
                settled(pool)
                nc.gpsimd.tensor_copy(step_par[:, odd].rearrange("p v c k -> p (v c k)"),
                                      ffn_par[:, bass.ds(s, 1)].rearrange("p o v c k -> p (o v c k)"))\
                    .then_inc(step_par_in, 1)

            def next_params(L, s, odd):
                pool.wait_ge(fy_done, FY_CREDIT + 2 * (L * STEPS + s) + 2)
                step_params(s + 2, odd)

            with pool.Fori(0, DEPTH) as L:
                chain = Chain(pool, pool_seq, L, POOL_STEPS)
                for u in (0, 2, 4, 5, 7, 8, 10, 11, 13):
                    split_lo(nc.gpsimd, L, u)
                conv_root_of(L, 0, chain)
                for u in range(14, 18):
                    split_lo(nc.gpsimd, L, u)
                conv_root_of(L, 1, chain)
                split_lo(nc.gpsimd, L, 18)
                for t in range(TT):
                    pool.wait_ge(att_ss, 2 * L + t + 1)
                    root(L, chain, mstat[:, t, :], mstat[:, t, :], 1e-6, 1.0 / HEAD, mroot[:, t, :], neg_half[:].to_broadcast([P, NH]), att_root)
                split_lo(nc.gpsimd, L, 19)
                split_lo(nc.gpsimd, L, 20)
                pool.wait_ge(par_ready, L + 1)
                for odd in range(2):
                    step_params(odd, odd)
                for t in range(TT):
                    pool.wait_ge(ln_stats, 4 * L + 1 + t)
                    root(L, chain, mv[:, t, 1:2], veps[:, t:t + 1], 1e-5, 1.0, rstd[:, t:t + 1], neg_half[:, 0:1], ln_root)
                for u in range(21, 25):
                    split_lo(nc.gpsimd, L, u)
                for s in range(3):
                    next_params(L, s, s % 2)
                    for u in (26 + 3 * s, 27 + 3 * s)[:2 * (s < 2)]:
                        split_lo(nc.gpsimd, L, u)
                with pool.Fori(0, (STEPS - 5) // 2) as i:
                    for odd in range(2):
                        split_lo(nc.gpsimd, L, 32 + 3 * odd, i)
                        split_lo(nc.gpsimd, L, 33 + 3 * odd, i)
                        next_params(L, 2 * i + 3 + odd, 1 - odd)
                for t in range(TT):
                    pool.wait_ge(ln_stats, 4 * L + 3 + t)
                    root(L, chain, mv[:, t, 1:2], veps[:, t:t + 1], 1e-5, 1.0, rstd[:, t:t + 1], neg_half[:, 0:1], ln_root)
                chain.close()

        @block.vector
        def _(dve):
            V = nc.vector
            for t in range(TT):
                dve.wait_ge(x_in[t], 16)
                dve.sem_inc(x_ready, 2)
            dve.sem_inc(fy_done, FY_CREDIT)
            dve.sem_inc(h_lo, H_CREDIT)
            dve.wait_ge(const_in, 16)
            V.tensor_copy(cmask_b[:], cst[:, C_CM:C_CM + P]).then_inc(masks_ready, 1)
            dve.wait_ge(const_ready, 4)

            def x_low(L, banks, t, hi, lo):
                for b in range(2):
                    dve.wait_ge(hi, 4 * L + 2 * t + b + 1)
                    dst = slice(4 * b, 4 * b + 4), slice(P * t, P * (t + 1))
                    V.tensor_tensor(xl[:, dst[0], dst[1]], bank[banks + 2 * t + b][:].rearrange("p (k n) -> p k n", k=4),
                                    xh[:, dst[0], dst[1]].bitcast(fp32), ALU.subtract).then_inc(lo, 1)

            def rope(L, t, chain):
                dve.wait_ge(qkv_copied, 6 * L + 5 + t)
                head = qkv[:, t, 0:14 * HEAD].rearrange("p (h d) -> p h d", d=HEAD)
                cc = bcast(cst[:, C_CC + 16 * t:C_CC + 16 * t + 16], 1, [P, 14, 16])
                ss = cst[:, C_SS + 16 * t:C_SS + 16 * t + 16]
                if t:
                    dve.wait_ge(rope_done, 2 * L + t)
                V.tensor_tensor(rope_a, head[:, :, 0:16], cc, ALU.mult)
                V.tensor_tensor(rope_b[:, :, 0:8], head[:, :, 8:16], bcast(ss[:, 0:8], 1, [P, 14, 8]), ALU.mult)
                chain.mark(V.tensor_tensor(rope_b[:, :, 8:16], head[:, :, 0:8], bcast(ss[:, 8:16], 1, [P, 14, 8]), ALU.mult))
                chain.wait()
                V.tensor_tensor(head[:, :, 0:16], rope_a, rope_b, ALU.add).then_inc(rope_done, 1)

            def conv_taps(L, pair, chain):
                dve.wait_ge(y_init, 2 * L + pair + 1)
                for back in (1, 2):
                    if back == 2:
                        chain.wait()
                    for m in range(2):
                        tap = 8 + (2 - back) * 4 + 2 * pair + m
                        ins = V.scalar_tensor_tensor(conv_y[:, m, back:], conv_z[:, m, 0:SEQ - back], par[:, tap:tap + 1],
                                                     conv_y[:, m, back:], ALU.mult, ALU.add)
                    chain.mark(ins)
                chain.wait()
                unit_used(dve, L, CONV_U[3 * pair + 2])
                V.tensor_tensor(conv_o[:, 2 * pair:2 * pair + 2, :].rearrange("p c n -> p (c n)"),
                                conv_y[:].rearrange("p c n -> p (c n)"), bank[4 + pair][:], ALU.mult).then_inc(conv_out, 1)

            def conv_gate(L, pair):
                unit_used(dve, L, CONV_U[3 * pair + 1])
                dve.wait_ge(c_copied, 2 * L + pair + 1)
                z = conv_z[:].rearrange("p c n -> p (c n)")
                V.tensor_tensor(z, z, bank[5 - pair][:], ALU.mult).then_inc(z_done, 1)

            def hidden(L, kv, chain):
                dve.wait_ge(hidT_done, 2 * L + kv + 1)
                if kv:
                    dve.wait_ge(hid_ready, 2 * L + 1)
                for h in range(2):
                    b1 = par[:, 20 + 2 * kv + h:21 + 2 * kv + h]
                    ins = V.tensor_scalar(hx[:, h, :], bank[2 + kv][:, 256 + 32 * h:286 + 32 * h], b1, None, ALU.add)
                chain.mark(ins)
                chain.wait()
                chain.mark(V.tensor_tensor(hu[:], hx[:], hx[:], ALU.mult))
                chain.wait()
                c = float(np.sqrt(2.0 / np.pi))
                chain.mark(V.tensor_scalar(hu[:], hu[:], 0.044715 * c, c, ALU.mult, ALU.add))
                chain.wait()
                V.tensor_tensor(hu[:], hu[:], hx[:], ALU.mult).then_inc(tanh_in, 1)
                dve.wait_ge(tanh_done, 2 * L + kv + 1)
                chain.mark(V.tensor_scalar(ht[:], ht[:], 0.5, 0.5, ALU.mult, ALU.add))
                chain.wait()
                if kv == 0:
                    V.tensor_tensor(hk[:], ht[:], hx[:], ALU.mult).then_inc(hid_ready, 1)
                else:
                    chain.mark(V.tensor_tensor(ht[:], ht[:], hx[:], ALU.mult))
                    chain.wait()
                    for h in range(2):
                        ins = V.tensor_copy(hv[:, h, :].rearrange("p (i n) -> p i n", i=NPAIR),
                                            bcast(ht[:, h, :], 1, [P, NPAIR, NG * NBLK]))
                    ins.then_inc(hid_ready, 1)

            def maxima(L, n, chain):
                br, t, g, heads, kb = ATT[n]
                dve.wait_ge(s_done, N_ATT * L + n + 1)
                nh = len(heads)
                chain.mark(V.tensor_reduce(smax[:, n, 0:nh], bank[n % 2][:].rearrange("p (h k) -> p h k", h=nh), AX.X, ALU.max))
                chain.wait()
                V.tensor_scalar(nmax[:, n % 2, 0:nh], smax[:, n, 0:nh], -SCALE, None, ALU.mult).then_inc(max_done, 1)

            def copy_pT(L, n):
                dve.wait_ge(pT_done, N_ATT * L + n + 1)
                if n >= 2:
                    dve.wait_ge(pv_done, 14 * L + n - 1)
                width = 512 if n < 12 else 2 * P
                rows = P if n < 12 else NH * NBLK
                V.tensor_copy(probsT[n % 2][0:rows, 0:width], bank[6 + n % 2][0:rows, 0:width]).then_inc(pT_copied, 1)

            def combine(L, og, chain):
                br, t = (0, 1, 2)[og // 2], og % 2
                if og == 0:
                    chain.mark(V.tensor_scalar(egate[:], egate[:], 1.0, None, ALU.add))
                if br < 2:
                    dve.wait_ge(exp_done, N_ATT * L + O_READY[og])
                chain.wait()
                chain.mark(V.tensor_tensor(coef[:, br, t, :], rsum[:, br, t, :],
                                           egate[:, t, :].rearrange("p (h b) -> p b h", b=3)[:, (br + 1) % 3, :], ALU.mult))
                chain.wait()
                chain.mark(V.reciprocal(coef[:, br, t, :], coef[:, br, t, :]))
                chain.wait()
                dve.wait_ge(pv_done, 14 * L + O_READY[og])
                o = bank[2][:].rearrange("p (h d) -> p h d", h=NH)
                c = bcast(coef[:, br, t, :], 2, [P, NH, HEAD])
                if og < 2:
                    ins = V.tensor_tensor(acc[:, t, :].rearrange("p (h d) -> p h d", h=NH), o, c, ALU.mult)
                    ins.then_inc(o_read, 1)
                else:
                    V.tensor_tensor(part[:, 0, :].rearrange("p (h d) -> p h d", h=NH), o, c, ALU.mult).then_inc(o_read, 1)
                    dve.wait_ge(o_read, 6 * L + og + 1)
                    chain.mark(V.tensor_tensor(acc[:, t, :], acc[:, t, :], part[:, 0, :], ALU.add))

            def copy_squares(L, pair):
                dve.wait_ge(ms_used, 2 * L + pair + 1)
                V.tensor_copy(cstat[:, pair].rearrange("p t h -> p (t h)"), bank[3][:, 8 * pair:8 * pair + 8]).then_inc(ms_read, 1)

            def roots_low(L, pair):
                dve.wait_ge(roots_hi, 2 * L + pair + 1)
                lo, hi = (a[:, pair].rearrange("p t (h d) -> p (t h) d", d=HEAD) for a in (roots_l, roots_h))
                V.tensor_tensor(lo, bcast(croot[:, pair].rearrange("p t h -> p (t h)"), 2, [P, 4 * TT, HEAD]), hi.bitcast(fp32),
                                ALU.subtract).then_inc(roots_lo, 1)

            def mix_low(L, j, src):
                V.scalar_tensor_tensor(xl[:, j, :], src, par[:, j:j + 1], xh[:, j, :].bitcast(fp32), ALU.mult,
                                       ALU.subtract).then_inc(mix_lo, 1)

            def layer_norm(L, which, t, banks, ready, chain):
                done = y1_done if which == 0 else y2_done
                xt = x_tok[:, t, :]
                for n in range(2):
                    if t + n < 2:
                        dve.wait_ge(done, 2 * L + t + 1)
                    else:
                        unit_used(dve, L, U_OUT + 3 if which == 0 else NU - 1)
                    cols = slice(512 * n, 512 * (n + 1))
                    chain.mark(V.scalar_tensor_tensor(xt[:, cols], xt[:, cols], ALPHA, bank[banks + 2 * t + n][:], ALU.mult, ALU.add))
                    chain.wait()
                    if n == 0:
                        chain.mark(V.bn_stats(stats[:, t, 0, :], xt[:, 0:512]))
                chain.wait()
                chain.mark(V.bn_stats(stats[:, t, 1, :], xt[:, 512:1024]))
                chain.wait()
                settled(dve)
                V.bn_aggr(mv[:, t, :], stats[:, t].rearrange("p n s -> p (n s)")).then_inc(ln_stats, 1)
                if t == 0:
                    dve.wait_ge(ln_in, 16 * (4 * L + 2 * which + 2))
                dve.wait_ge(ln_stats, 4 * L + 2 * which + t + 1)
                chain.mark(V.scalar_tensor_tensor(xt, xt, mv[:, t, 0:1], ln_par[:, 0, :], ALU.subtract, ALU.mult))
                chain.wait()
                dve.wait_ge(ln_root, 4 * L + 2 * which + t + 1)
                for n in range(2):
                    cols = slice(512 * n, 512 * (n + 1))
                    V.scalar_tensor_tensor(xt[:, cols], xt[:, cols], rstd[:, t:t + 1], ln_par[:, 1, cols], ALU.mult,
                                           ALU.add).then_inc(ready, 1)

            def ffn_step(L, s, odd, value, gate, units):
                G = L * STEPS + s
                for back in (1, 2):
                    for v in range(2):
                        b = bank[4 + 2 * odd + v]
                        if back == 1:
                            dve.wait_ge(fy_init, 2 * G + v + 1)
                        else:
                            dve.wait_ge(fy_mid, 2 * G + v + 1)
                        for c in range(2):
                            ins = V.scalar_tensor_tensor(ffn_y[:, odd, v, c, back:], b[:, SEQ * c:SEQ * (c + 1) - back],
                                                         step_par[:, odd, v, c, 2 - back:3 - back],
                                                         ffn_y[:, odd, v, c, back:], ALU.mult, ALU.add)
                        ins.then_inc(fy_mid if back == 1 else fy_done, 1)
                dve.wait_ge(silu_done, G + 1)
                y = ffn_y[:, odd].rearrange("p v c n -> p v (c n)")
                V.tensor_tensor(y[:, 0], y[:, 0], y[:, 1], ALU.mult).then_inc(h_done, 1)
                dve.wait_ge(h_hi, G + 1)
                V.tensor_tensor(hTl[:, odd].rearrange("p c n -> p (c n)"), y[:, 0],
                                hTh[:, odd].rearrange("p c n -> p (c n)").bitcast(fp32), ALU.subtract).then_inc(h_lo, 1)
                for u in units:
                    split_lo(V, L, *u)

            with dve.Fori(0, DEPTH) as L:
                chain = Chain(dve, dve_seq, L, DVE_STEPS)
                x_low(L, 4, 0, xT_hi, xT_lo)
                split_lo(V, L, 1)
                x_low(L, 4, 1, xT_hi, xT_lo)
                split_lo(V, L, 3)
                dve.wait_ge(gate_hi, L + 1)
                V.tensor_tensor(gate_wl[:], gate_w[:], gate_wh[:].bitcast(fp32), ALU.subtract).then_inc(gate_lo, 1)
                split_lo(V, L, 6)
                dve.wait_ge(par_ready, L + 1)
                for t in range(TT):
                    rope(L, t, chain)
                for b, (dst, hi, src) in enumerate(((qTl[:, 0:2, :], qTh[:, 0:2, :], bank[6]), (qTl[:, 2:4, :], qTh[:, 2:4, :], bank[7]),
                                                    (kTl[:], kTh[:], bank[0]))):
                    dve.wait_ge(qkT_hi, 3 * L + b + 1)
                    V.tensor_tensor(dst.rearrange("p i n -> p (i n)"), src[:], hi.rearrange("p i n -> p (i n)").bitcast(fp32),
                                    ALU.subtract).then_inc(qkT_copied, 1)
                dve.wait_ge(qkT_done, 4 * L + 4)
                for kv in range(2):
                    tok = bank[1][:, 256 * kv:256 * (kv + 1)].rearrange("p (g c r) -> p r g c", g=NG, r=8)
                    for half in range(2):
                        pos = par[:, 24 + 16 * kv + 8 * half:32 + 16 * kv + 8 * half]
                        ins = V.tensor_tensor(blocks[kv][:, 8 * half:8 * half + 8, :].rearrange("p r (g c) -> p r g c", g=NG),
                                              tok[:, :, :, half:half + NBLK],
                                              pos.unsqueeze(2).unsqueeze(3).to_broadcast([P, 8, NG, NBLK]), ALU.add)
                    ins.then_inc(blocks_in, 1)
                for kv in range(2):
                    dve.wait_ge(blocks_hi, 2 * L + kv + 1)
                    V.tensor_tensor(blocks_l[kv], blocks[kv], blocks_h[kv].bitcast(fp32), ALU.subtract).then_inc(blocks_lo, 1)
                conv_gate(L, 0)
                split_lo(V, L, 9)
                maxima(L, 0, chain)
                maxima(L, 1, chain)
                hidden(L, 0, chain)
                conv_taps(L, 0, chain)
                dve.wait_ge(kc_hi, L + 1)
                for g in range(NG):
                    rows = slice(HEAD * g, HEAD * (g + 1))
                    ins = V.tensor_tensor(kcTl[rows, g, :], bank[2][rows, 384:384 + NBLK], kcTh[rows, g, :].bitcast(fp32), ALU.subtract)
                ins.then_inc(cmp_copied, 1)
                split_lo(V, L, 12)
                copy_pT(L, 0)
                hidden(L, 1, chain)
                maxima(L, 2, chain)
                copy_pT(L, 1)
                dve.wait_ge(cmp_done, 2 * L + 2)
                V.tensor_tensor(vbd, bcast(bank[3][0:NH * NBLK, 384:384 + HEAD], 1, [NH * NBLK, NH, HEAD]),
                                bcast(cst[0:NH * NBLK, C_BM:C_BM + NH], 2, [NH * NBLK, NH, HEAD]), ALU.mult).then_inc(cmp_copied, 1)
                between = {2: [lambda: combine(L, 0, chain)], 3: [lambda: copy_squares(L, 0)], 4: [lambda: conv_gate(L, 1)],
                           6: [lambda: combine(L, 1, chain)], 8: [lambda: combine(L, 2, chain), lambda: conv_taps(L, 1, chain)]}
                for n in range(2, 11):
                    maxima(L, n + 1, chain)
                    copy_pT(L, n)
                    for step in between.get(n, []):
                        step()
                dve.wait_ge(s_done, N_ATT * L + 13)
                dve.wait_ge(pT_done, N_ATT * L + 11)
                flat = probs[0][:, 0:TT * NH * NBLK].rearrange("p (h c) -> p h c", c=NBLK)
                sc = probs[0][:, 0:TT * NH * NBLK].rearrange("p (t h c) -> p t h c", t=TT, h=NH)
                scores = bank[0][:, 0:TT * NH * NBLK].rearrange("p (t h c) -> p t h c", t=TT, h=NH)
                for t in range(TT):
                    ins = V.tensor_tensor(sc[:, t], scores[:, t], bcast(cst[:, C_MA + NBLK * t:C_MA + NBLK * (t + 1)], 1,
                                                                        [P, NH, NBLK]), ALU.add)
                chain.mark(ins)
                chain.wait()
                chain.mark(V.tensor_reduce(cmax[:], flat, AX.X, ALU.max))
                chain.wait()
                V.tensor_tensor(flat, flat, bcast(cmax[:], 2, [P, TT * NH, NBLK]), ALU.subtract).then_inc(max_done, 1)
                copy_pT(L, 11)
                dve.wait_ge(exp_done, N_ATT * L + 13)
                for t in range(TT):
                    ins = V.tensor_reduce(rsum[:, 2, t].rearrange("p (g i) -> p i g", g=NG),
                                          sc[:, t].rearrange("p (i g) c -> p i g c", g=NG), AX.X, ALU.add)
                chain.mark(ins)
                chain.wait()
                for t in range(TT):
                    ins = V.tensor_tensor(sc[:, t], sc[:, t], bcast(cst[:, C_M01 + NBLK * t:C_M01 + NBLK * (t + 1)], 1,
                                                                    [P, NH, NBLK]), ALU.mult)
                ins.then_inc(cmp_p, 1)
                combine(L, 3, chain)
                copy_pT(L, 12)
                copy_squares(L, 1)
                roots_low(L, 0)
                for t in range(TT):
                    combine(L, 4 + t, chain)
                    chain.wait()
                    chain.mark(V.tensor_tensor(part[:, 1, :], acc[:, t, :], acc[:, t, :], ALU.mult))
                    chain.wait()
                    V.tensor_reduce(mstat[:, t, :], part[:, 1, :].rearrange("p (h d) -> p h d", h=NH), AX.X, ALU.add).then_inc(att_ss, 1)
                roots_low(L, 1)
                for b in range(2):
                    dve.wait_ge(bc_done, 2 * L + b + 1)
                    half = conv_o[:, 2 * b:2 * b + 2, :].rearrange("p c n -> p (c n)")
                    V.tensor_tensor(half, half, bank[4 + b][:], ALU.mult).then_inc(conv_norm, 1)
                for j in range(4):
                    dve.wait_ge(mix_hi, 8 * L + j + 1)
                    mix_low(L, j, conv_o[:, j, :])
                for t in range(TT):
                    dve.wait_ge(att_root, 2 * L + t + 1)
                    a = acc[:, t, :].rearrange("p (h d) -> p h d", h=NH)
                    V.tensor_tensor(a, a, bcast(mroot[:, t, :], 2, [P, NH, HEAD]), ALU.mult).then_inc(att_ready, 1)
                for j in range(4):
                    dve.wait_ge(mix_hi, 8 * L + 4 + 2 * (j // 2) + 2)
                    mix_low(L, 4 + j, bank[6 + j // 2][:, SEQ * (j % 2):SEQ * (j % 2 + 1)])
                for t in range(TT):
                    layer_norm(L, 0, t, 4, x1_ready, chain)
                    x_low(L, 0, t, x1T_hi, x1T_lo)
                ffn_step(L, 0, 0, (19, 0), (20, 0), [(25, 0)])
                ffn_step(L, 1, 1, (21, 0), (22, 0), [(28, 0)])
                ffn_step(L, 2, 0, (23, 0), (24, 0), [(31, 0)])
                with dve.Fori(0, (STEPS - 5) // 2) as i:
                    ffn_step(L, 2 * i + 3, 1, (26, i), (27, i), [(34, i)])
                    ffn_step(L, 2 * i + 4, 0, (29, i), (30, i), [(37, i)])
                last = (STEPS - 5) // 2
                ffn_step(L, STEPS - 2, 1, (26, last), (27, last), [(NU - 2, 0), (NU - 1, 0)])
                ffn_step(L, STEPS - 1, 0, (29, last), (30, last), [])
                for t in range(TT):
                    layer_norm(L, 1, t, 0, x_ready, chain)
                chain.close()

        @block.tensor
        def _(pe):
            def mm3(dst, ah, al, bh, bl, start, stop, **kw):
                pe.matmul(dst, ah, bh, start=start, stop=False, **kw)
                pe.matmul(dst, ah, bl, start=False, stop=False, **kw)
                return pe.matmul(dst, al, bh, start=False, stop=stop, **kw)

            def wait_unit(L, u, i=0):
                pe.wait_ge(split_done[u % RAWS], CREDIT + raw_round(L, u, i) + 1)

            def free_unit(ins, u):
                ins.then_inc(slot_free[u % SLOTS], 1)

            def w_view(u, k):
                return (ring_hi[u % SLOTS][:].rearrange("p (k n) -> p k n", k=k),
                        ring_lo[u % SLOTS][:].rearrange("p (k n) -> p k n", k=k))

            def transpose_x(L, ready, banks, t, done):
                for b in range(2):
                    pe.wait_ge(ready, 4 * L + 2 * t + b + 1)
                    for k in range(4):
                        ins = pe.transpose(bank[banks + 2 * t + b][:, P * k:P * (k + 1)],
                                           x_tok[:, t, P * (4 * b + k):P * (4 * b + k + 1)], ident)
                    ins.then_inc(done, 1)

            def conv_unit(L, idx, part, half=None):
                u = CONV_U[idx]
                if part == 0 and half in (None, 0):
                    wait_unit(L, u)
                    if idx < 2:
                        pe.wait_ge(qkv_copied, 6 * L + 5 + idx)
                    elif idx == 2:
                        pe.wait_ge(c_copied, 2 * L + 1)
                    elif idx == 3:
                        pe.wait_ge(z_done, 2 * L + 1)
                    elif idx == 4:
                        pe.wait_ge(conv_out, 2 * L + 1)
                    else:
                        pe.wait_ge(c_copied, 2 * L + 2)
                wh, wl = w_view(u, KT)
                cols = slice(P * part, P * (part + 1))
                for k in range(KT) if half is None else range(4 * half, 4 * half + 4):
                    ins = mm3(bank[4 + idx % 2][:, SEQ * part:SEQ * (part + 1)], wh[:, k, cols], wl[:, k, cols],
                              xh[:, k, :], xl[:, k, :], k == 0, k == KT - 1)
                if part and half in (None, 1):
                    free_unit(ins, u)

            def scores(L, n):
                br, t, g, heads, kb = ATT[n]
                dst = bank[n % 2]
                if n == 0:
                    pe.wait_ge(qkT_copied, 3 * L + 3)
                elif n == 1:
                    pe.wait_ge(blocks_in, 2 * L + 2)
                else:
                    pe.wait_ge(exp_done, N_ATT * L + n - 1)
                rows = slice(HEAD * g, HEAD * (g + 1))
                keys = P * kb
                for j, h in enumerate(heads):
                    tok = slice(P * t, P * (t + 1))
                    mm3(dst[:, keys * j:keys * (j + 1)], qTh[rows, h, tok], qTl[rows, h, tok], kTh[rows, br, 0:keys],
                        kTl[rows, br, 0:keys], j == 0, False, skip_group_check=True)
                diag = dst[:].rearrange("p (h k) -> p h k", k=keys)[:, :, keys - P:keys]
                pe.matmul(diag, ident_b[:], bcast(cmask_b[:], 1, [P, len(heads), P]), start=False, stop=True,
                          skip_group_check=True).then_inc(s_done, 1)

            def transpose_p(L, n):
                pe.wait_ge(exp_done, N_ATT * L + n + 1)
                if n >= 2:
                    pe.wait_ge(pT_copied, N_ATT * L + n - 1)
                for m in range(4):
                    ins = pe.transpose(bank[6 + n % 2][:, P * m:P * (m + 1)], probs[n % 2][:, P * m:P * (m + 1)], ident)
                ins.then_inc(pT_done, 1)

            def times_v(L, n):
                br, t, g, heads, kb = ATT[n]
                pe.wait_ge(pT_copied, N_ATT * L + n + 1)
                if n in O_READY:
                    pe.wait_ge(o_read, 6 * L + O_READY.index(n) + 1)
                elif n == 0:
                    pe.wait_ge(cmp_copied, 2 * L + 1)
                v0 = (16 if br == 0 else 18) * HEAD + HEAD * g
                for j, h in enumerate(heads):
                    for b in range(kb):
                        ins = pe.matmul(bank[2][:, HEAD * (NPAIR * g + h):HEAD * (NPAIR * g + h + 1)],
                                        probsT[n % 2][:, P * (kb * j + b):P * (kb * j + b + 1)], qkv[:, b, v0:v0 + HEAD],
                                        start=(b == 0), stop=(b == kb - 1))
                ins.then_inc(pv_done, 1)

            def cmp_hidden(L, kv):
                pe.wait_ge(blocks_lo, 2 * L + kv + 1)
                for half, u in enumerate(W1_U[kv]):
                    wait_unit(L, u)
                    wh, wl = w_view(u, 8)
                    for j in range(8):
                        k = 8 * half + j
                        ins = mm3(bank[2 + kv][0:NG * NBLK, 0:CMP_HID], blocks_h[kv][:, k, :], blocks_l[kv][:, k, :],
                                  wh[:, j, :], wl[:, j, :], k == 0, k == NJ - 1)
                    free_unit(ins, u)

            def transpose_hidden(L, kv):
                pe.wait_ge(hid_copied, 2 * L + kv + 1)
                settled(pe)
                for h in range(2):
                    ins = pe.transpose(bank[2 + kv][:, 256 + 32 * h:286 + 32 * h], hid[:, P * h:P * (h + 1)],
                                       ident[0:NG * NBLK, 0:NG * NBLK])
                ins.then_inc(hidT_done, 1)

            def cmp_k(L):
                pe.wait_ge(hid_ready, 2 * L + 1)
                for g in range(NG):
                    dst = bank[2][HEAD * g:HEAD * (g + 1), 384:384 + NBLK]
                    for h in range(2):
                        pe.matmul(dst, w2[:, 0, h, :], hk[:, h, NBLK * g:NBLK * (g + 1)], start=(h == 0), stop=False)
                    ins = pe.matmul(dst, b2[0:1, 0, :], ones[0:1, 0:NBLK], start=False, stop=True)
                ins.then_inc(cmp_done, 1)

            def cmp_v(L):
                pe.wait_ge(hid_ready, 2 * L + 2)
                dst = bank[3][0:NH * NBLK, 384:384 + HEAD]
                for h in range(2):
                    pe.matmul(dst, hv[:, h, :], w2[:, 1, h, :], start=(h == 0), stop=False)
                pe.matmul(dst, ones[0:1, 0:NH * NBLK], b2[0:1, 1, :], start=False, stop=True).then_inc(cmp_done, 1)

            def cmp_scores(L):
                pe.wait_ge(exp_done, N_ATT * L + 11)
                pe.wait_ge(cmp_copied, 2 * L + 1)
                for t in range(TT):
                    for h in range(NPAIR):
                        c0 = NG * NBLK * (NPAIR * t + h)
                        tok = slice(P * t, P * (t + 1))
                        ins = mm3(bank[0][:, c0:c0 + NG * NBLK], qTh[:, h, tok], qTl[:, h, tok],
                                  *(a[:].rearrange("p g c -> p (g c)") for a in (kcTh, kcTl)), True, True)
                ins.then_inc(s_done, 1)

            def transpose_cmp(L):
                pe.wait_ge(cmp_p, L + 1)
                pe.wait_ge(pT_copied, N_ATT * L + 11)
                for t in range(TT):
                    ins = pe.transpose(bank[6][0:NH * NBLK, P * t:P * (t + 1)],
                                       probs[0][:, NH * NBLK * t:NH * NBLK * (t + 1)], ident)
                ins.then_inc(pT_done, 1)

            def times_v_cmp(L, t):
                pe.wait_ge(pT_copied, N_ATT * L + 13)
                pe.wait_ge(cmp_copied, 2 * L + 2)
                pe.wait_ge(o_read, 6 * L + 4 + t)
                pe.matmul(bank[2][:], probsT[0][0:NH * NBLK, P * t:P * (t + 1)], vbd.rearrange("p h d -> p (h d)"),
                          start=True, stop=True).then_inc(pv_done, 1)

            def mean_squares(L, pair):
                pe.wait_ge(sq_done, 2 * L + pair + 1)
                if pair == 0:
                    pe.wait_ge(cmp_copied, 2 * L + 2)
                for t in range(TT):
                    for m in range(2):
                        c0 = 8 * pair + 4 * t + 2 * m
                        ins = pe.matmul(bank[3][:, c0:c0 + 2], conv_sq[:, m, P * t:P * (t + 1)], cst[:, C_BLK:C_BLK + 2],
                                        start=True, stop=True)
                ins.then_inc(ms_used, 1)

            def conv_roots(L, pair):
                pe.wait_ge(roots_lo, 2 * L + pair + 1)
                pe.wait_ge(conv_out, 2 * L + 2)
                for m in range(2):
                    for t in range(TT):
                        for a in (roots_h, roots_l):
                            ins = pe.matmul(bank[4 + pair][:, SEQ * m + P * t:SEQ * m + P * (t + 1)], a[:, pair, t, P * m:P * (m + 1)],
                                            ident_r[:], start=(a is roots_h), stop=(a is roots_l))
                        if pair and m == 0 and t == 0:
                            ins.then_inc(stage_free, 1)
                ins.then_inc(bc_done, 1)

            def out_product(t, c, k):
                wh, wl = w_view(U_OUT + k // 2, 2)
                cols = slice(512 * c, 512 * (c + 1))
                return mm3(bank[4 + 2 * t + c][:], xh[:, k, P * t:P * (t + 1)], xl[:, k, P * t:P * (t + 1)],
                           wh[:, k % 2, cols], wl[:, k % 2, cols], k == 0, k == KT - 1)

            def up(L, s, odd, value, gate, first=False):
                G = L * STEPS + s
                for v, u in enumerate((value, gate)):
                    wait_unit(L, *u)
                    pe.wait_ge(fy_done, FY_CREDIT + 2 * (G - 2) + v + 1)
                    wh, wl = w_view(u[0], KT)
                    for part in range(2):
                        if first and v == 0:
                            pe.wait_ge(x1T_lo, 4 * L + 3 + part)
                        for c in range(2):
                            for k in range(4 * part, 4 * part + 4):
                                ins = mm3(bank[4 + 2 * odd + v][:, SEQ * c:SEQ * (c + 1)], wh[:, k, P * c:P * (c + 1)],
                                          wl[:, k, P * c:P * (c + 1)], xh[:, k, :], xl[:, k, :], k == 0 and c == 0, k == KT - 1,
                                          skip_group_check=True)
                    free_unit(ins, u[0])

            def down_product(s, odd, u, t, n, c):
                wh, wl = w_view(u, 2)
                tok, cols = slice(P * t, P * (t + 1)), slice(512 * n, 512 * (n + 1))
                return mm3(bank[2 * t + n][:], hTh[:, odd, c, tok], hTl[:, odd, c, tok], wh[:, c, cols], wl[:, c, cols],
                           s == 0 and c == 0, s == STEPS - 1 and c == 1)

            def down(L, s, odd, u):
                wait_unit(L, *u)
                pe.wait_ge(h_lo, H_CREDIT + L * STEPS + s + 1)
                for t in range(TT):
                    for c in range(2):
                        for n in range(2):
                            ins = down_product(s if isinstance(s, int) else None, odd, u[0], t, n, c)
                free_unit(ins, u[0])

            def down_last(L):
                for t in range(TT):
                    for halves in ((0, 1),) if t == 0 else ((0,), (1,)):
                        for s in (STEPS - 2, STEPS - 1):
                            u = NU - STEPS + s
                            if t == 0:
                                wait_unit(L, u)
                                pe.wait_ge(h_lo, H_CREDIT + L * STEPS + s + 1)
                            for c in range(2):
                                for n in halves:
                                    ins = down_product(s, s % 2, u, t, n, c)
                            if halves == (1,):
                                free_unit(ins, u)
                        if 0 in halves:
                            ins.then_inc(y2_done, 1)

            pe.wait_ge(ident_in, 16)
            pe.wait_ge(const_ready, 4)
            with pe.Fori(0, DEPTH) as L:
                transpose_x(L, x_ready, 4, 0, xT_done)
                for t in range(TT):
                    tok = slice(P * t, P * (t + 1))
                    for first in (0, 2):
                        for b in range(2):
                            u = first + b
                            if t == 0:
                                wait_unit(L, u)
                            if first == 0:
                                pe.wait_ge(xT_lo, 4 * L + 2 * t + b + 1)
                            wh, wl = w_view(u, 4)
                            for kk in range(4):
                                k = 4 * b + kk
                                ins = mm3(bank[first + t][:], xh[:, k, tok], xl[:, k, tok], wh[:, kk, :], wl[:, kk, :],
                                          k == 0, k == KT - 1)
                            if t:
                                free_unit(ins, u)
                            elif b:
                                ins.then_inc(proj_done, 1)
                            if t == 0 and u == 0:
                                transpose_x(L, x_ready, 4, 1, xT_done)
                pe.wait_ge(par_in, 16 * 8 * (L + 1))
                settled(pe)
                nf = 4 * STEPS
                for k in range(4):
                    pe.transpose(bank[6][:, nf * k:nf * (k + 1)], ffn_stage[:, k, :], ident[0:nf, 0:nf])
                pe.transpose(bank[6][:, 4 * nf:4 * nf + 56], par_stage[:], ident[0:56, 0:56]).then_inc(par_T, 1)
                wait_unit(L, 4)
                wh, wl = w_view(4, KT)
                for t in range(TT):
                    tok = slice(P * t, P * (t + 1))
                    for k in range(KT):
                        ins = mm3(bank[4 + t][:, 0:256], xh[:, k, tok], xl[:, k, tok], wh[:, k, :], wl[:, k, :], k == 0, k == KT - 1)
                    if t:
                        free_unit(ins, 4)
                    else:
                        pe.wait_ge(gate_lo, L + 1)
                    for k in range(KT):
                        ins = mm3(bank[4 + t][:, 256:256 + NGATE], xh[:, k, tok], xl[:, k, tok], gate_wh[:, k, :],
                                  gate_wl[:, k, :], k == 0, k == KT - 1)
                    ins.then_inc(proj_done, 1)
                for part in range(2):
                    conv_unit(L, 0, part)
                pe.wait_ge(par_ready, L + 1)
                for b in range(2):
                    for t in range(TT):
                        pe.wait_ge(rope_done, 2 * L + t + 1)
                        for m in range(2):
                            h = 2 * b + m
                            ins = pe.transpose(bank[6 + b][:, SEQ * m + P * t:SEQ * m + P * (t + 1)], qkv[:, t, P * h:P * (h + 1)], ident)
                    ins.then_inc(qkT_done, 1)
                for m in range(2):
                    for t in range(TT):
                        col = (10 + 2 * m) * HEAD
                        ins = pe.transpose(bank[0][:, SEQ * m + P * t:SEQ * m + P * (t + 1)], qkv[:, t, col:col + P], ident)
                ins.then_inc(qkT_done, 1)
                for kv in range(2):
                    for g in range(NG):
                        col = (8 + 6 * kv + g) * HEAD
                        for t in range(TT):
                            for odd in range(2):
                                dst = 256 * kv + P * g + 64 * t
                                ins = pe.matmul(bank[1][HEAD * odd:HEAD * (odd + 1), dst:dst + 64], qkv[:, t, col:col + HEAD],
                                                ident[:, odd:P:2], start=True, stop=True)
                ins.then_inc(qkT_done, 1)
                for part in range(2):
                    conv_unit(L, 1, part)
                pe.wait_ge(masks_ready, 3)
                scores(L, 0)
                cmp_hidden(L, 0)
                scores(L, 1)
                transpose_hidden(L, 0)
                for part in range(2):
                    conv_unit(L, 2, part)
                cmp_k(L)
                cmp_hidden(L, 1)
                transpose_p(L, 0)
                transpose_hidden(L, 1)
                pieces = [(idx, part, half) for idx in (3, 4, 5) for part in range(2) for half in range(2)]
                per_unit = [2, 2, 2, 2, 1, 1, 1, 1, 0, 0, 0, 0]
                for n in range(12):
                    if n < 10:
                        scores(L, n + 2)
                    elif n == 10:
                        cmp_scores(L)
                    if n < 11:
                        transpose_p(L, n + 1)
                    for _ in range(per_unit[n]):
                        conv_unit(L, *pieces.pop(0))
                    if n == 0:
                        cmp_v(L)
                    if n == 2:
                        mean_squares(L, 0)
                    if n == 11:
                        transpose_cmp(L)
                    times_v(L, n)
                mean_squares(L, 1)
                for t in range(TT):
                    times_v_cmp(L, t)
                for pair in range(2):
                    conv_roots(L, pair)
                pe.wait_ge(pT_copied, N_ATT * L + 13)
                for t in range(TT):
                    pe.wait_ge(att_ready, 2 * L + t + 1)
                    for j in range(4):
                        ins = pe.transpose(bank[6 + j // 2][:, SEQ * (j % 2) + P * t:SEQ * (j % 2) + P * (t + 1)],
                                           acc[:, t, P * j:P * (j + 1)], ident)
                        if t and j % 2:
                            ins.then_inc(mixT_done, 1)
                for n in range(4):
                    wait_unit(L, U_OUT + n)
                    for k in (2 * n, 2 * n + 1):
                        pe.wait_ge(mix_lo, 8 * L + k + 1)
                        for c in range(2):
                            ins = out_product(0, c, k)
                ins.then_inc(y1_done, 1)
                for c in range(2):
                    for k in range(KT):
                        ins = out_product(1, c, k)
                        if c and k % 2:
                            free_unit(ins, U_OUT + k // 2)
                    if c == 0:
                        ins.then_inc(y1_done, 1)
                        transpose_x(L, x1_ready, 0, 0, x1T_done)
                transpose_x(L, x1_ready, 0, 1, x1T_done)
                up(L, 0, 0, (19, 0), (20, 0), first=True)
                up(L, 1, 1, (21, 0), (22, 0))
                up(L, 2, 0, (23, 0), (24, 0))
                down(L, 0, 0, (25, 0))
                up(L, 3, 1, (26, 0), (27, 0))
                down(L, 1, 1, (28, 0))
                up(L, 4, 0, (29, 0), (30, 0))
                with pe.Fori(1, (STEPS - 3) // 2) as i:
                    down(L, 2 * i, 0, (25, i))
                    up(L, 2 * i + 3, 1, (26, i), (27, i))
                    down(L, 2 * i + 1, 1, (28, i))
                    up(L, 2 * i + 4, 0, (29, i), (30, i))
                down(L, STEPS - 3, 0, (NU - 3, 0))
                down_last(L)


_INS = ['x', 'w_in', 'short_conv_w', 'cmp_pe', 'cmp_w1', 'cmp_b1', 'cmp_w2', 'cmp_b2', 'head_norm_g', 'w_out', 'ln1_g',
        'ln1_b', 'w_up', 'ffn_conv_w', 'ffn_conv_b', 'w_down', 'ln2_g', 'ln2_b']


def kernel(**inputs):
    import concourse.bacc as bacc
    from concourse.bass_utils import run_bass_kernel_spmd

    nc = bacc.Bacc("TRN2", target_bir_lowering=False, num_devices=1, dynamic_dma_scratch_size=256)
    arrays, args = {}, []
    for name in _INS:
        a = np.ascontiguousarray(inputs[name])
        arrays[f"in_{name}"] = a
        args.append(nc.dram_tensor(f"in_{name}", a.shape, mybir.dt.from_np(a.dtype), kind="ExternalInput").ap())
    arrays["in_consts"] = shape_constants()
    args.append(nc.dram_tensor("in_consts", (P, C_ALL), mybir.dt.float32, kind="ExternalInput").ap())
    args.append(nc.dram_tensor("out_0", (1, SEQ, D_MODEL), mybir.dt.float32, kind="ExternalOutput").ap())
    build(nc, *args)
    return run_bass_kernel_spmd(nc, [arrays], core_ids=[0]).results[0]["out_0"]
```

```python
from contextlib import ExitStack

import concourse.bass as bass
import numpy as np
from concourse import mybir

P = 128
D_MODEL, SEQ, DEPTH, HEAD = 1024, 256, 2, 64
KT = D_MODEL // P
TT = SEQ // P
CONV_W, ATTN_W, KV_W = 512, 512, 128
NH, NG = ATTN_W // HEAD, 2
NPAIR = NH // NG
ROPE = HEAD // 4
NBLK = SEQ // 16 - 1
NJ = 16
CMP_HID = 256
D_FF = 2816
STEPS = D_FF // (2 * P)
ALPHA = (2.0 * DEPTH) ** 0.25
SCALE = HEAD ** -0.5
MASKED = -1e30
Q0, KV0, KW0, G0COL = 3 * CONV_W, 3 * CONV_W + ATTN_W, 3 * CONV_W + ATTN_W + 4 * KV_W, 3 * CONV_W + ATTN_W + 6 * KV_W
NGATE = NH * 3

UNIT = 2048
RAWS, SLOTS = 3, 6
CONV_U = (5, 6, 9, 12, 13, 14)
W1_U = ((7, 8), (10, 11))
U_OUT, U_FFN = 15, 19
NU = U_FFN + 3 * STEPS
RAW_USES = [len(range(i, NU, RAWS)) for i in range(RAWS)]
SLOT_USES = [len(range(i, NU, SLOTS)) for i in range(SLOTS)]
N_ATT = 13

C_ID, C_CM, C_CC, C_SS = 0, 128, 256, 288
C_MA, C_M01, C_BM, C_BLK = 320, 350, 380, 388
C_ALL = C_BLK + 2


def shape_constants():
    c = np.zeros((P, C_ALL), np.float32)
    p = np.arange(P)
    c[:, C_ID:C_ID + P] = np.eye(P)
    c[:, C_CM:C_CM + P] = np.where(p[None, :] > p[:, None], MASKED, 0.0)
    half = ROPE // 2
    inv_freq = (500000.0 ** (-(np.arange(half, dtype=np.float32) * 2.0 / ROPE))).astype(np.float32)
    for t in range(TT):
        ang = (p + P * t).astype(np.float32)[:, None] * inv_freq[None]
        cos, sin = np.cos(ang), np.sin(ang)
        c[:, C_CC + 16 * t:C_CC + 16 * t + 16] = np.concatenate([cos, cos], 1)
        c[:, C_SS + 16 * t:C_SS + 16 * t + 16] = np.concatenate([-sin, sin], 1)
        seen = (np.arange(NBLK)[None] * 16 + 31) <= (p + P * t)[:, None]
        c[:, C_MA + NBLK * t:C_MA + NBLK * (t + 1)] = np.where(seen, 0.0, MASKED)
        c[:, C_M01 + NBLK * t:C_M01 + NBLK * (t + 1)] = seen
    pos = p[:, None] // NBLK
    c[:, C_BM:C_BM + NH] = NPAIR * (pos % NG) + pos // NG == np.arange(NH)[None]
    c[:, C_BLK:C_BLK + 2] = (p[:, None] // HEAD == np.arange(2)[None]) / HEAD
    return c


class Chain:

    def __init__(self, eng, sem, layer, per_layer):
        self.eng, self.sem, self.base, self.per_layer, self.k = eng, sem, layer * per_layer, per_layer, 0

    def mark(self, ins):
        ins.then_inc(self.sem, 1)
        self.k += 1

    def wait(self):
        self.eng.wait_ge(self.sem, self.base + self.k)

    def close(self):
        assert self.k == self.per_layer, (self.k, self.per_layer)


def att_units():
    out = []
    for br in range(2):
        for t in range(TT):
            for g in range(NG):
                n = NPAIR // (t + 1)
                for part in range(t + 1):
                    out.append((br, t, g, range(part * n, part * n + n), t + 1))
    return out


ATT = att_units()
O_READY = [2, 6, 8, 12, 13, 14]

DVE_STEPS, POOL_STEPS = 71, 8
CREDIT = 1
FY_CREDIT = 4
H_CREDIT = 2
LN_CREDIT = 1


def build(nc, x, w_in, short_conv_w, cmp_pe, cmp_w1, cmp_b1, cmp_w2, cmp_b2, head_norm_g, w_out, ln1_g, ln1_b,
          w_up, ffn_conv_w, ffn_conv_b, w_down, ln2_g, ln2_b, consts, out):
    fp32, f32r, bf16 = mybir.dt.float32, mybir.dt.float32r, mybir.dt.bfloat16
    ALU, ACT, AX = mybir.AluOpType, mybir.ActivationFunctionType, mybir.AxisListType

    with ExitStack() as ctx:
        def sb(name, shape, dt=fp32):
            return ctx.enter_context(nc.sbuf_tensor(name, shape, dt))

        def sem(name):
            return ctx.enter_context(nc.semaphore(name))

        raw = [sb(f"raw{i}", [P, UNIT]) for i in range(RAWS)]
        ring_hi = [sb(f"ring_hi{i}", [P, UNIT], f32r) for i in range(SLOTS)]
        ring_lo = [sb(f"ring_lo{i}", [P, UNIT], f32r) for i in range(SLOTS)]
        x_tok = sb("x_tok", [P, TT, D_MODEL])
        xh = sb("xh", [P, KT, SEQ], f32r)
        xl = sb("xl", [P, KT, SEQ], f32r)
        cst = sb("cst", [P, C_ALL])
        ident = cst[:, C_ID:C_ID + P]
        ident_b = sb("ident_b", [P, P], bf16)
        ident_r = sb("ident_r", [P, P], f32r)
        cmask_b = sb("cmask_b", [P, P], bf16)
        ones = sb("ones", [1, P])
        neg_half = sb("neg_half", [P, 1])
        stage = sb("stage", [P, 4 * P])
        ffn_stage = stage[0:4 * STEPS, :].rearrange("c (k p) -> c k p", k=4)
        par_stage = sb("par_stage", [56, P])
        ffn_par = sb("ffn_par", [P, STEPS, 2, 2, 4])
        step_par = sb("step_par", [P, 2, 2, 2, 4])
        par = sb("par", [P, 56])
        gate_w = sb("gate_w", [P, KT, NGATE])
        gate_wh = sb("gate_wh", [P, KT, NGATE], f32r)
        gate_wl = sb("gate_wl", [P, KT, NGATE], f32r)
        qkv = sb("qkv", [P, TT, 20 * HEAD])
        ln_par = qkv[:, :, :].rearrange("p t f -> p (t f)")[:, 0:2 * D_MODEL].rearrange("p (a f) -> p a f", a=2)
        work = sb("work", [P, 2048])
        acc = work[:, 0:1024].rearrange("p (t f) -> p t f", t=TT)
        part = work[:, 1024:2048].rearrange("p (t f) -> p t f", t=TT)
        xT0 = work[:, 1024:2048].rearrange("p (k n) -> p k n", k=KT)
        ffn_y = work[:].rearrange("p (s v c n) -> p s v c n", s=2, v=2, c=2)
        w2 = sb("w2", [P, 2, 2, HEAD])
        b2 = sb("b2", [1, 2, HEAD])
        egateT = sb("egateT", [NGATE, SEQ])
        egate = sb("egate", [P, TT, NGATE])
        qTh = sb("qTh", [P, NPAIR, SEQ], f32r)
        qTl = sb("qTl", [P, NPAIR, SEQ], f32r)
        kTh = sb("kTh", [P, 2, SEQ], f32r)
        kTl = sb("kTl", [P, 2, SEQ], f32r)
        blocks = [part[:, :, :].rearrange("p t f -> p (t f)")[:, 480 * kv:480 * (kv + 1)]
                  .rearrange("p (j b) -> p j b", j=NJ) for kv in range(2)]
        hid = sb("hid", [NG * NBLK, CMP_HID])
        hx = sb("hx", [P, 2, 2 * NBLK])
        hu = sb("hu", [P, 2, 2 * NBLK])
        ht = sb("ht", [P, 2, 2 * NBLK])
        hk = sb("hk", [P, 2, 2 * NBLK])
        hv = sb("hv", [P, 2, NH * NBLK])
        kcTh = sb("kcTh", [P, NG, NBLK], f32r)
        kcTl = sb("kcTl", [P, NG, NBLK], f32r)
        vbd = stage[0:NH * NBLK, :].rearrange("p (h d) -> p h d", h=NH)
        probs = [sb(f"probs{i}", [P, 512]) for i in range(2)]
        probsT = [sb(f"probsT{i}", [P, 512]) for i in range(2)]
        smax = sb("smax", [P, N_ATT - 1, NPAIR])
        cmax = sb("cmax", [P, TT * NH])
        nmax = sb("nmax", [P, 2, NPAIR])
        rsum = sb("rsum", [P, 3, TT, NH])
        coef = sb("coef", [P, 3, TT, NH])
        mstat = sb("mstat", [P, TT, NH])
        mroot = sb("mroot", [P, TT, NH])
        conv_z = sb("conv_z", [P, 2, SEQ])
        conv_y = sb("conv_y", [P, 2, SEQ])
        conv_o = sb("conv_o", [P, 4, SEQ])
        conv_sq = sb("conv_sq", [P, 2, SEQ])
        rope_a, rope_b = (conv_sq[:, n, 0:14 * ROPE].rearrange("p (h d) -> p h d", h=14) for n in range(2))
        cstat = sb("cstat", [P, 2, TT, 4])
        croot = sb("croot", [P, 2, TT, 4])
        hTh = sb("hTh", [P, 2, 2, SEQ], f32r)
        hTl = sb("hTl", [P, 2, 2, SEQ], f32r)
        blocks_h, blocks_l = ([a[:, kv].rearrange("p c n -> p (c n)")[:, 0:480].rearrange("p (j b) -> p j b", j=NJ)
                               for kv in range(2)] for a in (hTh, hTl))
        roots_h, roots_l = (a[:].rearrange("p a (t c) n -> p a t (c n)", t=TT) for a in (hTh, hTl))
        stats = sb("stats", [P, TT, 2, 6])
        mv = sb("mv", [P, TT, 2])
        veps = sb("veps", [P, TT])
        rstd = sb("rstd", [P, TT])
        CMP_BANK = (7, 2)
        XT_BANK, MIX_BANK, X1T_BANK, FFN_BANK = (4, 6), (4, 0), (6, 2), (0, 2)
        bank = [ctx.enter_context(nc.psum_tensor(f"bank{i}", [P, 512], fp32)) for i in range(8)]

        raw_in = [sem(f"raw_in{i}") for i in range(RAWS)]
        split_done = [sem(f"split_done{i}") for i in range(RAWS)]
        slot_free = [sem(f"slot_free{i}") for i in range(SLOTS)]
        hi_done = sem("hi_done")
        x_in, ident_in = [sem("x_in0"), sem("x_in1")], sem("ident_in")
        const_in, par_in, gate_in = sem("const_in"), sem("par_in"), sem("gate_in")
        ln_in, out_done, stage_free = sem("ln_in"), sem("out_done"), sem("stage_free")
        const_ready, masks_ready = sem("const_ready"), sem("masks_ready")
        par_T, par_ready, gate_hi, gate_lo = sem("par_T"), sem("par_ready"), sem("gate_hi"), sem("gate_lo")
        gates_in, gates_T = sem("gates_in"), sem("gates_T")
        xT_copied, x1T_copied = sem("xT_copied"), sem("x1T_copied")
        x_ready, xT_done, xT_hi, xT_lo = sem("x_ready"), sem("xT_done"), sem("xT_hi"), [sem("xT_lo0"), sem("xT_lo1")]
        x1_ready, x1T_done, x1T_hi, x1T_lo = sem("x1_ready"), sem("x1T_done"), sem("x1T_hi"), [sem("x1T_lo0"), sem("x1T_lo1")]
        proj_done, qkv_copied, rope_done = sem("proj_done"), sem("qkv_copied"), sem("rope_done")
        qkT_done, qkT_copied, qkT_hi = sem("qkT_done"), sem("qkT_copied"), sem("qkT_hi")
        blocks_in, blocks_hi, blocks_lo = sem("blocks_in"), sem("blocks_hi"), sem("blocks_lo")
        hid_copied, hidT_done = sem("hid_copied"), sem("hidT_done")
        tanh_in, tanh_done, hid_ready = sem("tanh_in"), sem("tanh_done"), sem("hid_ready")
        cmp_done, kc_hi, cmp_copied = sem("cmp_done"), sem("kc_hi"), sem("cmp_copied")
        s_done, max_done, exp_done, cmp_p = sem("s_done"), sem("max_done"), sem("exp_done"), sem("cmp_p")
        pT_done, pT_copied, pv_done, o_read = sem("pT_done"), sem("pT_copied"), sem("pv_done"), sem("o_read")
        att_ss, att_root, att_ready, mixT_done = sem("att_ss"), sem("att_root"), sem("att_ready"), sem("mixT_done")
        c_copied, z_done, y_init, conv_tapped = sem("c_copied"), sem("z_done"), sem("y_init"), sem("conv_tapped")
        conv_out, sq_done, ms_used = sem("conv_out"), sem("sq_done"), sem("ms_used")
        ms_read, conv_root, roots_hi, roots_lo = sem("ms_read"), sem("conv_root"), sem("roots_hi"), sem("roots_lo")
        bc_done, conv_norm = sem("bc_done"), sem("conv_norm")
        mix_hi, mix_lo, y1_done = sem("mix_hi"), sem("mix_lo"), sem("y1_done")
        ln_stats, ln_root = sem("ln_stats"), sem("ln_root")
        step_par_in, fy_init = sem("step_par_in"), sem("fy_init")
        fy_mid, fy_done = sem("fy_mid"), sem("fy_done")
        silu_done, h_done, h_hi, h_lo = sem("silu_done"), sem("h_done"), sem("h_hi"), sem("h_lo")
        y2_done = sem("y2_done")
        passed = sem("passed")
        dve_seq, pool_seq = sem("dve_seq"), sem("pool_seq")

        def raw_round(L, u, i=0):
            return L * RAW_USES[u % RAWS] + u // RAWS + 2 * i

        def slot_round(L, u, i=0):
            return L * SLOT_USES[u % SLOTS] + u // SLOTS + i

        def unit_used(eng, L, u, i=0):
            eng.wait_ge(slot_free[u % SLOTS], CREDIT + slot_round(L, u, i) + 1)

        def split_hi(act, L, u, i=0):
            act.wait_ge(raw_in[u % RAWS], 16 * (raw_round(L, u, i) + 1))
            act.wait_ge(slot_free[u % SLOTS], CREDIT + slot_round(L, u, i))
            nc.scalar.activation(ring_hi[u % SLOTS][:], raw[u % RAWS][:], ACT.Copy).then_inc(hi_done, 1)

        def split_lo(eng, L, u, i=0):
            eng.wait_ge(hi_done, L * NU + u + 6 * i + 1)
            eng.tensor_tensor(ring_lo[u % SLOTS][:], raw[u % RAWS][:], ring_hi[u % SLOTS][:].bitcast(fp32),
                              ALU.subtract).then_inc(split_done[u % RAWS], 1)

        def bcast(ap, axis, shape):
            return ap.unsqueeze(axis).to_broadcast(shape)

        def settled(eng):
            eng.sem_inc(passed, 1)

        block = ctx.enter_context(nc.Block())

        @block.sync
        def _(sp):
            def load(L, u, i, src, **view):
                dst = raw[u % RAWS][:]
                if view:
                    dst = dst.rearrange(view.pop("to"), **view)
                sp.wait_ge(split_done[u % RAWS], CREDIT + raw_round(L, u, i))
                settled(sp)
                sp.dma_start(dst, src).then_inc(raw_in[u % RAWS], 16)

            def of(w, L):
                return w[bass.ds(L, 1)].rearrange("o a b -> (o a) b")

            def load_in(L, u, k0, nk, col):
                src = of(w_in, L)[P * k0:P * (k0 + nk), col:col + UNIT // nk].rearrange("(k p) n -> p k n", p=P)
                load(L, u, 0, src, to="p (k n) -> p k n", k=nk)

            def load_w1(L, kv):
                for half, u in enumerate(W1_U[kv]):
                    src = cmp_w1[bass.ds(L, 1), kv, P * 8 * half:P * 8 * (half + 1), :].rearrange("o (j p) n -> p (o j) n", p=P)
                    load(L, u, 0, src, to="p (k n) -> p k n", k=8)

            def load_up(L, u, i, gate, step):
                src = of(w_up, L)[:, bass.ds(D_FF * gate + step * 2 * P, 2 * P)].rearrange("(k p) n -> p k n", p=P)
                load(L, u, i, src, to="p (k n) -> p k n", k=KT)

            def load_rows(L, u, i, w, row):
                src = of(w, L)[bass.ds(row, 2 * P), :].rearrange("(k p) n -> p k n", p=P)
                load(L, u, i, src, to="p (k n) -> p k n", k=2)

            sp.sem_inc(stage_free, CREDIT)
            for free in split_done:
                sp.sem_inc(free, CREDIT)
            with sp.Fori(0, DEPTH) as L:
                load_in(L, 0, 0, 4, Q0)
                load_in(L, 1, 4, 4, Q0)
                load_in(L, 2, 0, 4, KV0)
                sp.wait_ge(stage_free, CREDIT + L)
                sp.dma_start(gate_w[:], of(w_in, L)[:, G0COL:G0COL + NGATE].rearrange("(k p) n -> p k n", p=P)).then_inc(gate_in, 16)
                sp.dma_start(ffn_stage[:, 0:3, :], of(ffn_conv_w, L).rearrange("k (c p) -> c k p", p=P)).then_inc(par_in, 16)
                sp.dma_start(ffn_stage[:, 3, :], ffn_conv_b[bass.ds(L, 1)].rearrange("o (c p) -> (o c) p", p=P)).then_inc(par_in, 16)
                sp.dma_start(par_stage[0:8, :], head_norm_g[bass.ds(L, 1)].rearrange("o (c p) -> (o c) p", p=P)).then_inc(par_in, 16)
                sp.dma_start(par_stage[8:20, :], of(short_conv_w, L).rearrange("k (c p) -> (k c) p", p=P)).then_inc(par_in, 16)
                sp.dma_start(par_stage[20:24, :], of(cmp_b1, L).rearrange("k (c p) -> (k c) p", p=P)).then_inc(par_in, 16)
                sp.dma_start(par_stage[24:56, :], cmp_pe[bass.ds(L, 1)].rearrange("o k (j l) d -> (o k j) (l d)", l=2)).then_inc(par_in, 16)
                sp.dma_start(w2[:], cmp_w2[bass.ds(L, 1)].rearrange("o k (h p) d -> p (o k) h d", p=P)).then_inc(par_in, 16)
                sp.dma_start(b2[:], cmp_b2[bass.ds(L, 1)]).then_inc(par_in, 16)
                load_in(L, 3, 4, 4, KV0)
                load_in(L, 4, 0, 8, KW0)
                for pair in range(2):
                    for n, sect in enumerate((1, 2, 0)):
                        if pair == 0 and n == 2:
                            load_w1(L, 0)
                        load_in(L, CONV_U[3 * pair + n], 0, 8, CONV_W * sect + 2 * P * pair)
                    if pair == 0:
                        load_w1(L, 1)
                for n in range(4):
                    load_rows(L, U_OUT + n, 0, w_out, 2 * P * n)
                for s in range(3):
                    for gate in range(2):
                        load_up(L, U_FFN + 2 * s + gate, 0, gate, s)
                with sp.Fori(0, (STEPS - 3) // 2) as i:
                    for odd in range(2):
                        load_rows(L, 25 + 3 * odd, i, w_down, (2 * i + odd) * 2 * P)
                        for gate in range(2):
                            load_up(L, 26 + 3 * odd + gate, i, gate, 2 * i + 3 + odd)
                for s in range(STEPS - 3, STEPS):
                    load_rows(L, NU - STEPS + s, 0, w_down, s * 2 * P)
            for t in range(TT):
                for n in range(2):
                    sp.wait_ge(x_ready, 4 * DEPTH + 2 * t + n + 1)
                    cols = slice(512 * n, 512 * (n + 1))
                    sp.dma_start(out[0, P * t:P * (t + 1), cols], x_tok[:, t, cols]).then_inc(out_done, 16)
            sp.wait_ge(out_done, 16 * 2 * TT)

        @block.scalar
        def _(act):
            for free in slot_free:
                act.sem_inc(free, CREDIT)
            act.dma_start(x_tok[:, 0, :], x[0, 0:P, :]).then_inc(x_in[0], 16)
            act.dma_start(ident, consts[:, C_ID:C_ID + P]).then_inc(ident_in, 16)
            act.dma_start(cst[:, P:], consts[:, P:]).then_inc(const_in, 16)
            act.dma_start(x_tok[:, 1, :], x[0, P:2 * P, :]).then_inc(x_in[1], 16)

            def x_high(L, banks, t, done, hi, copied):
                for b in range(2):
                    act.wait_ge(done, 4 * L + 2 * t + b + 1)
                    nc.scalar.activation(xh[:, 4 * b:4 * b + 4, P * t:P * (t + 1)],
                                         bank[banks[t] + b][:].rearrange("p (k n) -> p k n", k=4),
                                         ACT.Copy).then_inc(hi, 1)
                    if t == 0:
                        nc.scalar.activation(xT0[:, 4 * b:4 * b + 4, :].rearrange("p k n -> p (k n)"), bank[banks[t] + b][:],
                                             ACT.Copy).then_inc(copied, 1)

            def copy_q(L, t):
                if t == 0:
                    act.wait_ge(proj_done, 4 * L + 1)
                else:
                    unit_used(act, L, 1)
                nc.scalar.activation(qkv[:, t, 0:512].rearrange("p (i g d) -> p g i d", i=NPAIR, g=NG),
                                     bank[t][:].rearrange("p (g i d) -> p g i d", i=NPAIR, g=NG),
                                     ACT.Copy).then_inc(qkv_copied, 1)

            def kv_slots(t):
                return qkv[:, t, 512:1280].rearrange("p (b a f) -> p b a f", b=2, a=3)

            def copy_kv(L, t):
                if t == 0:
                    act.wait_ge(proj_done, 4 * L + 2)
                else:
                    unit_used(act, L, 3)
                for b in range(2):
                    ins = nc.scalar.activation(kv_slots(t)[:, b, 0:2, :],
                                               bank[2 + t][:].rearrange("p (a b f) -> p b a f", a=2, b=2)[:, b], ACT.Copy)
                ins.then_inc(qkv_copied, 1)

            def copy_kw(L, t):
                if t == 0:
                    act.wait_ge(proj_done, 4 * L + 3)
                else:
                    unit_used(act, L, 4)
                nc.scalar.activation(kv_slots(t)[:, :, 2, :], bank[4 + t][:, 0:256].rearrange("p (b f) -> p b f", b=2),
                                     ACT.Copy).then_inc(qkv_copied, 1)

            def copy_c(L, pair):
                unit_used(act, L, CONV_U[3 * pair])
                if pair:
                    act.wait_ge(conv_out, 2 * L + pair)
                nc.scalar.activation(conv_z[:].rearrange("p c n -> p (c n)"), bank[4 + pair][:], ACT.Copy).then_inc(c_copied, 1)

            def conv_init(L, pair):
                act.wait_ge(z_done, 2 * L + pair + 1)
                for m in range(2):
                    tap = 8 + 2 * 4 + 2 * pair + m
                    ins = nc.scalar.activation(conv_y[:, m, :], conv_z[:, m, :], ACT.Copy, scale=par[:, tap:tap + 1])
                ins.then_inc(y_init, 1)

            def conv_square(L, pair):
                act.wait_ge(conv_out, 2 * L + pair + 1)
                if pair:
                    act.wait_ge(ms_used, 2 * L + pair)
                nc.scalar.activation(conv_sq[:], conv_o[:, 2 * pair:2 * pair + 2, :], ACT.Square).then_inc(sq_done, 1)

            def copy_hidden(L, kv):
                unit_used(act, L, W1_U[kv][1])
                if kv:
                    act.wait_ge(hidT_done, 2 * L + 1)
                nc.scalar.activation(hid[:], bank[2 + kv][0:NG * NBLK, 0:CMP_HID], ACT.Copy).then_inc(hid_copied, 1)

            def tanh(L, kv):
                act.wait_ge(tanh_in, 2 * L + kv + 1)
                nc.scalar.activation(ht[:], hu[:], ACT.Tanh).then_inc(tanh_done, 1)

            def exps(L, n):
                br, t, g, heads, kb = ATT[n]
                keys = P * kb
                act.wait_ge(max_done, N_ATT * L + n + 1)
                if n >= 2:
                    act.wait_ge(pT_done, N_ATT * L + n - 1)
                for j, h in enumerate(heads):
                    ins = nc.scalar.activation(probs[n % 2][:, keys * j:keys * (j + 1)], bank[n % 2][:, keys * j:keys * (j + 1)],
                                               ACT.Exp, bias=nmax[:, n % 2, j:j + 1], scale=SCALE,
                                               accum_out=rsum[:, br, t, NPAIR * g + h:NPAIR * g + h + 1])
                ins.then_inc(exp_done, 1)

            def roots_high(L, pair):
                act.wait_ge(conv_root, 2 * L + pair + 1)
                nc.scalar.activation(roots_h[:, pair].rearrange("p t (h d) -> p (t h) d", d=HEAD),
                                     bcast(croot[:, pair].rearrange("p t h -> p (t h)"), 2, [P, 4 * TT, HEAD]),
                                     ACT.Copy).then_inc(roots_hi, 1)

            def mix_high(j, dst, src):
                nc.scalar.activation(dst, src, ACT.Copy, scale=par[:, j:j + 1]).then_inc(mix_hi, 1)

            def mix_conv(L, pair):
                act.wait_ge(conv_norm, 2 * L + pair + 1)
                for j in (2 * pair, 2 * pair + 1):
                    mix_high(j, xh[:, j, :], conv_o[:, j, :])

            def ffn_step(L, s, odd, value, gate, h_user, units):
                G = L * STEPS + s
                act.wait_ge(step_par_in, G + 1)
                act.wait_ge(h_lo, H_CREDIT + G - 1)
                for v, u in enumerate((value, gate)):
                    unit_used(act, L, *u)
                    for c in range(2):
                        ins = nc.scalar.activation(ffn_y[:, odd, v, c, :], bank[4 + 2 * odd + v][:, SEQ * c:SEQ * (c + 1)],
                                                   ACT.Identity, scale=step_par[:, odd, v, c, 2:3],
                                                   bias=step_par[:, odd, v, c, 3:4])
                    ins.then_inc(fy_init, 1)
                for u in units[0:1]:
                    split_hi(act, L, *u)
                act.wait_ge(fy_done, FY_CREDIT + 2 * G + 2)
                y = ffn_y[:, odd].rearrange("p v c n -> p v (c n)")
                nc.scalar.activation(y[:, 1], y[:, 1], ACT.Silu).then_inc(silu_done, 1)
                for u in units[1:2]:
                    split_hi(act, L, *u)
                act.wait_ge(h_done, G + 1)
                if h_user:
                    unit_used(act, L, *h_user)
                nc.scalar.activation(hTh[:, odd].rearrange("p c n -> p (c n)"), y[:, 0], ACT.Copy).then_inc(h_hi, 1)
                for u in units[2:3]:
                    split_hi(act, L, *u)

            with act.Fori(0, DEPTH) as L:
                split_hi(act, L, 0)
                split_hi(act, L, 1)
                x_high(L, XT_BANK, 0, xT_done, xT_hi, xT_copied)
                split_hi(act, L, 2)
                split_hi(act, L, 3)
                x_high(L, XT_BANK, 1, xT_done, xT_hi, xT_copied)
                split_hi(act, L, 4)
                copy_q(L, 0)
                act.wait_ge(gate_in, 16 * (L + 1))
                nc.scalar.activation(gate_wh[:], gate_w[:], ACT.Copy).then_inc(gate_hi, 1)
                split_hi(act, L, 5)
                copy_kv(L, 0)
                copy_q(L, 1)
                split_hi(act, L, 6)
                split_hi(act, L, 7)
                copy_kv(L, 1)
                act.wait_ge(par_T, L + 1)
                for v in range(2):
                    nc.scalar.activation(
                        ffn_par[:, :, v].rearrange("p s c k -> p k s c"),
                        bank[6][:, 0:176].rearrange("p (k v s c) -> p k v s c", k=4, v=2, c=2)[:, :, v], ACT.Copy)
                nc.scalar.activation(par[:], bank[6][:, 176:232], ACT.Copy).then_inc(par_ready, 1)
                split_hi(act, L, 8)
                copy_kw(L, 0)
                split_hi(act, L, 9)
                copy_kw(L, 1)
                act.wait_ge(proj_done, 4 * L + 4)
                nc.scalar.activation(egateT[:], bank[7][0:NGATE, 0:SEQ], ACT.Exp, scale=-1.0).then_inc(gates_in, 1)
                split_hi(act, L, 10)
                copy_c(L, 0)
                for b, (dst, src) in enumerate(((qTh[:, 0:2, :], bank[6]), (qTh[:, 2:4, :], bank[7]), (kTh[:], bank[0]))):
                    act.wait_ge(qkT_done, 4 * L + b + 1)
                    nc.scalar.activation(dst.rearrange("p i n -> p (i n)"), src[:], ACT.Copy).then_inc(qkT_hi, 1)
                for kv in range(2):
                    act.wait_ge(blocks_in, 2 * L + kv + 1)
                    nc.scalar.activation(blocks_h[kv], blocks[kv], ACT.Copy).then_inc(blocks_hi, 1)
                split_hi(act, L, 11)
                conv_init(L, 0)
                exps(L, 0)
                copy_hidden(L, 0)
                tanh(L, 0)
                exps(L, 1)
                split_hi(act, L, 12)
                act.wait_ge(cmp_done, 2 * L + 1)
                for g in range(NG):
                    rows = slice(HEAD * g, HEAD * (g + 1))
                    ins = nc.scalar.activation(kcTh[rows, g, :], bank[2][rows, 384:384 + NBLK], ACT.Copy)
                ins.then_inc(kc_hi, 1)
                split_hi(act, L, 13)
                split_hi(act, L, 14)
                copy_hidden(L, 1)
                conv_square(L, 0)
                tanh(L, 1)
                for n in range(2, 12):
                    exps(L, n)
                    if n == 3:
                        copy_c(L, 1)
                    elif n == 5:
                        conv_init(L, 1)
                    elif n == 7:
                        roots_high(L, 0)
                    elif n == 9:
                        mix_conv(L, 0)
                    elif n == 10:
                        conv_square(L, 1)
                    else:
                        split_hi(act, L, {2: 15, 4: 16, 6: 17, 8: 18, 11: 19}[n])
                act.wait_ge(max_done, N_ATT * L + 13)
                flat = probs[0][:, 0:TT * NH * NBLK]
                nc.scalar.activation(flat, flat, ACT.Exp, scale=SCALE).then_inc(exp_done, 1)
                roots_high(L, 1)
                split_hi(act, L, 20)
                mix_conv(L, 1)
                for t in range(TT):
                    act.wait_ge(mixT_done, 2 * L + t + 1)
                    for j in range(4):
                        mix_high(4 + j, xh[:, 4 + j, P * t:P * (t + 1)], bank[6 + t][:, P * j:P * (j + 1)])
                act.wait_ge(pv_done, 14 * L + 14)
                act.wait_ge(rope_done, 2 * L + 2)
                for a, w in enumerate((ln1_g, ln1_b)):
                    act.dma_start(ln_par[:, a, :], w[bass.ds(L, 1)].to_broadcast([P, D_MODEL])).then_inc(ln_in, 16)
                x_high(L, X1T_BANK, 0, x1T_done, x1T_hi, x1T_copied)
                split_hi(act, L, 21)
                split_hi(act, L, 22)
                x_high(L, X1T_BANK, 1, x1T_done, x1T_hi, x1T_copied)
                for a, w in enumerate((ln2_g, ln2_b)):
                    act.dma_start(ln_par[:, a, :], w[bass.ds(L, 1)].to_broadcast([P, D_MODEL])).then_inc(ln_in, 16)
                split_hi(act, L, 23)
                split_hi(act, L, 24)
                ffn_step(L, 0, 0, (19, 0), (20, 0), None, [(25, 0), (26, 0)])
                ffn_step(L, 1, 1, (21, 0), (22, 0), None, [(27, 0), (28, 0)])
                ffn_step(L, 2, 0, (23, 0), (24, 0), (25, 0), [(29, 0), (30, 0), (31, 0)])
                with act.Fori(0, (STEPS - 5) // 2) as i:
                    ffn_step(L, 2 * i + 3, 1, (26, i), (27, i), (28, i), [(32, i), (33, i), (34, i)])
                    ffn_step(L, 2 * i + 4, 0, (29, i), (30, i), (31, i), [(35, i), (36, i), (37, i)])
                last = (STEPS - 5) // 2
                ffn_step(L, STEPS - 2, 1, (26, last), (27, last), (28, last), [(NU - 2, 0), (NU - 1, 0)])
                ffn_step(L, STEPS - 1, 0, (29, last), (30, last), (31, last), [])

        @block.gpsimd
        def _(pool):
            nc.gpsimd.memset(neg_half[:], -0.5).then_inc(const_ready, 1)
            nc.gpsimd.memset(kcTl[:].bitcast(fp32), 0.0).then_inc(const_ready, 1)
            nc.gpsimd.memset(ones[:], 1.0).then_inc(const_ready, 1)
            nc.gpsimd.memset(kcTh[:].bitcast(fp32), 0.0).then_inc(const_ready, 1)
            pool.wait_ge(const_ready, 4)

            def root(chain, var, eps_out, eps, mul, result, half, signal):
                settled(pool)
                chain.mark(nc.gpsimd.tensor_scalar(eps_out, var, mul, eps, ALU.mult, ALU.add))
                chain.wait()
                nc.gpsimd.tensor_tensor(result, eps_out, half, ALU.pow).then_inc(signal, 1)

            def x_low_0(L, b, copied, lo):
                pool.wait_ge(copied, 2 * L + b + 1)
                nc.gpsimd.tensor_tensor(xl[:, 4 * b:4 * b + 4, 0:P], xT0[:, 4 * b:4 * b + 4, :],
                                        xh[:, 4 * b:4 * b + 4, 0:P].bitcast(fp32), ALU.subtract).then_inc(lo, 1)

            def deviation(count, t, chain):
                pool.wait_ge(ln_stats, count)
                root(chain, mv[:, t, 1:2], veps[:, t:t + 1], 1e-5, 1.0, rstd[:, t:t + 1], neg_half[:, 0:1], ln_root)

            def conv_deviation(L, pair, chain):
                pool.wait_ge(ms_read, 2 * L + pair + 1)
                flat = [a[:, pair].rearrange("p t h -> p (t h)") for a in (cstat, croot)]
                root(chain, flat[0], flat[0], 1e-6, 1.0, flat[1], neg_half[:].to_broadcast([P, 4 * TT]), conv_root)

            def step_params(s, odd):
                settled(pool)
                nc.gpsimd.tensor_copy(step_par[:, odd].rearrange("p v c k -> p (v c k)"),
                                      ffn_par[:, bass.ds(s, 1)].rearrange("p o v c k -> p (o v c k)"))\
                    .then_inc(step_par_in, 1)

            def next_params(L, s, odd):
                pool.wait_ge(fy_done, FY_CREDIT + 2 * (L * STEPS + s) + 2)
                step_params(s + 2, odd)

            with pool.Fori(0, DEPTH) as L:
                chain = Chain(pool, pool_seq, L, POOL_STEPS)
                split_lo(nc.gpsimd, L, 0)
                x_low_0(L, 0, xT_copied, xT_lo[0])
                deviation(LN_CREDIT + 4 * L, 1, chain)
                x_low_0(L, 1, xT_copied, xT_lo[0])
                for u in (2, 4, 5, 7, 8, 10, 11, 13):
                    split_lo(nc.gpsimd, L, u)
                conv_deviation(L, 0, chain)
                for u in range(14, 19):
                    split_lo(nc.gpsimd, L, u)
                conv_deviation(L, 1, chain)
                split_lo(nc.gpsimd, L, 19)
                for t in range(TT):
                    pool.wait_ge(att_ss, 2 * L + t + 1)
                    root(chain, mstat[:, t, :], mstat[:, t, :], 1e-6, 1.0 / HEAD, mroot[:, t, :], neg_half[:].to_broadcast([P, NH]),
                         att_root)
                split_lo(nc.gpsimd, L, 20)
                pool.wait_ge(par_ready, L + 1)
                for odd in range(2):
                    step_params(odd, odd)
                deviation(LN_CREDIT + 4 * L + 1, 0, chain)
                deviation(LN_CREDIT + 4 * L + 2, 1, chain)
                for b in range(2):
                    x_low_0(L, b, x1T_copied, x1T_lo[0])
                for u in range(21, 25):
                    split_lo(nc.gpsimd, L, u)
                for s in range(3):
                    next_params(L, s, s % 2)
                    for u in (26 + 3 * s, 27 + 3 * s)[:2 * (s < 2)]:
                        split_lo(nc.gpsimd, L, u)
                with pool.Fori(0, (STEPS - 5) // 2) as i:
                    for odd in range(2):
                        split_lo(nc.gpsimd, L, 32 + 3 * odd, i)
                        split_lo(nc.gpsimd, L, 33 + 3 * odd, i)
                        next_params(L, 2 * i + 3 + odd, 1 - odd)
                deviation(LN_CREDIT + 4 * L + 3, 0, chain)
                chain.close()
            deviation(LN_CREDIT + 4 * DEPTH, 1, Chain(pool, pool_seq, DEPTH, POOL_STEPS))

        @block.vector
        def _(dve):
            V = nc.vector
            dve.wait_ge(x_in[0], 16)
            dve.sem_inc(x_ready, 2)
            dve.wait_ge(ident_in, 16)
            V.tensor_copy(ident_b[:], ident).then_inc(masks_ready, 1)
            V.tensor_copy(ident_r[:], ident).then_inc(masks_ready, 1)
            dve.wait_ge(const_in, 16)
            V.tensor_copy(cmask_b[:], cst[:, C_CM:C_CM + P]).then_inc(masks_ready, 1)
            dve.wait_ge(x_in[1], 16)
            dve.sem_inc(x_ready, 2)
            dve.sem_inc(fy_done, FY_CREDIT)
            dve.sem_inc(h_lo, H_CREDIT)
            V.memset(mv[:], 1.0).then_inc(ln_stats, LN_CREDIT)
            dve.wait_ge(const_ready, 4)

            def x_low(L, banks, t, hi, lo):
                for b in range(2):
                    dve.wait_ge(hi, 4 * L + 2 * t + b + 1)
                    dst = slice(4 * b, 4 * b + 4), slice(P * t, P * (t + 1))
                    V.tensor_tensor(xl[:, dst[0], dst[1]], bank[banks[t] + b][:].rearrange("p (k n) -> p k n", k=4),
                                    xh[:, dst[0], dst[1]].bitcast(fp32), ALU.subtract).then_inc(lo, 1)

            def rope(L, t, chain):
                dve.wait_ge(qkv_copied, 6 * L + 5 + t)
                head = qkv[:, t, 0:14 * HEAD].rearrange("p (h d) -> p h d", d=HEAD)
                cc = bcast(cst[:, C_CC + 16 * t:C_CC + 16 * t + 16], 1, [P, 14, 16])
                ss = cst[:, C_SS + 16 * t:C_SS + 16 * t + 16]
                if t:
                    dve.wait_ge(rope_done, 2 * L + t)
                V.tensor_tensor(rope_a, head[:, :, 0:16], cc, ALU.mult)
                V.tensor_tensor(rope_b[:, :, 0:8], head[:, :, 8:16], bcast(ss[:, 0:8], 1, [P, 14, 8]), ALU.mult)
                chain.mark(V.tensor_tensor(rope_b[:, :, 8:16], head[:, :, 0:8], bcast(ss[:, 8:16], 1, [P, 14, 8]), ALU.mult))
                chain.wait()
                V.tensor_tensor(head[:, :, 0:16], rope_a, rope_b, ALU.add).then_inc(rope_done, 1)

            def conv_taps(L, pair, chain):
                dve.wait_ge(y_init, 2 * L + pair + 1)
                for back in (1, 2):
                    if back == 2:
                        chain.wait()
                    for m in range(2):
                        tap = 8 + (2 - back) * 4 + 2 * pair + m
                        ins = V.scalar_tensor_tensor(conv_y[:, m, back:], conv_z[:, m, 0:SEQ - back], par[:, tap:tap + 1],
                                                     conv_y[:, m, back:], ALU.mult, ALU.add)
                    if back == 1:
                        chain.mark(ins)
                    else:
                        ins.then_inc(conv_tapped, 1)

            def conv_product(L, pair):
                dve.wait_ge(conv_tapped, 2 * L + pair + 1)
                unit_used(dve, L, CONV_U[3 * pair + 2])
                V.tensor_tensor(conv_o[:, 2 * pair:2 * pair + 2, :].rearrange("p c n -> p (c n)"),
                                conv_y[:].rearrange("p c n -> p (c n)"), bank[4 + pair][:], ALU.mult).then_inc(conv_out, 1)

            def conv_gate(L, pair):
                unit_used(dve, L, CONV_U[3 * pair + 1])
                dve.wait_ge(c_copied, 2 * L + pair + 1)
                z = conv_z[:].rearrange("p c n -> p (c n)")
                V.tensor_tensor(z, z, bank[5 - pair][:], ALU.mult).then_inc(z_done, 1)

            def hidden(L, kv, chain):
                dve.wait_ge(hidT_done, 2 * L + kv + 1)
                if kv:
                    dve.wait_ge(hid_ready, 2 * L + 1)
                for h in range(2):
                    b1 = par[:, 20 + 2 * kv + h:21 + 2 * kv + h]
                    ins = V.tensor_scalar(hx[:, h, :], bank[2 + kv][:, 256 + 32 * h:286 + 32 * h], b1, None, ALU.add)
                chain.mark(ins)
                chain.wait()
                chain.mark(V.tensor_tensor(hu[:], hx[:], hx[:], ALU.mult))
                chain.wait()
                c = float(np.sqrt(2.0 / np.pi))
                chain.mark(V.tensor_scalar(hu[:], hu[:], 0.044715 * c, c, ALU.mult, ALU.add))
                chain.wait()
                V.tensor_tensor(hu[:], hu[:], hx[:], ALU.mult).then_inc(tanh_in, 1)
                dve.wait_ge(tanh_done, 2 * L + kv + 1)
                chain.mark(V.tensor_scalar(ht[:], ht[:], 0.5, 0.5, ALU.mult, ALU.add))
                chain.wait()
                if kv == 0:
                    V.tensor_tensor(hk[:], ht[:], hx[:], ALU.mult).then_inc(hid_ready, 1)
                else:
                    chain.mark(V.tensor_tensor(ht[:], ht[:], hx[:], ALU.mult))
                    chain.wait()
                    for h in range(2):
                        ins = V.tensor_copy(hv[:, h, :].rearrange("p (i n) -> p i n", i=NPAIR),
                                            bcast(ht[:, h, :], 1, [P, NPAIR, NG * NBLK]))
                    ins.then_inc(hid_ready, 1)

            def maxima(L, n, chain):
                br, t, g, heads, kb = ATT[n]
                dve.wait_ge(s_done, N_ATT * L + n + 1)
                nh = len(heads)
                chain.mark(V.tensor_reduce(smax[:, n, 0:nh], bank[n % 2][:].rearrange("p (h k) -> p h k", h=nh), AX.X, ALU.max))
                chain.wait()
                V.tensor_scalar(nmax[:, n % 2, 0:nh], smax[:, n, 0:nh], -SCALE, None, ALU.mult).then_inc(max_done, 1)

            def copy_pT(L, n):
                dve.wait_ge(pT_done, N_ATT * L + n + 1)
                if n >= 2:
                    dve.wait_ge(pv_done, 14 * L + n - 1)
                width = 512 if n < 12 else 2 * P
                rows = P if n < 12 else NH * NBLK
                V.tensor_copy(probsT[n % 2][0:rows, 0:width], bank[6 + n % 2][0:rows, 0:width]).then_inc(pT_copied, 1)

            def combine(L, og, chain):
                br, t = (0, 1, 2)[og // 2], og % 2
                if br < 2:
                    dve.wait_ge(exp_done, N_ATT * L + O_READY[og])
                chain.wait()
                chain.mark(V.tensor_tensor(coef[:, br, t, :], rsum[:, br, t, :],
                                           egate[:, t, :].rearrange("p (h b) -> p b h", b=3)[:, (br + 1) % 3, :], ALU.mult))
                chain.wait()
                chain.mark(V.reciprocal(coef[:, br, t, :], coef[:, br, t, :]))
                chain.wait()
                dve.wait_ge(pv_done, 14 * L + O_READY[og])
                o = bank[2 if br < 2 else CMP_BANK[t]][:].rearrange("p (h d) -> p h d", h=NH)
                c = bcast(coef[:, br, t, :], 2, [P, NH, HEAD])
                if og < 2:
                    ins = V.tensor_tensor(acc[:, t, :].rearrange("p (h d) -> p h d", h=NH), o, c, ALU.mult)
                    ins.then_inc(o_read, 1)
                else:
                    V.tensor_tensor(part[:, 0, :].rearrange("p (h d) -> p h d", h=NH), o, c, ALU.mult).then_inc(o_read, 1)
                    dve.wait_ge(o_read, 6 * L + og + 1)
                    chain.mark(V.tensor_tensor(acc[:, t, :], acc[:, t, :], part[:, 0, :], ALU.add))

            def head_squares(L, t, chain):
                chain.wait()
                chain.mark(V.tensor_tensor(part[:, 1, :], acc[:, t, :], acc[:, t, :], ALU.mult))
                chain.wait()
                V.tensor_reduce(mstat[:, t, :], part[:, 1, :].rearrange("p (h d) -> p h d", h=NH), AX.X, ALU.add).then_inc(att_ss, 1)

            def scale_heads(L, t):
                dve.wait_ge(att_root, 2 * L + t + 1)
                a = acc[:, t, :].rearrange("p (h d) -> p h d", h=NH)
                V.tensor_tensor(a, a, bcast(mroot[:, t, :], 2, [P, NH, HEAD]), ALU.mult).then_inc(att_ready, 1)

            def copy_squares(L, pair):
                dve.wait_ge(ms_used, 2 * L + pair + 1)
                V.tensor_copy(cstat[:, pair].rearrange("p t h -> p (t h)"), bank[3][:, 8 * pair:8 * pair + 8]).then_inc(ms_read, 1)

            def roots_low(L, pair):
                dve.wait_ge(roots_hi, 2 * L + pair + 1)
                lo, hi = (a[:, pair].rearrange("p t (h d) -> p (t h) d", d=HEAD) for a in (roots_l, roots_h))
                V.tensor_tensor(lo, bcast(croot[:, pair].rearrange("p t h -> p (t h)"), 2, [P, 4 * TT, HEAD]), hi.bitcast(fp32),
                                ALU.subtract).then_inc(roots_lo, 1)

            def normalise_conv(L, pair):
                dve.wait_ge(bc_done, 2 * L + pair + 1)
                half = conv_o[:, 2 * pair:2 * pair + 2, :].rearrange("p c n -> p (c n)")
                V.tensor_tensor(half, half, bank[3][:], ALU.mult).then_inc(conv_norm, 1)

            def mix_low(j, lo, hi, src):
                V.scalar_tensor_tensor(lo, src, par[:, j:j + 1], hi.bitcast(fp32), ALU.mult, ALU.subtract).then_inc(mix_lo, 1)

            def mix_conv_low(L, pair):
                for j in (2 * pair, 2 * pair + 1):
                    dve.wait_ge(mix_hi, 12 * L + j + 1)
                    mix_low(j, xl[:, j, :], xh[:, j, :], conv_o[:, j, :])

            def residual(L, which, t, n, banks, chain):
                if t + n < 2:
                    dve.wait_ge(y1_done if which == 0 else y2_done, 2 * L + t + 1)
                else:
                    unit_used(dve, L, U_OUT + 3 if which == 0 else NU - 1)
                xt = x_tok[:, t, 512 * n:512 * (n + 1)]
                chain.mark(V.scalar_tensor_tensor(xt, xt, ALPHA, bank[banks[t] + n][:], ALU.mult, ALU.add))
                chain.wait()
                chain.mark(V.bn_stats(stats[:, t, n, :], xt))

            def layer_norm(L, which, t, ready, chain):
                chain.wait()
                settled(dve)
                V.bn_aggr(mv[:, t, :], stats[:, t].rearrange("p n s -> p (n s)")).then_inc(ln_stats, 1)
                if t == 0:
                    dve.wait_ge(ln_in, 16 * (4 * L + 2 * which + 2))
                dve.wait_ge(ln_stats, LN_CREDIT + 4 * L + 2 * which + t + 1)
                for n in range(2):
                    xt, cols = x_tok[:, t, 512 * n:512 * (n + 1)], slice(512 * n, 512 * (n + 1))
                    chain.mark(V.scalar_tensor_tensor(xt, xt, mv[:, t, 0:1], ln_par[:, 0, cols], ALU.subtract, ALU.mult))
                    chain.wait()
                    dve.wait_ge(ln_root, LN_CREDIT + 4 * L + 2 * which + t + 1)
                    V.scalar_tensor_tensor(xt, xt, rstd[:, t:t + 1], ln_par[:, 1, cols], ALU.mult, ALU.add).then_inc(ready, 1)

            def ffn_step(L, s, odd, value, gate, units):
                G = L * STEPS + s
                for back in (1, 2):
                    for v in range(2):
                        b = bank[4 + 2 * odd + v]
                        if back == 1:
                            dve.wait_ge(fy_init, 2 * G + v + 1)
                        else:
                            dve.wait_ge(fy_mid, 2 * G + v + 1)
                        for c in range(2):
                            ins = V.scalar_tensor_tensor(ffn_y[:, odd, v, c, back:], b[:, SEQ * c:SEQ * (c + 1) - back],
                                                         step_par[:, odd, v, c, 2 - back:3 - back],
                                                         ffn_y[:, odd, v, c, back:], ALU.mult, ALU.add)
                        ins.then_inc(fy_mid if back == 1 else fy_done, 1)
                dve.wait_ge(silu_done, G + 1)
                y = ffn_y[:, odd].rearrange("p v c n -> p v (c n)")
                V.tensor_tensor(y[:, 0], y[:, 0], y[:, 1], ALU.mult).then_inc(h_done, 1)
                dve.wait_ge(h_hi, G + 1)
                V.tensor_tensor(hTl[:, odd].rearrange("p c n -> p (c n)"), y[:, 0],
                                hTh[:, odd].rearrange("p c n -> p (c n)").bitcast(fp32), ALU.subtract).then_inc(h_lo, 1)
                for u in units:
                    split_lo(V, L, *u)

            with dve.Fori(0, DEPTH) as L:
                chain = Chain(dve, dve_seq, L, DVE_STEPS)
                split_lo(V, L, 1)
                x_low(L, XT_BANK, 1, xT_hi, xT_lo[1])
                split_lo(V, L, 3)
                dve.wait_ge(gate_hi, L + 1)
                V.tensor_tensor(gate_wl[:], gate_w[:], gate_wh[:].bitcast(fp32), ALU.subtract).then_inc(gate_lo, 1)
                split_lo(V, L, 6)
                dve.wait_ge(par_ready, L + 1)
                for t in range(TT):
                    rope(L, t, chain)
                split_lo(V, L, 9)
                for b, (dst, hi, src) in enumerate(((qTl[:, 0:2, :], qTh[:, 0:2, :], bank[6]), (qTl[:, 2:4, :], qTh[:, 2:4, :], bank[7]),
                                                    (kTl[:], kTh[:], bank[0]))):
                    dve.wait_ge(qkT_hi, 3 * L + b + 1)
                    V.tensor_tensor(dst.rearrange("p i n -> p (i n)"), src[:], hi.rearrange("p i n -> p (i n)").bitcast(fp32),
                                    ALU.subtract).then_inc(qkT_copied, 1)
                dve.wait_ge(qkT_done, 4 * L + 4)
                for kv in range(2):
                    tok = bank[1][:, 256 * kv:256 * (kv + 1)].rearrange("p (g c r) -> p r g c", g=NG, r=8)
                    for half in range(2):
                        pos = par[:, 24 + 16 * kv + 8 * half:32 + 16 * kv + 8 * half]
                        ins = V.tensor_tensor(blocks[kv][:, 8 * half:8 * half + 8, :].rearrange("p r (g c) -> p r g c", g=NG),
                                              tok[:, :, :, half:half + NBLK],
                                              pos.unsqueeze(2).unsqueeze(3).to_broadcast([P, 8, NG, NBLK]), ALU.add)
                    ins.then_inc(blocks_in, 1)
                for kv in range(2):
                    dve.wait_ge(blocks_hi, 2 * L + kv + 1)
                    V.tensor_tensor(blocks_l[kv], blocks[kv], blocks_h[kv].bitcast(fp32), ALU.subtract).then_inc(blocks_lo, 1)
                dve.wait_ge(gates_T, L + 1)
                chain.mark(V.tensor_scalar(egate[:].rearrange("p t n -> p (t n)"), bank[3][:, 448:448 + TT * NGATE], 1.0, None,
                                           ALU.add))
                conv_gate(L, 0)
                maxima(L, 0, chain)
                maxima(L, 1, chain)
                hidden(L, 0, chain)
                conv_taps(L, 0, chain)
                conv_product(L, 0)
                dve.wait_ge(kc_hi, L + 1)
                for g in range(NG):
                    rows = slice(HEAD * g, HEAD * (g + 1))
                    ins = V.tensor_tensor(kcTl[rows, g, :], bank[2][rows, 384:384 + NBLK], kcTh[rows, g, :].bitcast(fp32), ALU.subtract)
                ins.then_inc(cmp_copied, 1)
                split_lo(V, L, 12)
                copy_pT(L, 0)
                hidden(L, 1, chain)
                maxima(L, 2, chain)
                copy_pT(L, 1)
                dve.wait_ge(cmp_done, 2 * L + 2)
                V.tensor_tensor(vbd, bcast(bank[3][0:NH * NBLK, 384:384 + HEAD], 1, [NH * NBLK, NH, HEAD]),
                                bcast(cst[0:NH * NBLK, C_BM:C_BM + NH], 2, [NH * NBLK, NH, HEAD]), ALU.mult).then_inc(cmp_copied, 1)
                for n in range(2, 11):
                    maxima(L, n + 1, chain)
                    copy_pT(L, n)
                    if n == 2:
                        combine(L, 0, chain)
                    elif n == 3:
                        copy_squares(L, 0)
                    elif n == 4:
                        conv_gate(L, 1)
                    elif n == 6:
                        combine(L, 1, chain)
                    elif n == 7:
                        roots_low(L, 0)
                        conv_taps(L, 1, chain)
                    elif n == 8:
                        combine(L, 2, chain)
                        normalise_conv(L, 0)
                    elif n == 9:
                        conv_product(L, 1)
                        mix_conv_low(L, 0)
                copy_pT(L, 11)
                dve.wait_ge(s_done, N_ATT * L + 13)
                dve.wait_ge(pT_done, N_ATT * L + 11)
                flat = probs[0][:, 0:TT * NH * NBLK].rearrange("p (h c) -> p h c", c=NBLK)
                sc = probs[0][:, 0:TT * NH * NBLK].rearrange("p (t h c) -> p t h c", t=TT, h=NH)
                scores = bank[0][:, 0:TT * NH * NBLK].rearrange("p (t h c) -> p t h c", t=TT, h=NH)
                for t in range(TT):
                    ins = V.tensor_tensor(sc[:, t], scores[:, t], bcast(cst[:, C_MA + NBLK * t:C_MA + NBLK * (t + 1)], 1,
                                                                        [P, NH, NBLK]), ALU.add)
                chain.mark(ins)
                chain.wait()
                chain.mark(V.tensor_reduce(cmax[:], flat, AX.X, ALU.max))
                chain.wait()
                V.tensor_tensor(flat, flat, bcast(cmax[:], 2, [P, TT * NH, NBLK]), ALU.subtract).then_inc(max_done, 1)
                dve.wait_ge(exp_done, N_ATT * L + 13)
                for t in range(TT):
                    ins = V.tensor_reduce(rsum[:, 2, t].rearrange("p (g i) -> p i g", g=NG),
                                          sc[:, t].rearrange("p (i g) c -> p i g c", g=NG), AX.X, ALU.add)
                chain.mark(ins)
                chain.wait()
                for t in range(TT):
                    ins = V.tensor_tensor(sc[:, t], sc[:, t], bcast(cst[:, C_M01 + NBLK * t:C_M01 + NBLK * (t + 1)], 1,
                                                                    [P, NH, NBLK]), ALU.mult)
                ins.then_inc(cmp_p, 1)
                copy_squares(L, 1)
                copy_pT(L, 12)
                combine(L, 3, chain)
                combine(L, 4, chain)
                roots_low(L, 1)
                head_squares(L, 0, chain)
                normalise_conv(L, 1)
                combine(L, 5, chain)
                mix_conv_low(L, 1)
                head_squares(L, 1, chain)
                scale_heads(L, 0)
                scale_heads(L, 1)
                for t in range(TT):
                    dve.wait_ge(mix_hi, 12 * L + 8 + 4 * t)
                    for j in range(4):
                        tok = slice(P * t, P * (t + 1))
                        mix_low(4 + j, xl[:, 4 + j, tok], xh[:, 4 + j, tok], bank[6 + t][:, P * j:P * (j + 1)])
                for n in range(2):
                    residual(L, 0, 0, n, MIX_BANK, chain)
                layer_norm(L, 0, 0, x1_ready, chain)
                for n in range(2):
                    residual(L, 0, 1, n, MIX_BANK, chain)
                layer_norm(L, 0, 1, x1_ready, chain)
                x_low(L, X1T_BANK, 1, x1T_hi, x1T_lo[1])
                ffn_step(L, 0, 0, (19, 0), (20, 0), [(25, 0)])
                ffn_step(L, 1, 1, (21, 0), (22, 0), [(28, 0)])
                ffn_step(L, 2, 0, (23, 0), (24, 0), [(31, 0)])
                with dve.Fori(0, (STEPS - 5) // 2) as i:
                    ffn_step(L, 2 * i + 3, 1, (26, i), (27, i), [(34, i)])
                    ffn_step(L, 2 * i + 4, 0, (29, i), (30, i), [(37, i)])
                last = (STEPS - 5) // 2
                ffn_step(L, STEPS - 2, 1, (26, last), (27, last), [(NU - 2, 0), (NU - 1, 0)])
                ffn_step(L, STEPS - 1, 0, (29, last), (30, last), [])
                for t in range(TT):
                    for n in range(2):
                        residual(L, 1, t, n, FFN_BANK, chain)
                    layer_norm(L, 1, t, x_ready, chain)
                chain.close()

        @block.tensor
        def _(pe):
            def mm3(dst, ah, al, bh, bl, start, stop, **kw):
                pe.matmul(dst, ah, bh, start=start, stop=False, **kw)
                pe.matmul(dst, ah, bl, start=False, stop=False, **kw)
                return pe.matmul(dst, al, bh, start=False, stop=stop, **kw)

            def wait_unit(L, u, i=0):
                pe.wait_ge(split_done[u % RAWS], CREDIT + raw_round(L, u, i) + 1)

            def free_unit(ins, u):
                ins.then_inc(slot_free[u % SLOTS], 1)

            def w_view(u, k):
                return (ring_hi[u % SLOTS][:].rearrange("p (k n) -> p k n", k=k),
                        ring_lo[u % SLOTS][:].rearrange("p (k n) -> p k n", k=k))

            def transpose_x(L, ready, banks, t, done):
                for b in range(2):
                    pe.wait_ge(ready, 4 * L + 2 * t + b + 1)
                    for k in range(4):
                        ins = pe.transpose(bank[banks[t] + b][:, P * k:P * (k + 1)],
                                           x_tok[:, t, P * (4 * b + k):P * (4 * b + k + 1)], ident)
                    ins.then_inc(done, 1)

            def conv_unit(L, idx, part, half=None):
                u = CONV_U[idx]
                if part == 0 and half in (None, 0):
                    wait_unit(L, u)
                    if idx < 2:
                        pe.wait_ge(qkv_copied, 6 * L + 5 + idx)
                    elif idx == 2:
                        pe.wait_ge(c_copied, 2 * L + 1)
                    elif idx == 3:
                        pe.wait_ge(z_done, 2 * L + 1)
                    elif idx == 4:
                        pe.wait_ge(conv_out, 2 * L + 1)
                    else:
                        pe.wait_ge(c_copied, 2 * L + 2)
                wh, wl = w_view(u, KT)
                cols = slice(P * part, P * (part + 1))
                for k in range(KT) if half is None else range(4 * half, 4 * half + 4):
                    ins = mm3(bank[4 + idx % 2][:, SEQ * part:SEQ * (part + 1)], wh[:, k, cols], wl[:, k, cols],
                              xh[:, k, :], xl[:, k, :], k == 0, k == KT - 1)
                if part and half in (None, 1):
                    free_unit(ins, u)

            def scores(L, n):
                br, t, g, heads, kb = ATT[n]
                dst = bank[n % 2]
                if n == 0:
                    pe.wait_ge(qkT_copied, 3 * L + 3)
                elif n == 1:
                    pe.wait_ge(blocks_in, 2 * L + 2)
                else:
                    pe.wait_ge(exp_done, N_ATT * L + n - 1)
                rows = slice(HEAD * g, HEAD * (g + 1))
                keys = P * kb
                for j, h in enumerate(heads):
                    tok = slice(P * t, P * (t + 1))
                    mm3(dst[:, keys * j:keys * (j + 1)], qTh[rows, h, tok], qTl[rows, h, tok], kTh[rows, br, 0:keys],
                        kTl[rows, br, 0:keys], j == 0, False, skip_group_check=True)
                diag = dst[:].rearrange("p (h k) -> p h k", k=keys)[:, :, keys - P:keys]
                pe.matmul(diag, ident_b[:], bcast(cmask_b[:], 1, [P, len(heads), P]), start=False, stop=True,
                          skip_group_check=True).then_inc(s_done, 1)

            def transpose_p(L, n):
                pe.wait_ge(exp_done, N_ATT * L + n + 1)
                if n >= 2:
                    pe.wait_ge(pT_copied, N_ATT * L + n - 1)
                for m in range(4):
                    ins = pe.transpose(bank[6 + n % 2][:, P * m:P * (m + 1)], probs[n % 2][:, P * m:P * (m + 1)], ident)
                ins.then_inc(pT_done, 1)

            def times_v(L, n):
                br, t, g, heads, kb = ATT[n]
                pe.wait_ge(pT_copied, N_ATT * L + n + 1)
                if n in O_READY:
                    pe.wait_ge(o_read, 6 * L + O_READY.index(n) + 1)
                elif n == 0:
                    pe.wait_ge(cmp_copied, 2 * L + 1)
                v0 = (16 if br == 0 else 18) * HEAD + HEAD * g
                for j, h in enumerate(heads):
                    for b in range(kb):
                        ins = pe.matmul(bank[2][:, HEAD * (NPAIR * g + h):HEAD * (NPAIR * g + h + 1)],
                                        probsT[n % 2][:, P * (kb * j + b):P * (kb * j + b + 1)], qkv[:, b, v0:v0 + HEAD],
                                        start=(b == 0), stop=(b == kb - 1))
                ins.then_inc(pv_done, 1)

            def cmp_hidden(L, kv):
                pe.wait_ge(blocks_lo, 2 * L + kv + 1)
                for half, u in enumerate(W1_U[kv]):
                    wait_unit(L, u)
                    wh, wl = w_view(u, 8)
                    for j in range(8):
                        k = 8 * half + j
                        ins = mm3(bank[2 + kv][0:NG * NBLK, 0:CMP_HID], blocks_h[kv][:, k, :], blocks_l[kv][:, k, :],
                                  wh[:, j, :], wl[:, j, :], k == 0, k == NJ - 1)
                    free_unit(ins, u)

            def transpose_hidden(L, kv):
                pe.wait_ge(hid_copied, 2 * L + kv + 1)
                settled(pe)
                for h in range(2):
                    ins = pe.transpose(bank[2 + kv][:, 256 + 32 * h:286 + 32 * h], hid[:, P * h:P * (h + 1)],
                                       ident[0:NG * NBLK, 0:NG * NBLK])
                ins.then_inc(hidT_done, 1)

            def cmp_k(L):
                pe.wait_ge(hid_ready, 2 * L + 1)
                for g in range(NG):
                    dst = bank[2][HEAD * g:HEAD * (g + 1), 384:384 + NBLK]
                    for h in range(2):
                        pe.matmul(dst, w2[:, 0, h, :], hk[:, h, NBLK * g:NBLK * (g + 1)], start=(h == 0), stop=False)
                    ins = pe.matmul(dst, b2[0:1, 0, :], ones[0:1, 0:NBLK], start=False, stop=True)
                ins.then_inc(cmp_done, 1)

            def cmp_v(L):
                pe.wait_ge(hid_ready, 2 * L + 2)
                dst = bank[3][0:NH * NBLK, 384:384 + HEAD]
                for h in range(2):
                    pe.matmul(dst, hv[:, h, :], w2[:, 1, h, :], start=(h == 0), stop=False)
                pe.matmul(dst, ones[0:1, 0:NH * NBLK], b2[0:1, 1, :], start=False, stop=True).then_inc(cmp_done, 1)

            def cmp_scores(L):
                pe.wait_ge(exp_done, N_ATT * L + 11)
                pe.wait_ge(cmp_copied, 2 * L + 1)
                for t in range(TT):
                    for h in range(NPAIR):
                        c0 = NG * NBLK * (NPAIR * t + h)
                        tok = slice(P * t, P * (t + 1))
                        ins = mm3(bank[0][:, c0:c0 + NG * NBLK], qTh[:, h, tok], qTl[:, h, tok],
                                  *(a[:].rearrange("p g c -> p (g c)") for a in (kcTh, kcTl)), True, True)
                ins.then_inc(s_done, 1)

            def transpose_cmp(L):
                pe.wait_ge(cmp_p, L + 1)
                pe.wait_ge(pT_copied, N_ATT * L + 11)
                for t in range(TT):
                    ins = pe.transpose(bank[6][0:NH * NBLK, P * t:P * (t + 1)],
                                       probs[0][:, NH * NBLK * t:NH * NBLK * (t + 1)], ident)
                ins.then_inc(pT_done, 1)

            def times_v_cmp(L, t):
                pe.wait_ge(pT_copied, N_ATT * L + 13)
                pe.wait_ge(cmp_copied, 2 * L + 2)
                if t:
                    pe.wait_ge(o_read, 6 * L + 4)
                pe.matmul(bank[CMP_BANK[t]][:], probsT[0][0:NH * NBLK, P * t:P * (t + 1)], vbd.rearrange("p h d -> p (h d)"),
                          start=True, stop=True).then_inc(pv_done, 1)

            def mean_squares(L, pair):
                pe.wait_ge(sq_done, 2 * L + pair + 1)
                if pair == 0:
                    pe.wait_ge(cmp_copied, 2 * L + 2)
                else:
                    pe.wait_ge(conv_norm, 2 * L + 1)
                for t in range(TT):
                    for m in range(2):
                        c0 = 8 * pair + 4 * t + 2 * m
                        ins = pe.matmul(bank[3][:, c0:c0 + 2], conv_sq[:, m, P * t:P * (t + 1)], cst[:, C_BLK:C_BLK + 2],
                                        start=True, stop=True)
                ins.then_inc(ms_used, 1)

            def conv_roots(L, pair):
                pe.wait_ge(roots_lo, 2 * L + pair + 1)
                for m in range(2):
                    for t in range(TT):
                        for a in (roots_h, roots_l):
                            ins = pe.matmul(bank[3][:, SEQ * m + P * t:SEQ * m + P * (t + 1)], a[:, pair, t, P * m:P * (m + 1)],
                                            ident_r[:], start=(a is roots_h), stop=(a is roots_l))
                ins.then_inc(bc_done, 1)

            def out_product(t, c, k):
                wh, wl = w_view(U_OUT + k // 2, 2)
                cols = slice(512 * c, 512 * (c + 1))
                return mm3(bank[MIX_BANK[t] + c][:], xh[:, k, P * t:P * (t + 1)], xl[:, k, P * t:P * (t + 1)],
                           wh[:, k % 2, cols], wl[:, k % 2, cols], k == 0, k == KT - 1)

            def wait_mix(L, t, k):
                pe.wait_ge(mix_lo, 12 * L + (k + 1 if k < 4 else 4 * t + k + 1))

            def heads_T(L, t):
                pe.wait_ge(att_ready, 2 * L + t + 1)
                for j in range(4):
                    ins = pe.transpose(bank[6 + t][:, P * j:P * (j + 1)], acc[:, t, P * j:P * (j + 1)], ident)
                    if t == 0 and j == 0:
                        ins.then_inc(stage_free, 1)
                ins.then_inc(mixT_done, 1)

            def out_part(L, t, n, part):
                if t == 0 and part == 0:
                    wait_unit(L, U_OUT + n)
                k = 2 * n + part
                wait_mix(L, t, k)
                for c in range(2):
                    ins = out_product(t, c, k)
                if t and part:
                    free_unit(ins, U_OUT + n)
                return ins

            def out_unit(L, t, n):
                out_part(L, t, n, 0)
                return out_part(L, t, n, 1)

            def up(L, s, odd, value, gate, first=False):
                G = L * STEPS + s
                for v, u in enumerate((value, gate)):
                    wait_unit(L, *u)
                    pe.wait_ge(fy_done, FY_CREDIT + 2 * (G - 2) + v + 1)
                    wh, wl = w_view(u[0], KT)
                    for part in range(2):
                        if first and v == 0:
                            for t in range(TT):
                                pe.wait_ge(x1T_lo[t], 2 * L + part + 1)
                        for c in range(2):
                            for k in range(4 * part, 4 * part + 4):
                                ins = mm3(bank[4 + 2 * odd + v][:, SEQ * c:SEQ * (c + 1)], wh[:, k, P * c:P * (c + 1)],
                                          wl[:, k, P * c:P * (c + 1)], xh[:, k, :], xl[:, k, :], k == 0 and c == 0, k == KT - 1,
                                          skip_group_check=True)
                    free_unit(ins, u[0])

            def down_product(odd, u, t, n, c, first=False, last=False):
                wh, wl = w_view(u, 2)
                tok, cols = slice(P * t, P * (t + 1)), slice(512 * n, 512 * (n + 1))
                return mm3(bank[FFN_BANK[t] + n][:], hTh[:, odd, c, tok], hTl[:, odd, c, tok], wh[:, c, cols], wl[:, c, cols],
                           first, last)

            def down(L, s, odd, u, first=False):
                wait_unit(L, *u)
                pe.wait_ge(h_lo, H_CREDIT + L * STEPS + s + 1)
                for t in range(TT):
                    for c in range(2):
                        for n in range(2):
                            ins = down_product(odd, u[0], t, n, c, first=(first and c == 0))
                free_unit(ins, u[0])

            def down_last(L):
                for t in range(TT):
                    for halves in ((0, 1),) if t == 0 else ((0,), (1,)):
                        for s in (STEPS - 2, STEPS - 1):
                            u = NU - STEPS + s
                            if t == 0:
                                wait_unit(L, u)
                                pe.wait_ge(h_lo, H_CREDIT + L * STEPS + s + 1)
                            for c in range(2):
                                for n in halves:
                                    ins = down_product(s % 2, u, t, n, c, last=(s == STEPS - 1 and c == 1))
                            if halves == (1,):
                                free_unit(ins, u)
                        if 0 in halves:
                            ins.then_inc(y2_done, 1)

            pe.wait_ge(ident_in, 16)
            pe.wait_ge(const_ready, 4)
            with pe.Fori(0, DEPTH) as L:
                transpose_x(L, x_ready, XT_BANK, 0, xT_done)
                for t in range(TT):
                    tok = slice(P * t, P * (t + 1))
                    for first in (0, 2):
                        for b in range(2):
                            u = first + b
                            if t == 0:
                                wait_unit(L, u)
                            if first == 0:
                                pe.wait_ge(xT_lo[t], 2 * L + b + 1)
                            wh, wl = w_view(u, 4)
                            for kk in range(4):
                                k = 4 * b + kk
                                ins = mm3(bank[first + t][:], xh[:, k, tok], xl[:, k, tok], wh[:, kk, :], wl[:, kk, :],
                                          k == 0, k == KT - 1)
                            if t:
                                free_unit(ins, u)
                            elif b:
                                ins.then_inc(proj_done, 1)
                            if t == 0 and u == 0:
                                transpose_x(L, x_ready, XT_BANK, 1, xT_done)
                pe.wait_ge(par_in, 16 * 8 * (L + 1))
                settled(pe)
                nf = 4 * STEPS
                for k in range(4):
                    pe.transpose(bank[6][:, nf * k:nf * (k + 1)], ffn_stage[:, k, :], ident[0:nf, 0:nf])
                pe.transpose(bank[6][:, 4 * nf:4 * nf + 56], par_stage[:], ident[0:56, 0:56]).then_inc(par_T, 1)
                wait_unit(L, 4)
                wh, wl = w_view(4, KT)
                for t in range(TT):
                    tok = slice(P * t, P * (t + 1))
                    for k in range(KT):
                        ins = mm3(bank[4 + t][:, 0:256], xh[:, k, tok], xl[:, k, tok], wh[:, k, :], wl[:, k, :], k == 0, k == KT - 1)
                    if t:
                        free_unit(ins, 4)
                    else:
                        ins.then_inc(proj_done, 1)
                pe.wait_ge(gate_lo, L + 1)
                for k in range(KT):
                    ins = mm3(bank[7][0:NGATE, 0:SEQ], gate_wh[:, k, :], gate_wl[:, k, :], xh[:, k, :], xl[:, k, :],
                              k == 0, k == KT - 1)
                ins.then_inc(proj_done, 1)
                for part in range(2):
                    conv_unit(L, 0, part)
                pe.wait_ge(gates_in, L + 1)
                settled(pe)
                for t in range(TT):
                    ins = pe.transpose(bank[3][:, 448 + NGATE * t:448 + NGATE * (t + 1)], egateT[:, P * t:P * (t + 1)],
                                       ident[0:NGATE, 0:NGATE])
                ins.then_inc(gates_T, 1)
                pe.wait_ge(par_ready, L + 1)
                for b in range(2):
                    for t in range(TT):
                        pe.wait_ge(rope_done, 2 * L + t + 1)
                        for m in range(2):
                            h = 2 * b + m
                            ins = pe.transpose(bank[6 + b][:, SEQ * m + P * t:SEQ * m + P * (t + 1)], qkv[:, t, P * h:P * (h + 1)], ident)
                    ins.then_inc(qkT_done, 1)
                for m in range(2):
                    for t in range(TT):
                        col = (10 + 2 * m) * HEAD
                        ins = pe.transpose(bank[0][:, SEQ * m + P * t:SEQ * m + P * (t + 1)], qkv[:, t, col:col + P], ident)
                ins.then_inc(qkT_done, 1)
                for kv in range(2):
                    for g in range(NG):
                        col = (8 + 6 * kv + g) * HEAD
                        for t in range(TT):
                            for odd in range(2):
                                dst = 256 * kv + P * g + 64 * t
                                ins = pe.matmul(bank[1][HEAD * odd:HEAD * (odd + 1), dst:dst + 64], qkv[:, t, col:col + HEAD],
                                                ident[:, odd:P:2], start=True, stop=True)
                ins.then_inc(qkT_done, 1)
                for part in range(2):
                    conv_unit(L, 1, part)
                pe.wait_ge(masks_ready, 3)
                scores(L, 0)
                cmp_hidden(L, 0)
                scores(L, 1)
                transpose_hidden(L, 0)
                for part in range(2):
                    conv_unit(L, 2, part)
                cmp_k(L)
                cmp_hidden(L, 1)
                transpose_p(L, 0)
                transpose_hidden(L, 1)
                pieces = [(idx, part, half) for idx in (3, 4, 5) for part in range(2) for half in range(2)]
                for n in range(12):
                    if n < 10:
                        scores(L, n + 2)
                    elif n == 10:
                        pe.wait_ge(conv_out, 2 * L + 2)
                        out_part(L, 0, 0, 0)
                        cmp_scores(L)
                    if n < 11:
                        transpose_p(L, n + 1)
                    for piece in pieces[2 * n:2 * n + 2] if n < 4 else pieces[n + 4:n + 5]:
                        conv_unit(L, *piece)
                    if n == 0:
                        cmp_v(L)
                    if n == 2:
                        mean_squares(L, 0)
                    if n == 8:
                        conv_roots(L, 0)
                    if n == 11:
                        out_part(L, 0, 0, 1)
                    times_v(L, n)
                mean_squares(L, 1)
                transpose_cmp(L)
                times_v_cmp(L, 0)
                pe.wait_ge(exp_done, N_ATT * L + 13)
                out_part(L, 1, 0, 0)
                times_v_cmp(L, 1)
                conv_roots(L, 1)
                out_part(L, 1, 0, 1)
                out_unit(L, 0, 1)
                heads_T(L, 0)
                for k in (2, 3):
                    out_product(1, 0, k)
                heads_T(L, 1)
                out_unit(L, 0, 2)
                out_unit(L, 0, 3).then_inc(y1_done, 1)
                for c in range(2):
                    for k in range(4 if c == 0 else 2, KT):
                        wait_mix(L, 1, k)
                        ins = out_product(1, c, k)
                        if c and k % 2:
                            free_unit(ins, U_OUT + k // 2)
                        if c and k == 6:
                            transpose_x(L, x1_ready, X1T_BANK, 0, x1T_done)
                    if c == 0:
                        ins.then_inc(y1_done, 1)
                transpose_x(L, x1_ready, X1T_BANK, 1, x1T_done)
                up(L, 0, 0, (19, 0), (20, 0), first=True)
                up(L, 1, 1, (21, 0), (22, 0))
                up(L, 2, 0, (23, 0), (24, 0))
                down(L, 0, 0, (25, 0), first=True)
                up(L, 3, 1, (26, 0), (27, 0))
                down(L, 1, 1, (28, 0))
                up(L, 4, 0, (29, 0), (30, 0))
                with pe.Fori(1, (STEPS - 3) // 2) as i:
                    down(L, 2 * i, 0, (25, i))
                    up(L, 2 * i + 3, 1, (26, i), (27, i))
                    down(L, 2 * i + 1, 1, (28, i))
                    up(L, 2 * i + 4, 0, (29, i), (30, i))
                down(L, STEPS - 3, 0, (NU - 3, 0))
                down_last(L)


_INS = ['x', 'w_in', 'short_conv_w', 'cmp_pe', 'cmp_w1', 'cmp_b1', 'cmp_w2', 'cmp_b2', 'head_norm_g', 'w_out', 'ln1_g',
        'ln1_b', 'w_up', 'ffn_conv_w', 'ffn_conv_b', 'w_down', 'ln2_g', 'ln2_b']


def kernel(**inputs):
    import concourse.bacc as bacc
    from concourse.bass_utils import run_bass_kernel_spmd

    nc = bacc.Bacc("TRN2", target_bir_lowering=False, num_devices=1, dynamic_dma_scratch_size=256)
    arrays, args = {}, []
    for name in _INS:
        a = np.ascontiguousarray(inputs[name])
        arrays[f"in_{name}"] = a
        args.append(nc.dram_tensor(f"in_{name}", a.shape, mybir.dt.from_np(a.dtype), kind="ExternalInput").ap())
    arrays["in_consts"] = shape_constants()
    args.append(nc.dram_tensor("in_consts", (P, C_ALL), mybir.dt.float32, kind="ExternalInput").ap())
    args.append(nc.dram_tensor("out_0", (1, SEQ, D_MODEL), mybir.dt.float32, kind="ExternalOutput").ap())
    build(nc, *args)
    return run_bass_kernel_spmd(nc, [arrays], core_ids=[0]).results[0]["out_0"]
```
